# Optimizing a Trainium2 kernel written in Bass

```python
import jax, jax.numpy as jnp
from jax import lax
import numpy as np

D_MODEL = 1024
BATCH = 1
SEQ = 256
DEPTH = 2

GRID_W = 64
CTX_LEN = 256
N_MOD = 9
RET_HEADS = 4
RET_DK = 256
RET_DV = 512
RET_CHUNK = 128
ATT_HEADS = 8
ATT_KV_HEADS = 2
ATT_HD = 128
Q_BLOCK = 128
FFN_DIM = 2816
ROPE_THETA = 10000.0
EPS = 1e-6
N_RET = (DEPTH + 1) // 2
N_ATT = DEPTH // 2
ADA_SCALE = 0.5

kernel_name = "hybrid_retention_gqa_macaron_dit"

F32 = jnp.float32

def _rms(x, g):
    xf = x.astype(F32)
    y = xf * lax.rsqrt(jnp.mean(xf * xf, axis=-1, keepdims=True) + EPS)
    return (y * g.astype(F32)).astype(x.dtype)

def _modulated(x, g, shift, scale):
    return _rms(x, g) * (1.0 + scale) + shift

def _swiglu(h, w1, w2):
    gate, up = jnp.split(h @ w1, 2, axis=-1)
    return (jax.nn.silu(gate) * up) @ w2

def _rotate(x, ang):
    half = x.shape[-1] // 2
    xf = x.astype(F32)
    x1, x2 = xf[..., :half], xf[..., half:]
    cos, sin = jnp.cos(ang), jnp.sin(ang)
    return jnp.concatenate([x1 * cos - x2 * sin, x2 * cos + x1 * sin], axis=-1).astype(x.dtype)

def _axial_angles(n_tok, dim):
    rows = n_tok // GRID_W
    r, cl = jnp.meshgrid(jnp.arange(rows), jnp.arange(GRID_W), indexing="ij")
    r = r.reshape(-1).astype(F32)
    cl = cl.reshape(-1).astype(F32)
    quarter = dim // 4
    freqs = ROPE_THETA ** (-jnp.arange(quarter, dtype=F32) / quarter)
    return jnp.concatenate([r[:, None] * freqs, cl[:, None] * freqs], axis=-1)

def _seq_angles(n_tok, dim):
    half = dim // 2
    freqs = ROPE_THETA ** (-jnp.arange(half, dtype=F32) / half)
    return jnp.arange(n_tok, dtype=F32)[:, None] * freqs

def _ret_decays(log_g, C):
    pos = jnp.arange(C, dtype=F32)
    diff = pos[:, None] - pos[None, :]
    intra = jnp.where(diff[None] >= 0, jnp.exp(jnp.maximum(diff, 0.0)[None] * log_g[:, None, None]), 0.0)
    xi = jnp.exp((pos + 1.0)[None] * log_g[:, None])
    zeta = jnp.exp((C - 1.0 - pos)[None] * log_g[:, None])
    chunk = jnp.exp(C * log_g)
    return intra, xi, zeta, chunk

def _ret_scan(q, k, v, log_g, state0):
    B, H, L, dk = q.shape
    dv = v.shape[-1]
    C = RET_CHUNK
    N = L // C
    intra, xi, zeta, chunk = _ret_decays(log_g, C)
    qc = q.reshape(B, H, N, C, dk)
    kc = k.reshape(B, H, N, C, dk)
    vc = v.reshape(B, H, N, C, dv)
    s = jnp.einsum("bhncd,bhnmd->bhncm", qc, kc) * intra[None, :, None]
    inner = jnp.einsum("bhncm,bhnme->bhnce", s, vc)
    xs = (jnp.moveaxis(qc * xi[None, :, None, :, None], 2, 0),
          jnp.moveaxis(kc * zeta[None, :, None, :, None], 2, 0),
          jnp.moveaxis(vc, 2, 0))

    def step(state, blk):
        qx, kz, vb = blk
        cross = jnp.einsum("bhcd,bhde->bhce", qx, state)
        state = state * chunk[None, :, None, None] + jnp.einsum("bhcd,bhce->bhde", kz, vb)
        return state, cross

    final, cross = lax.scan(step, state0, xs)
    out = inner + jnp.moveaxis(cross, 0, 2)
    return out.reshape(B, H, L, dv), final

def _ret_final_state(k, v, log_g):
    L = k.shape[2]
    w = jnp.exp((L - 1.0 - jnp.arange(L, dtype=F32))[None] * log_g[:, None])
    return jnp.einsum("bhld,bhle,hl->bhde", k, v, w)

def _to_heads(p, n, d):
    B, L, _ = p.shape
    return p.reshape(B, L, n, d).transpose(0, 2, 1, 3)

def _retention(h, hc, w_in, w_out, dec_f, dec_b, ctx_out):
    QD = RET_HEADS * RET_DK
    VD = RET_HEADS * RET_DV
    log_f = -jnp.exp(dec_f.astype(F32))
    log_b = -jnp.exp(dec_b.astype(F32))
    flip = lambda a: a[:, :, ::-1]

    def qkvg(z):
        p = (z @ w_in).astype(F32)
        q, k, v, g = jnp.split(p, [QD, 2 * QD, 2 * QD + VD], axis=-1)
        return (_to_heads(q, RET_HEADS, RET_DK), _to_heads(k, RET_HEADS, RET_DK) * RET_DK ** -0.5,
                _to_heads(v, RET_HEADS, RET_DV), g)

    def merge(o, g):
        o = o * lax.rsqrt(jnp.mean(o * o, axis=-1, keepdims=True) + EPS)
        B, H, L, dv = o.shape
        o = o.transpose(0, 2, 1, 3).reshape(B, L, H * dv)
        return ((o * jax.nn.silu(g)) @ w_out).astype(h.dtype)

    B, L, _ = h.shape
    q, k, v, g = qkvg(h)
    ang = _seq_angles(L, RET_DK)
    q = _rotate(q, ang)
    k = _rotate(k, ang)

    if ctx_out:
        qc, kc, vc, gc = qkvg(hc)
        zeros = jnp.zeros((B, RET_HEADS, RET_DK, RET_DV), F32)
        oc_f, s_f = _ret_scan(qc, kc, vc, log_f, zeros)
        oc_b, s_b = _ret_scan(flip(qc), flip(kc), flip(vc), log_b, zeros)
        yc = merge(oc_f + flip(oc_b), gc)
    else:
        p = (hc @ w_in[:, QD:2 * QD + VD]).astype(F32)
        kc = _to_heads(p[..., :QD], RET_HEADS, RET_DK) * RET_DK ** -0.5
        vc = _to_heads(p[..., QD:], RET_HEADS, RET_DV)
        s_f = _ret_final_state(kc, vc, log_f)
        s_b = _ret_final_state(flip(kc), flip(vc), log_b)
        yc = None

    o_f, _ = _ret_scan(q, k, v, log_f, s_f)
    o_b, _ = _ret_scan(flip(q), flip(k), flip(v), log_b, s_b)
    y = merge(o_f + flip(o_b), g)
    return y, yc

def _attend(q, k, v):
    s = jnp.einsum("bkgqd,bksd->bkgqs", q, k).astype(F32) * ATT_HD ** -0.5
    p = jax.nn.softmax(s, axis=-1)
    return jnp.einsum("bkgqs,bksd->bkgqd", p.astype(v.dtype), v)

def _gqa(h, hc, w_qkv, w_o, q_gain, k_gain, ctx_out):
    QD = ATT_HEADS * ATT_HD
    KD = ATT_KV_HEADS * ATT_HD
    G = ATT_HEADS // ATT_KV_HEADS

    def kv(p):
        k = _rms(_to_heads(p[..., :KD], ATT_KV_HEADS, ATT_HD), k_gain)
        v = _to_heads(p[..., KD:], ATT_KV_HEADS, ATT_HD)
        return k, v

    def merge(o):
        B, _, _, L, _ = o.shape
        return o.reshape(B, ATT_HEADS, L, ATT_HD).transpose(0, 2, 1, 3).reshape(B, L, QD) @ w_o

    B, L, _ = h.shape
    p = h @ w_qkv
    q = _rms(_to_heads(p[..., :QD], ATT_HEADS, ATT_HD), q_gain)
    k, v = kv(p[..., QD:])
    ang = _axial_angles(L, ATT_HD)
    q = _rotate(q, ang)
    k = _rotate(k, ang)

    if ctx_out:
        pc = hc @ w_qkv
        qc = _rms(_to_heads(pc[..., :QD], ATT_HEADS, ATT_HD), q_gain)
        kc, vc = kv(pc[..., QD:])
        Lc = hc.shape[1]
        yc = merge(_attend(qc.reshape(B, ATT_KV_HEADS, G, Lc, ATT_HD), kc, vc))
    else:
        kc, vc = kv(hc @ w_qkv[:, QD:])
        yc = None

    k_all = jnp.concatenate([k, kc], axis=2)
    v_all = jnp.concatenate([v, vc], axis=2)
    NB = L // Q_BLOCK
    qb = jnp.moveaxis(q.reshape(B, ATT_KV_HEADS, G, NB, Q_BLOCK, ATT_HD), 3, 0)
    o = lax.map(lambda qi: _attend(qi, k_all, v_all), qb)
    o = jnp.moveaxis(o, 0, 3).reshape(B, ATT_KV_HEADS, G, L, ATT_HD)
    return merge(o), yc

def setup_inputs(seed: int = 0) -> dict:
    key = jax.random.key(seed)
    ks = jax.random.split(key, 20)
    D = D_MODEL
    nrm = lambda k, shp, fan: jax.random.normal(k, shp, F32) * fan ** -0.5
    ret_in = RET_HEADS * (2 * RET_DK + 2 * RET_DV)
    att_in = (ATT_HEADS + 2 * ATT_KV_HEADS) * ATT_HD
    base = jnp.log(-jnp.log1p(-(2.0 ** (-5.0 - jnp.arange(RET_HEADS, dtype=F32)))))
    return {
        "x": jax.random.normal(ks[0], (BATCH, SEQ, D), F32),
        "c": jax.random.normal(ks[1], (BATCH, D), F32),
        "ctx": jax.random.normal(ks[2], (BATCH, CTX_LEN, D), F32),
        "c_ctx": jax.random.normal(ks[3], (D,), F32),
        "ada_w": nrm(ks[4], (DEPTH, D, N_MOD * D), D) * ADA_SCALE,
        "ada_b": 0.01 * jax.random.normal(ks[5], (DEPTH, N_MOD * D), F32),
        "norm_g": 1.0 + 0.02 * jax.random.normal(ks[6], (DEPTH, 3, D), F32),
        "ffn_w1": nrm(ks[7], (DEPTH, 2, D, 2 * FFN_DIM), D),
        "ffn_w2": nrm(ks[8], (DEPTH, 2, FFN_DIM, D), FFN_DIM),
        "ret_w_in": nrm(ks[9], (N_RET, D, ret_in), D),
        "ret_w_out": nrm(ks[10], (N_RET, RET_HEADS * RET_DV, D), RET_HEADS * RET_DV),
        "ret_decay_f": base[None] + 0.01 * jax.random.normal(ks[11], (N_RET, RET_HEADS), F32),
        "ret_decay_b": base[None] + 0.01 * jax.random.normal(ks[12], (N_RET, RET_HEADS), F32),
        "att_w_qkv": nrm(ks[13], (N_ATT, D, att_in), D),
        "att_w_o": nrm(ks[14], (N_ATT, ATT_HEADS * ATT_HD, D), ATT_HEADS * ATT_HD),
        "att_q_gain": 1.0 + 0.02 * jax.random.normal(ks[15], (N_ATT, ATT_HD), F32),
        "att_k_gain": 1.0 + 0.02 * jax.random.normal(ks[16], (N_ATT, ATT_HD), F32),
        "final_g": 1.0 + 0.02 * jax.random.normal(ks[17], (D,), F32),
    }

def reference(x, c, ctx, c_ctx, ada_w, ada_b, norm_g, ffn_w1, ffn_w2, ret_w_in, ret_w_out,
              ret_decay_f, ret_decay_b, att_w_qkv, att_w_o, att_q_gain, att_k_gain, final_g):
    xc = ctx
    sc = jax.nn.silu(c)
    scc = jax.nn.silu(c_ctx)
    for i in range(DEPTH):
        last = i == DEPTH - 1
        m = jnp.split((sc @ ada_w[i] + ada_b[i])[:, None, :], N_MOD, axis=-1)
        mc = jnp.split(scc @ ada_w[i] + ada_b[i], N_MOD, axis=-1)
        x = x + 0.5 * m[2] * _swiglu(_modulated(x, norm_g[i, 0], m[0], m[1]), ffn_w1[i, 0], ffn_w2[i, 0])
        xc = xc + 0.5 * mc[2] * _swiglu(_modulated(xc, norm_g[i, 0], mc[0], mc[1]), ffn_w1[i, 0], ffn_w2[i, 0])
        h = _modulated(x, norm_g[i, 1], m[3], m[4])
        hc = _modulated(xc, norm_g[i, 1], mc[3], mc[4])
        j = i // 2
        if i % 2 == 0:
            y, yc = _retention(h, hc, ret_w_in[j], ret_w_out[j], ret_decay_f[j], ret_decay_b[j], not last)
        else:
            y, yc = _gqa(h, hc, att_w_qkv[j], att_w_o[j], att_q_gain[j], att_k_gain[j], not last)
        x = x + m[5] * y
        if not last:
            xc = xc + mc[5] * yc
            xc = xc + 0.5 * mc[8] * _swiglu(_modulated(xc, norm_g[i, 2], mc[6], mc[7]), ffn_w1[i, 1], ffn_w2[i, 1])
        x = x + 0.5 * m[8] * _swiglu(_modulated(x, norm_g[i, 2], m[6], m[7]), ffn_w1[i, 1], ffn_w2[i, 1])
    return _rms(x, final_g)


_drawn_inputs = setup_inputs


def setup_inputs(seed=0):
    import zlib

    import numpy as np

    out = dict(_drawn_inputs(seed))
    spreads = {}
    factors = {'ada_b': 4.237, 'norm_g': 5.705, 'att_q_gain': 8.0, 'att_k_gain': 8.0, 'final_g': 2.869}
    for name, (base, spread) in spreads.items():
        noise = np.random.default_rng([zlib.crc32(name.encode()), seed]).standard_normal(out[name].shape)
        drawn = base * np.exp(spread * noise) if base else spread * noise
        out[name] = __import__('jax').numpy.asarray(drawn.astype(out[name].dtype))
    for name, factor in factors.items():
        out[name] = (out[name] * factor).astype(out[name].dtype)
    return out
```

```python
from contextlib import ExitStack

import concourse.bass as bass
from concourse import mybir

F32 = mybir.dt.float32
F32R = mybir.dt.float32r
ALU = mybir.AluOpType
ACT = mybir.ActivationFunctionType
AX_X = mybir.AxisListType.X

P = 128
D = 1024
KD = D // P
LAT = 256
CTX = 256
N = LAT + CTX
DEPTH = 2
NMOD = 9
FFN = 2816
EPS = 1e-6
RH, RDK, RDV = 4, 256, 512
AH, AKV, AHD = 8, 2, 128
UNIT = 2048
HALVES = (12, 10)
ADA = 256
ADA_L = NMOD * D // ADA
ADA_PRO = 8
BAND = 384

UNITS_FFN = sum(HALVES) + 2 * KD
UNITS_RET_HEAD = 8
U_FFN = {(0, 0): 0}
U_RET = UNITS_FFN
U_FFN[(0, 1)] = U_RET + RH * UNITS_RET_HEAD
U_FFN[(1, 0)] = U_FFN[(0, 1)] + UNITS_FFN
U_GQA = U_FFN[(1, 0)] + UNITS_FFN
U_FFN[(1, 1)] = U_GQA + 10
U_END = U_FFN[(1, 1)] + UNITS_FFN
G_FFN = {(0, 0): 0, (0, 1): 22, (1, 0): 44, (1, 1): 66}

ROW_NG, ROW_FG, ROW_C, ROW_CX, ROW_QG, ROW_KG, ROWS = 144, 192, 200, 208, 216, 217, 218
C_ID, C_ONE, C_D, C_RC, C_RS, C_AC, C_AS, C_END = 0, 128, 256, 640, 896, 1152, 1408, 1664

CH_Q, CH_K, CH_V, CH_S = 4, 6, 8, 12
CH_GV, CH_GQ, CH_GO, CH_GP = 2, 4, 8, 12
S_NORM = {(0, 0): 0, (0, 1): 1, (0, 2): 6, (1, 0): 7, (1, 1): 8, (1, 2): 15}
S_RET, S_GQA, S_FIN = 2, 9, 16


def ada_plan():
    return {("gu", 0, 0, 0): 6, ("down", 0, 0, 0): 3, ("gu", 0, 0, 1): 5, ("gu", 0, 1, 0): 2}


def ada_base():
    base, a = {}, ADA_PRO
    for key in (("gu", 0, 0, 0), ("down", 0, 0, 0), ("gu", 0, 0, 1)):
        base[key] = a
        a += 2 * ada_plan()[key]
    base["ret"] = a
    a += RH * UNITS_RET_HEAD
    base[("gu", 0, 1, 0)] = a
    assert base["ret"] == ADA_L and a + 4 == DEPTH * ADA_L
    return base


class Steps:

    def __init__(self, sem):
        self.sem, self.base, self.it, self.per, self.local = sem, 0, 0, 0, 0

    def enter(self, it, per):
        self.base += self.local
        self.it, self.per, self.local = it, per, 0

    def leave(self, count):
        assert self.local == self.per, (self.local, self.per)
        self.base, self.it, self.per, self.local = self.base + self.per * count, 0, 0, 0

    def mark(self, ins):
        ins.then_inc(self.sem, 1)
        self.local += 1
        return self.it * self.per + (self.base + self.local)


def build(nc, x, ctx, vecs, dec, consts, ada_w, w1, w2, ret_in, ret_out, qkv, wo, out):
    stack = ExitStack()
    with stack:
        def sb(name, shape, dt=F32):
            return stack.enter_context(nc.sbuf_tensor(name, shape, dt))

        def sem(name):
            return stack.enter_context(nc.semaphore(name))

        xT = sb("xT", [P, KD, N])
        h_hi = sb("h_hi", [P, KD, N], F32R)
        h_lo = sb("h_lo", [P, KD, N], F32R)
        a_hi = sb("a_hi", [P, 15, N], F32R)
        a_lo = sb("a_lo", [P, 15, N], F32R)
        raw = sb("raw", [P, 2, UNIT])
        w_hi = sb("w_hi", [P, 2, UNIT], F32R)
        w_lo = sb("w_lo", [P, 2, UNIT], F32R)
        ada = sb("ada", [P, UNIT])
        acc = sb("acc", [P, 2, ADA])
        park = sb("park", [P, 8, N])
        tmp = sb("tmp", [P, 2, N])
        full = sb("full", [P, 2, N])
        ssum = sb("ssum", [P, N])
        sq = sb("sq", [P, N])
        diag = sb("diag", [P, N])
        cst = sb("cst", [P, C_END])
        band = sb("band", [P, 2, BAND])
        vecT = sb("vecT", [P, ROWS])
        modT = sb("modT", [P, DEPTH * NMOD * KD, 2])
        sT = sb("sT", [P, KD, 2])
        aff = sb("aff", [P, KD, 2])
        gate = sb("gate", [P, KD, 2])
        sd = sb("sd", [P, 4])
        rs = sb("rs", [P, 4])
        lg = sb("lg", [P, 2 * RH])
        dec_row = sb("dec_row", [1, 2 * RH])
        smx, snb, sden, sinv = (band[:, 0, 2 * AH * i:2 * AH * (i + 1)] for i in range(4))
        mark = sb("mark", [P, 1])

        pair = stack.enter_context(nc.psum_tensor("pair", [P, 2, 2, N], F32))
        ps_s = stack.enter_context(nc.psum_tensor("ps_s", [P, N], F32))
        psx = stack.enter_context(nc.psum_tensor("psx", [P, 3, N], F32))

        ident = cst[:, C_ID:C_ID + P]
        ones = cst[:, C_ONE:C_ONE + P]
        diff = cst[:, C_D:C_D + BAND]
        rcos, rsin = cst[:, C_RC:C_RC + LAT], cst[:, C_RS:C_RS + LAT]
        acos, asin = cst[:, C_AC:C_AC + LAT], cst[:, C_AS:C_AS + LAT]
        vrows = tmp[:, 0, 0:2 * P]
        o_buf, sg_buf = park[:, 0:4, :], park[:, 4:8, :]

        names = """consts_in vecs_in dec_in x_in raw_landed0 raw_landed1 pro_landed0 pro_landed1 pro_landed2
            ada_landed vec_tr vec_up mod_up x_tr x_up dec_mm dec_exp silu_c s_rdy pro_mm hi_ready lo_ready pe_unit pair_free acc_ready
            ada_mm mod_ready silu_ready u_ready u_hi xsq ss_ready st_sum st_sqrt st_diag st_bcast t_ready n_hi
            h_ready dve_step q_ctx_hi rot_ready q_lat_hi v_hi e_pre e_exp s_mm ms_ready ms_hi s_split o_mm
            o_copied o_sq sg_ready og_ready og_hi og_lo g_sq kn_ready kn_hi kn_lo sc_mm nb_ready p_exp p_ready
            pt_mm pt_hi pt_lo oT_mm oT_hi oT_lo fin_ready fin_tr fin_copied out_done pool_step gv_hi""".split()
        S = {n: sem(n) for n in names}
        raw_landed = [S["raw_landed0"], S["raw_landed1"]]
        pro_landed = [S["pro_landed0"], S["pro_landed1"], S["pro_landed2"]]
        A0 = ada_base()
        APLAN = ada_plan()

        def f32(ap):
            return ap.bitcast(F32)

        block = stack.enter_context(nc.Block())

        @block.sync
        def _(sp):
            ada_v = [ada_w[l].rearrange("(k p) n -> p k n", p=P) for l in range(DEPTH)]
            ada3 = ada[:, :].rearrange("p (k n) -> p k n", k=KD)

            def slot(u):
                return raw[:, u % 2, :]

            def load(j, dst, src, wait=None):
                half = dst.shape[1] // 2
                if wait is not None:
                    sp.wait_ge(S["lo_ready"], wait)
                sp.dma_start(dst[:, 0:half], src[:, 0:half]).then_inc(raw_landed[j], 16)
                sp.dma_start(dst[:, half:], src[:, half:]).then_inc(raw_landed[j], 16)

            def load_ada(a, layer):
                sp.wait_ge(S["acc_ready"], a - ADA_PRO)
                sp.dma_start(ada3, ada_v[layer][:, :, bass.ds(a * ADA - layer * NMOD * D, ADA)]
                             ).then_inc(S["ada_landed"], 16)

            def load_gu(l, f, u, j, chunk, wait):
                w = w1[l, f].rearrange("(k p) n -> p k n", p=P)
                dst = slot(j).rearrange("p (c k n) -> p c k n", c=2, k=KD)
                if wait is not None:
                    sp.wait_ge(S["lo_ready"], wait)
                for c in range(2):
                    sp.dma_start(dst[:, c], w[:, :, bass.ds(chunk * P + c * FFN, P)]
                                 ).then_inc(raw_landed[j], 16)

            sp.dma_start(cst[:, :], consts).then_inc(S["consts_in"], 16)
            sp.dma_start(vrows[:, 0:P], vecs[0:P, :]).then_inc(S["vecs_in"], 16)
            sp.dma_start(vrows[0:ROWS - P, P:2 * P], vecs[P:ROWS, :]).then_inc(S["vecs_in"], 16)
            sp.dma_start(dec_row[:, :], dec).then_inc(S["dec_in"], 16)
            slots3 = [slot(0), slot(1), ada[:, :]]
            for a in range(ADA_PRO):
                if a >= 3:
                    sp.wait_ge(S["pro_mm"], a - 2)
                sp.dma_start(slots3[a % 3].rearrange("p (k n) -> p k n", k=KD),
                             ada_v[0][:, :, a * ADA:(a + 1) * ADA]).then_inc(pro_landed[a % 3], 16)
                if a == 2:
                    xin = park[:, :, :].rearrange("p (t a) n -> p t (a n)", t=4)
                    sp.dma_start(xin[:, 0:2], x.rearrange("(t p) d -> p t d", p=P)).then_inc(S["x_in"], 16)
                    sp.dma_start(xin[:, 2:4], ctx.rearrange("(t p) d -> p t d", p=P)).then_inc(S["x_in"], 16)

            def ffn(l, f):
                u = U_FFN[(l, f)]
                r0 = 0
                for half, rows in enumerate(HALVES):
                    key = ("gu", l, f, half)
                    na = APLAN.get(key, 0)

                    def body(it, first, with_ada):
                        for j in range(2):
                            uu = u + 2 * it + j
                            if first:
                                sp.wait_ge(S["pro_mm"], ADA_PRO - 1 + j)
                            load_gu(l, f, uu, j, 2 * it + (r0 + j), None if first else uu - 1)
                            if with_ada:
                                if first and j == 0:
                                    sp.wait_ge(S["pro_mm"], ADA_PRO - 2)
                                a = 2 * it + (A0[key] + j)
                                if isinstance(a, int) and a == ADA_PRO:
                                    sp.dma_start(ada3, ada_v[0][:, :, a * ADA:(a + 1) * ADA]
                                                 ).then_inc(S["ada_landed"], 16)
                                else:
                                    load_ada(a, 0 if l == 0 and f == 0 else 1)
                    start = 0
                    if u == 0:
                        body(0, True, True)
                        start = 1
                    if na > start:
                        with sp.Fori(start, na) as it:
                            body(it, False, True)
                    if rows // 2 > max(na, start):
                        with sp.Fori(max(na, start), rows // 2) as it:
                            body(it, False, False)
                    u += rows
                    key = ("down", l, f, half)
                    na = APLAN.get(key, 0)
                    w = w2[l, f].rearrange("(r p) n -> p r n", p=P)

                    def dbody(it, with_ada):
                        for j in range(2):
                            uu = u + 2 * it + j
                            dst = slot(j)[:, 0:rows * P].rearrange("p (r n) -> p r n", r=rows)
                            load(j, dst, w[:, r0:r0 + rows, bass.ds((2 * it + j) * P, P)], uu - 1)
                            if with_ada:
                                load_ada(2 * it + (A0[key] + j), 0)
                    if na:
                        with sp.Fori(0, na) as it:
                            dbody(it, True)
                    if KD // 2 > na:
                        with sp.Fori(na, KD // 2) as it:
                            dbody(it, False)
                    u += KD
                    r0 += rows

            def retention():
                win = ret_in.rearrange("(k p) n -> p k n", p=P)
                wout = ret_out.rearrange("(r p) n -> p r n", p=P)
                with sp.Fori(0, RH) as hd:
                    for j in range(8):
                        uu = U_RET + 8 * hd + j
                        if j < 6:
                            col = (RDK * hd, D + RDK * hd, 2 * D + RDV * hd, 2 * D + RDV * hd + 256,
                                   4 * D + RDV * hd, 4 * D + RDV * hd + 256)[j]
                            load(j % 2, slot(j).rearrange("p (k n) -> p k n", k=KD),
                                 win[:, :, bass.ds(col, 256)], uu - 1)
                        else:
                            load(j % 2, slot(j).rearrange("p (k n) -> p k n", k=4),
                                 wout[:, bass.ds(4 * hd, 4), (j - 6) * 512:(j - 5) * 512], uu - 1)
                        load_ada(8 * hd + (A0["ret"] + j), 1)

            def gqa():
                w = qkv.rearrange("(k p) n -> p k n", p=P)
                o = wo.rearrange("(k p) n -> p k n", p=P)
                cols = [D, D + 256, 0, 256, 512, 768]
                for j in range(10):
                    src = w[:, :, cols[j]:cols[j] + 256] if j < 6 else o[:, :, (j - 6) * 256:(j - 5) * 256]
                    load(j % 2, slot(j).rearrange("p (k n) -> p k n", k=KD), src, U_GQA + j - 1)

            ffn(0, 0)
            retention()
            ffn(0, 1)
            ffn(1, 0)
            gqa()
            ffn(1, 1)
            outv = out.rearrange("(t p) d -> p t d", p=P)
            for t in range(2):
                sp.wait_ge(S["fin_copied"], t + 1)
                sp.dma_start(outv[:, t], park[:, 2 * t:2 * t + 2, :].rearrange("p a n -> p (a n)")
                             ).then_inc(S["out_done"], 16)
            sp.wait_ge(S["out_done"], 32)

        @block.tensor
        def _(pe):
            mm = nc.tensor.matmul

            def mm3(dst, whi, wlo, xhi, xlo, start, stop):
                mm(dst, wlo, xhi, start=start, stop=False)
                mm(dst, whi, xlo, start=False, stop=False)
                return mm(dst, whi, xhi, start=False, stop=stop)

            def wait_unit(u):
                if not isinstance(u, int) or u > 0:
                    pe.wait_ge(S["pair_free"], u + 1)
                pe.wait_ge(S["lo_ready"], u + 1)

            def rows_sum(src, s, tiles, extra=None):
                for t in range(tiles):
                    last = mm(ps_s[:, 8 + t:9 + t], src[:, t * P:(t + 1) * P], ones[:, 0:1], start=True, stop=True)
                last.then_inc(S["st_sum"], 1)

            def rows_bcast(bank, s, width):
                pe.wait_ge(S["st_diag"], s + 1)
                mm(bank[:, 0:width], ones, diag[:, 0:width], start=True, stop=True).then_inc(S["st_bcast"], 1)

            def ada_mm(a):
                pe.wait_ge(S["acc_ready"], a - (ADA_PRO - 1))
                for c in range(2):
                    for cond in range(2):
                        last = mm(ps_s[:, 2 * c + cond:2 * c + cond + 1], acc[:, cond, c * P:(c + 1) * P],
                                  ones[:, 0:1], start=True, stop=True)
                last.then_inc(S["ada_mm"], 1)

            def unit_cols(u, j, width, h0, banks=None):
                wait_unit(u)
                whi = w_hi[:, j, :].rearrange("p (k c n) -> p k c n", k=KD, c=2)
                wlo = w_lo[:, j, :].rearrange("p (k c n) -> p k c n", k=KD, c=2)
                dst = banks or [pair[:, j, 0, 0:width], pair[:, j, 1, 0:width]]
                for k in range(KD):
                    pe.wait_ge(S["h_ready"], h0 + k + 1)
                    for c in range(2):
                        last = mm3(dst[c], whi[:, k, c], wlo[:, k, c], h_hi[:, k, 0:width], h_lo[:, k, 0:width],
                                   k == 0, k == KD - 1)
                last.then_inc(S["pe_unit"], 1)

            def unit_gu(u, j, width, h0):
                wait_unit(u)
                whi = w_hi[:, j, :].rearrange("p (c k n) -> p c k n", c=2, k=KD)
                wlo = w_lo[:, j, :].rearrange("p (c k n) -> p c k n", c=2, k=KD)
                for k in range(KD):
                    pe.wait_ge(S["h_ready"], h0 + k + 1)
                    for c in range(2):
                        last = mm3(pair[:, j, c, 0:width], whi[:, c, k], wlo[:, c, k], h_hi[:, k, 0:width],
                                   h_lo[:, k, 0:width], k == 0, k == KD - 1)
                last.then_inc(S["pe_unit"], 1)

            def unit_down(u, j, rows, width, u_gu):
                wait_unit(u)
                for r in range(rows):
                    pe.wait_ge(S["pair_free"], u_gu + r + 3)
                    last = mm3(pair[:, j, 0, 0:width], w_hi[:, j, r * P:(r + 1) * P], w_lo[:, j, r * P:(r + 1) * P],
                               a_hi[:, r, 0:width], a_lo[:, r, 0:width], r == 0, r == rows - 1)
                last.then_inc(S["pe_unit"], 1)

            def norm(n, u_prev, tiles, bank=1):
                pe.wait_ge(S["ss_ready"], NSS[n])
                rows_sum(ssum, n, tiles)
                rows_bcast(psx[:, bank], n, tiles * P)

            def ffn(l, f, width):
                u = U_FFN[(l, f)]
                h0 = H0[(l, 2 * f)]
                for half, rows in enumerate(HALVES):
                    key = ("gu", l, f, half)
                    na = APLAN.get(key, 0)
                    u_gu = u

                    def body(it, with_ada):
                        for j in range(2):
                            unit_gu(u + 2 * it + j, j, width, h0)
                            if with_ada:
                                ada_mm(2 * it + (A0[key] + j))
                    if na:
                        with pe.Fori(0, na) as it:
                            body(it, True)
                    if rows // 2 > na:
                        with pe.Fori(na, rows // 2) as it:
                            body(it, False)
                    u += rows
                    key = ("down", l, f, half)
                    na = APLAN.get(key, 0)

                    def dbody(it, with_ada):
                        for j in range(2):
                            unit_down(u + 2 * it + j, j, rows, width, u_gu)
                            if with_ada:
                                ada_mm(2 * it + (A0[key] + j))
                    if na:
                        with pe.Fori(0, na) as it:
                            dbody(it, True)
                    if KD // 2 > na:
                        with pe.Fori(na, KD // 2) as it:
                            dbody(it, False)
                    u += KD

            pe.wait_ge(S["consts_in"], 16)
            pe.wait_ge(S["vecs_in"], 32)
            nc.tensor.transpose(psx[:, 0, 0:P], vrows[:, 0:P], ident).then_inc(S["pe_unit"], 1)
            nc.tensor.transpose(psx[:, 0, P:ROWS], vrows[0:ROWS - P, P:2 * P], ident[0:ROWS - P, 0:ROWS - P]
                                ).then_inc(S["vec_tr"], 1)
            pe.wait_ge(S["dec_in"], 16)
            mm(psx[:, 1, 0:2 * RH], ones[0:1, :], dec_row[:, :], start=True, stop=True).then_inc(S["dec_mm"], 1)

            def x_transposes(d):
                xin = park[:, :, :].rearrange("p (t a) n -> p t (a n)", t=4)
                if d >= 4:
                    pe.wait_ge(S["x_up"], d - 3)
                for t in range(4):
                    last = nc.tensor.transpose(pair[:, (d % 4) // 2, d % 2, t * P:(t + 1) * P],
                                               xin[:, t, d * P:(d + 1) * P], ident)
                last.then_inc(S["x_tr"], 1)

            slots3 = [raw[:, 0, :], raw[:, 1, :], ada[:, :]]
            for a in range(ADA_PRO):
                if a == 0:
                    pe.wait_ge(S["s_rdy"], 1)
                if a == 3:
                    pe.wait_ge(S["x_in"], 32)
                    for d in range(KD):
                        x_transposes(d)
                pe.wait_ge(pro_landed[a % 3], 16 * (a // 3 + 1))
                w = slots3[a % 3].rearrange("p (k c n) -> p k c n", k=KD, c=2)
                for c in range(2):
                    for k in range(KD):
                        last = mm(ps_s[:, 16 + 4 * a + 2 * c:18 + 4 * a + 2 * c], w[:, k, c], sT[:, k, :],
                                  start=k == 0, stop=k == KD - 1)
                last.then_inc(S["pro_mm"], 1)

            pe.wait_ge(S["mod_up"], 1)
            norm(0, 0, 4)
            ffn(0, 0, N)
            pe.wait_ge(S["mod_ready"], MODS_NORM[(0, 1)])
            norm(1, 0, 4)

            def retention(hd, last_head):
                U = U_RET + 8 * hd
                A = A0["ret"] + 8 * hd
                h0 = H0[(0, 1)]
                for j in (0, 1):
                    unit_cols(U + j, j, N, h0)
                    ada_mm(A + j)
                for j in (2, 3):
                    wait_unit(U + j)
                    whi = w_hi[:, j % 2, :].rearrange("p (k n) -> p k n", k=KD)
                    wlo = w_lo[:, j % 2, :].rearrange("p (k n) -> p k n", k=KD)
                    for t in range(4):
                        dst = pair[:, j % 2, t // 2, (t % 2) * 256:(t % 2 + 1) * 256]
                        for k in range(KD):
                            last = mm3(dst, h_hi[:, k, t * P:(t + 1) * P], h_lo[:, k, t * P:(t + 1) * P],
                                       whi[:, k], wlo[:, k], k == 0, k == KD - 1)
                    last.then_inc(S["pe_unit"], 1)
                    ada_mm(A + j)
                pe.wait_ge(S["pair_free"], U + 3 + 1)
                for g in range(3):
                    for kt, q0, qn in ([(2 + g, 0, N)] if g < 2 else [(0, 0, LAT), (1, LAT, LAT)]):
                        for c in range(2):
                            last = mm3(psx[:, g, q0:q0 + qn], a_hi[:, CH_K + c, kt * P:(kt + 1) * P],
                                       a_lo[:, CH_K + c, kt * P:(kt + 1) * P], a_hi[:, CH_Q + c, 0:qn],
                                       a_lo[:, CH_Q + c, 0:qn], c == 0, c == 1)
                    last.then_inc(S["s_mm"], 1)
                unit_cols(U + 4, 0, N, h0)
                ada_mm(A + 4)
                pe.wait_ge(S["s_split"], 3 * hd + 3)
                pe.wait_ge(S["pair_free"], U + 5 + 1)
                for e in range(4):
                    bank = psx[:, e % 3]
                    if e == 3:
                        pe.wait_ge(S["o_copied"], 4 * hd + 1)
                    for n, (kt, ch, c0, qn) in enumerate(((2, 0, 0, N), (3, 1, 0, N), (0, 2, 0, LAT), (1, 2, LAT, LAT))):
                        last = mm3(bank[:, 0:qn], a_hi[:, CH_V + kt, e * P:(e + 1) * P],
                                   a_lo[:, CH_V + kt, e * P:(e + 1) * P], a_hi[:, CH_S + ch, c0:c0 + qn],
                                   a_lo[:, CH_S + ch, c0:c0 + qn], n == 0, n == 3)
                    last.then_inc(S["o_mm"], 1)
                wait_unit(U + 5)
                whi = w_hi[:, 1, :].rearrange("p (k c n) -> p k c n", k=KD, c=2)
                wlo = w_lo[:, 1, :].rearrange("p (k c n) -> p k c n", k=KD, c=2)
                for c in range(2):
                    for k in range(KD):
                        last = mm3(pair[:, 1, c], whi[:, k, c], wlo[:, k, c], h_hi[:, k], h_lo[:, k],
                                   k == 0, k == KD - 1)
                        if c == 1 and k == 3:
                            pe.wait_ge(S["o_copied"], 4 * hd + 4)
                            rows_bcast(psx[:, 1], S_RET + hd, N)
                    if c == 0:
                        pe.wait_ge(S["pool_step"], 3 * hd + (POOL_RET + 3))
                        pe.wait_ge(S["mod_ready"], A + (5 - ADA_PRO))
                        rows_sum(ssum, S_RET + hd, 4)
                last.then_inc(S["pe_unit"], 1)
                ada_mm(A + 5)
                for j in (6, 7):
                    wait_unit(U + j)
                    whi = w_hi[:, j % 2, :].rearrange("p (k n) -> p k n", k=4)
                    wlo = w_lo[:, j % 2, :].rearrange("p (k n) -> p k n", k=4)
                    for i in range(4):
                        dst = (pair[:, j % 2, 0], pair[:, j % 2, 1], psx[:, 0], psx[:, 2])[i]
                        if i == 2:
                            pe.wait_ge(S["o_copied"], 4 * hd + 4)
                            pe.wait_ge(S["pair_free"], U + (j + 1) + 1)
                        for k in range(4):
                            pe.wait_ge(S["og_lo"], 4 * hd + (k + 1))
                            last = mm3(dst, whi[:, k, i * P:(i + 1) * P], wlo[:, k, i * P:(i + 1) * P],
                                       a_hi[:, k], a_lo[:, k], k == 0, k == 3)
                    last.then_inc(S["pe_unit"], 1)
                    ada_mm(A + j)

            with pe.Fori(0, RH - 1) as hd:
                retention(hd, False)
            retention(RH - 1, True)
            pe.wait_ge(S["mod_ready"], MODS_NORM[(0, 2)])
            norm(S_NORM[(0, 2)], 0, 4)
            ffn(0, 1, N)
            pe.wait_ge(S["mod_ready"], MODS_NORM[(1, 0)])
            norm(S_NORM[(1, 0)], 0, 4)
            ffn(1, 0, N)
            norm(S_NORM[(1, 1)], 0, 4)

            h0 = H0[(1, 1)]
            U = U_GQA

            def job_stats(job, bank):
                pe.wait_ge(S["g_sq"], job + 1)
                rows_sum(sq if job % 2 else ssum, S_GQA + job, 4)
                rows_bcast(psx[:, bank], S_GQA + job, N)
            unit_cols(U, 0, N, h0)
            wait_unit(U + 1)
            whi = w_hi[:, 1, :].rearrange("p (k n) -> p k n", k=KD)
            wlo = w_lo[:, 1, :].rearrange("p (k n) -> p k n", k=KD)
            for t in range(4):
                for k in range(KD):
                    last = mm3(pair[:, 1, t // 2, (t % 2) * 256:(t % 2 + 1) * 256], h_hi[:, k, t * P:(t + 1) * P],
                               h_lo[:, k, t * P:(t + 1) * P], whi[:, k], wlo[:, k], k == 0, k == KD - 1)
                if t == 0:
                    job_stats(0, 0)
                if t == 2:
                    job_stats(1, 1)
            last.then_inc(S["pe_unit"], 1)
            for i in range(4):
                j = i % 2
                unit_cols(U + 2 + i, j, LAT, h0, [pair[:, j, 0, 0:LAT], pair[:, j, 1, 0:LAT]])
                if i > 0:
                    pe.wait_ge(S["kn_lo"], 2 + i - 1)
                    job_stats(2 + i - 1, (i - 1) % 2)
            pe.wait_ge(S["kn_lo"], 4)
            job_stats(5, 1)

            def scores(hh):
                g = hh // (AH // AKV)
                pe.wait_ge(S["kn_lo"], 3 + hh // 2)
                if hh >= 2:
                    pe.wait_ge(S["p_exp"], 2 * (hh - 2) + 2)
                else:
                    pe.wait_ge(S["pair_free"], U + 7 + 1)
                for qb in range(2):
                    c0 = (hh % 2) * LAT + qb * P
                    last = mm3(pair[:, hh % 2, qb], a_hi[:, CH_GQ + hh // 2, c0:c0 + P],
                               a_lo[:, CH_GQ + hh // 2, c0:c0 + P], a_hi[:, g], a_lo[:, g], True, True)
                    last.then_inc(S["sc_mm"], 1)

            scores(0)
            for hh in range(AH):
                g = hh // (AH // AKV)
                if hh + 1 < AH:
                    scores(hh + 1)
                for qb in range(2):
                    pe.wait_ge(S["p_ready"], 2 * hh + qb + 1)
                    if hh and qb == 0:
                        pe.wait_ge(S["pt_lo"], 2 * hh)
                    for kt in range(4):
                        last = nc.tensor.transpose(psx[:, kt // 2, (kt % 2) * LAT + qb * P:(kt % 2) * LAT + (qb + 1) * P],
                                                   park[:, 2 * (hh % 2) + qb, kt * P:(kt + 1) * P], ident)
                last.then_inc(S["pt_mm"], 1)
                if hh:
                    pe.wait_ge(S["oT_lo"], hh)
                for kt in range(4):
                    pe.wait_ge(S["pt_lo"], 2 * hh + kt // 2 + 1)
                    vt = (kt % 2) * 256 + g * P
                    last = mm3(psx[:, 2, 0:LAT], a_hi[:, CH_GV + kt // 2, vt:vt + P], a_lo[:, CH_GV + kt // 2, vt:vt + P],
                               a_hi[:, CH_GP + kt // 2, (kt % 2) * LAT:(kt % 2 + 1) * LAT],
                               a_lo[:, CH_GP + kt // 2, (kt % 2) * LAT:(kt % 2 + 1) * LAT], kt == 0, kt == 3)
                last.then_inc(S["oT_mm"], 1)
            for i in range(4):
                j = i % 2
                wait_unit(U + 6 + i)
                whi = w_hi[:, j, :].rearrange("p (k c n) -> p k c n", k=KD, c=2)
                wlo = w_lo[:, j, :].rearrange("p (k c n) -> p k c n", k=KD, c=2)
                for k in range(KD):
                    pe.wait_ge(S["oT_lo"], k + 1)
                    src = (CH_GO + k // 2, (k % 2) * LAT)
                    for c in range(2):
                        last = mm3(pair[:, j, c, 0:LAT], whi[:, k, c], wlo[:, k, c],
                                   a_hi[:, src[0], src[1]:src[1] + LAT], a_lo[:, src[0], src[1]:src[1] + LAT],
                                   k == 0, k == KD - 1)
                last.then_inc(S["pe_unit"], 1)
            norm(S_NORM[(1, 2)], 0, 2)
            ffn(1, 1, LAT)
            norm(S_FIN, 0, 2)
            for d in range(KD):
                pe.wait_ge(S["fin_ready"], d + 1)
                for t in range(2):
                    last = nc.tensor.transpose(pair[:, t, d // 4, (d % 4) * P:(d % 4 + 1) * P],
                                               tmp[:, d % 2, t * P:(t + 1) * P], ident)
                last.then_inc(S["fin_tr"], 1)

        @block.scalar
        def _(act):
            fn = nc.scalar.activation

            def split_hi(base, it, off, mul=2):
                slot = off % 2
                act.wait_ge(raw_landed[slot], it * (16 * mul) + 32 * ((base + off) // 2 + 1))
                v = it * mul + (base + off)
                if not isinstance(v, int) or v >= 2:
                    act.wait_ge(S["pe_unit"], v)
                fn(w_hi[:, slot, :], raw[:, slot, :], ACT.Copy).then_inc(S["hi_ready"], 1)

            def norm(n, l, third, width):
                act.wait_ge(S["st_sum"], n + 1)
                fn(sd[:, 0:width // P], ps_s[:, 8:8 + width // P], ACT.Sqrt, scale=1.0 / D, bias=EPS
                   ).then_inc(S["st_sqrt"], 1)
                if l is None:
                    return
                h0 = H0[(l, third)]
                for d in range(KD):
                    act.wait_ge(S["t_ready"], h0 + d + 1)
                    for cond in range(width // 256):
                        q = (l * NMOD + 3 * third) * KD + d
                        last = fn(h_hi[:, d, cond * 256:(cond + 1) * 256], tmp[:, d % 2, cond * 256:(cond + 1) * 256],
                                  ACT.Identity, scale=aff[:, d, cond:cond + 1], bias=modT[:, q, cond:cond + 1])
                    last.then_inc(S["n_hi"], 1)

            def ffn(l, f, width):
                u = U_FFN[(l, f)]
                g = G_FFN[(l, f)]
                act_last = (l, f) == (1, 1)
                nc.scalar.preload_act_table(ACT.Silu)
                for half, rows in enumerate(HALVES):
                    with act.Fori(0, rows // 2) as it:
                        for j in range(2):
                            uu = u + 2 * it + j
                            gg = g + 2 * it + j
                            split_hi(u, it, j + 1)
                            act.wait_ge(S["pe_unit"], uu + 2)
                            fn(tmp[:, j, 0:width], pair[:, j, 0, 0:width], ACT.Silu).then_inc(S["silu_ready"], 1)
                            act.wait_ge(S["u_ready"], gg + 1)
                            fn(a_hi[:, bass.ds(2 * it + j, 1), 0:width], full[:, j:j + 1, 0:width], ACT.Copy
                               ).then_inc(S["u_hi"], 1)
                    u += rows
                    g += rows
                    last = act_last and half == 1
                    with act.Fori(0, KD // 2 - last) as it:
                        for j in range(2):
                            split_hi(u, it, j + 1)
                    if last:
                        split_hi(u, KD // 2 - 1, 1)
                    u += KD

            act.wait_ge(S["vec_up"], 1)
            for cond, row in enumerate((ROW_C, ROW_CX)):
                last = fn(sT[:, :, cond], vecT[:, row:row + KD], ACT.Silu)
            last.then_inc(S["s_rdy"], 1)
            act.wait_ge(S["dec_mm"], 1)
            fn(lg[:, :], psx[:, 1, 0:2 * RH], ACT.Exp).then_inc(S["dec_exp"], 1)
            split_hi(0, 0, 0)
            norm(0, 0, 0, N)
            ffn(0, 0, N)
            norm(1, 0, 1, N)

            def retention(hd):
                U = U_RET + 8 * hd
                for j in range(8):
                    split_hi(U_RET, hd, j + 1, 8)
                    if j < 2:
                        ch, sc = (CH_Q, 1.0) if j == 0 else (CH_K, RDK ** -0.5)
                        act.wait_ge(S["pe_unit"], U + (j + 1) + 1)
                        fn(a_hi[:, ch:ch + 2, LAT:N], pair[:, j % 2, :, LAT:N], ACT.Copy, scale=sc
                           ).then_inc(S["q_ctx_hi"], 1)
                        act.wait_ge(S["rot_ready"], 2 * hd + (j + 1))
                        fn(a_hi[:, ch:ch + 2, 0:LAT], full[:, j, :].rearrange("p (c n) -> p c n", c=2), ACT.Copy, scale=sc
                           ).then_inc(S["q_lat_hi"], 1)
                    elif j < 4:
                        if j == 2:
                            act.wait_ge(S["e_pre"], 4 * hd + 4)
                            fn(o_buf[:, :, 0:BAND], o_buf[:, :, 0:BAND], ACT.Exp).then_inc(S["e_exp"], 1)
                        act.wait_ge(S["pe_unit"], U + (j + 1) + 1)
                        fn(a_hi[:, CH_V:CH_V + 4, (j - 2) * 256:(j - 1) * 256],
                           pair[:, j % 2, :, :].rearrange("p b (t n) -> p (b t) n", t=2), ACT.Copy
                           ).then_inc(S["v_hi"], 1)
                        if j == 3:
                            for g in range(3):
                                act.wait_ge(S["ms_ready"], 3 * hd + (g + 1))
                                fn(a_hi[:, CH_S + g, :], tmp[:, g % 2, :], ACT.Copy).then_inc(S["ms_hi"], 1)
                    elif j < 6:
                        if j == 5:
                            for e in range(4):
                                act.wait_ge(S["o_copied"], 4 * hd + (e + 1))
                                if e == 0:
                                    fn(ssum[:, :], o_buf[:, 0, :], ACT.Square).then_inc(S["o_sq"], 1)
                                    continue
                                if e > 1:
                                    act.wait_ge(S["pool_step"], 3 * hd + (POOL_RET + e - 1))
                                fn(sq[:, :], o_buf[:, e, :], ACT.Square).then_inc(S["o_sq"], 1)
                            act.wait_ge(S["st_sum"], S_RET + 1 + hd)
                            fn(sd[:, :], ps_s[:, 8:12], ACT.Sqrt, scale=1.0 / RDV, bias=EPS
                               ).then_inc(S["st_sqrt"], 1)
                        act.wait_ge(S["pe_unit"], U + (j + 1) + 1)
                        fn(sg_buf[:, 2 * (j - 4):2 * (j - 3), :], pair[:, j % 2, :, :], ACT.Silu
                           ).then_inc(S["sg_ready"], 1)
                        if j == 5:
                            for e in range(4):
                                act.wait_ge(S["og_ready"], 4 * hd + (e + 1))
                                fn(a_hi[:, e, :], tmp[:, e % 2, :], ACT.Copy).then_inc(S["og_hi"], 1)

            with act.Fori(0, RH) as hd:
                retention(hd)
            norm(S_NORM[(0, 2)], 0, 2, N)
            ffn(0, 1, N)
            norm(S_NORM[(1, 0)], 1, 0, N)
            ffn(1, 0, N)
            norm(S_NORM[(1, 1)], 1, 1, N)

            U = U_GQA

            def square(job, src):
                if job >= 2:
                    act.wait_ge(S["st_sum"], S_GQA + job - 1)
                fn((sq if job % 2 else ssum)[:, :], src, ACT.Square).then_inc(S["g_sq"], 1)

            def root(job):
                act.wait_ge(S["st_sum"], S_GQA + job + 1)
                fn(sd[:, :], ps_s[:, 8:12], ACT.Sqrt, scale=1.0 / AHD, bias=EPS).then_inc(S["st_sqrt"], 1)

            def job_hi(job):
                act.wait_ge(S["kn_ready"], job + 1)
                fn(a_hi[:, job if job < 2 else CH_GQ + job - 2, :], full[:, 0, :], ACT.Copy).then_inc(S["kn_hi"], 1)
            split_hi(U, 0, 1)
            act.wait_ge(S["pe_unit"], U + 2)
            square(0, pair[:, 0, 0])
            square(1, pair[:, 0, 1])
            root(0)
            root(1)
            split_hi(U, 0, 2)
            job_hi(0)
            job_hi(1)
            act.wait_ge(S["pe_unit"], U + 3)
            fn(a_hi[:, CH_GV:CH_GV + 2, :], pair[:, 1, :, :], ACT.Copy).then_inc(S["gv_hi"], 1)
            for i in range(4):
                split_hi(U, 0, 3 + i)
                act.wait_ge(S["pe_unit"], U + 3 + i + 1)
                square(2 + i, pair[:, i % 2, :, 0:LAT])
                root(2 + i)
                job_hi(2 + i)
            split_hi(U, 0, 7)

            def probs(hh, qb):
                act.wait_ge(S["nb_ready"], 2 * hh + qb + 1)
                n = 2 * hh + qb
                fn(park[:, 2 * (hh % 2) + qb, :], pair[:, hh % 2, qb], ACT.Exp, bias=snb[:, n:n + 1],
                   scale=AHD ** -0.5, accum_out=sden[:, n:n + 1]).then_inc(S["p_exp"], 1)
            probs(0, 0)
            probs(0, 1)
            for hh in range(AH):
                if hh + 1 < AH:
                    if hh >= 1:
                        act.wait_ge(S["pt_mm"], hh)
                    probs(hh + 1, 0)
                    probs(hh + 1, 1)
                act.wait_ge(S["pt_mm"], hh + 1)
                if hh:
                    act.wait_ge(S["oT_mm"], hh)
                for b in range(2):
                    fn(a_hi[:, CH_GP + b, :], psx[:, b], ACT.Copy).then_inc(S["pt_hi"], 1)
                act.wait_ge(S["oT_mm"], hh + 1)
                fn(a_hi[:, CH_GO + hh // 2, (hh % 2) * LAT:(hh % 2 + 1) * LAT], psx[:, 2, 0:LAT], ACT.Copy
                   ).then_inc(S["oT_hi"], 1)
            for i in range(3):
                split_hi(U, 0, 8 + i)
            norm(S_NORM[(1, 2)], 1, 2, LAT)
            ffn(1, 1, LAT)
            norm(S_FIN, None, 0, LAT)

        @block.vector
        def _(dve):
            V = nc.vector
            step = Steps(S["dve_step"])

            def after(value):
                dve.wait_ge(S["dve_step"], value)

            def split_lo(v, slot):
                dve.wait_ge(S["hi_ready"], v + 1)
                V.tensor_tensor(w_lo[:, slot, :], raw[:, slot, :], f32(w_hi[:, slot, :]), ALU.subtract
                                ).then_inc(S["lo_ready"], 1)

            def ada_sum(a):
                w = ada[:, :].rearrange("p (k n) -> p k n", k=KD)
                dve.wait_ge(S["ada_landed"], (a - (ADA_PRO - 1)) * 16)
                ready = {}
                for k in range(KD):
                    for cond in range(2):
                        s = sT[:, k, cond:cond + 1]
                        if k == 0:
                            ins = V.tensor_scalar(acc[:, cond, :], w[:, k], s, None, ALU.mult)
                        else:
                            after(ready[cond])
                            ins = V.scalar_tensor_tensor(out=acc[:, cond, :], in0=w[:, k], scalar=s,
                                                         in1=acc[:, cond, :], op0=ALU.mult, op1=ALU.add)
                        if k == KD - 1 and cond == 1:
                            ins.then_inc(S["acc_ready"], 1)
                        else:
                            ready[cond] = step.mark(ins)

            def ada_out(a):
                dve.wait_ge(S["ada_mm"], a - (ADA_PRO - 1))
                V.tensor_tensor(modT[:, bass.ds(2 * a, 2), :], ps_s[:, 0:4].rearrange("p (c o) -> p c o", o=2),
                                vecT[:, bass.ds(2 * a, 2)].unsqueeze(2).to_broadcast([P, 2, 2]), ALU.add
                                ).then_inc(S["mod_ready"], 1)
            ADA_STEPS = 2 * KD - 1

            def norm_rstd(n, count, width):
                tiles = width // P
                dve.wait_ge(S["st_sqrt"], n + 1)
                r = step.mark(V.reciprocal(rs[:, 0:tiles], sd[:, 0:tiles]))
                after(r)
                for t in range(tiles):
                    last = V.tensor_scalar(diag[:, t * P:(t + 1) * P], ident, rs[:, t:t + 1], None, ALU.mult)
                last.then_inc(S["st_diag"], 1)

            def norm(n, l, third, width):
                g0 = ROW_NG + (3 * l + third) * KD
                q0 = (l * NMOD + 3 * third) * KD
                if MODS_NORM[(l, third)]:
                    dve.wait_ge(S["mod_ready"], MODS_NORM[(l, third)])
                V.scalar_tensor_tensor(out=aff[:, :, :], in0=modT[:, q0 + KD:q0 + 2 * KD, :], scalar=1.0,
                                       in1=vecT[:, g0:g0 + KD].unsqueeze(2).to_broadcast([P, KD, 2]),
                                       op0=ALU.add, op1=ALU.mult)
                norm_rstd(n, 1, width)
                dve.wait_ge(S["st_bcast"], n + 1)
                h0 = H0[(l, third)]

                def t(d):
                    V.tensor_tensor(tmp[:, d % 2, 0:width], xT[:, d, 0:width], psx[:, 1, 0:width], ALU.mult
                                    ).then_inc(S["t_ready"], 1)
                t(0)
                for d in range(KD):
                    if d + 1 < KD:
                        t(d + 1)
                    dve.wait_ge(S["t_ready"], h0 + d + 1)
                    if d >= 2:
                        dve.wait_ge(S["h_ready"], h0 + d - 1)
                    for cond in range(width // 256):
                        v = step.mark(V.tensor_scalar(
                            full[:, d % 2, cond * 256:(cond + 1) * 256], tmp[:, d % 2, cond * 256:(cond + 1) * 256],
                            aff[:, d, cond:cond + 1], modT[:, q0 + d, cond:cond + 1], ALU.mult, ALU.add))
                    dve.wait_ge(S["n_hi"], h0 + d + 1)
                    after(v)
                    V.tensor_tensor(h_lo[:, d, 0:width], full[:, d % 2, 0:width], f32(h_hi[:, d, 0:width]), ALU.subtract
                                    ).then_inc(S["h_ready"], 1)
                dve.wait_ge(S["h_ready"], h0 + KD)

            def gates(l, m, factor):
                q = (l * NMOD + m) * KD
                after(step.mark(V.tensor_scalar(gate[:, :, :], modT[:, q:q + KD, :], factor, None, ALU.mult)))

            def add_x(d, src, width, done):
                dd = bass.ds(d, 1)
                for cond in range(width // 256):
                    cols = slice(cond * 256, (cond + 1) * 256)
                    ins = V.scalar_tensor_tensor(out=xT[:, dd, cols], in0=src[:, cols].unsqueeze(1),
                                                 scalar=gate[:, dd, cond], in1=xT[:, dd, cols],
                                                 op0=ALU.mult, op1=ALU.add)
                if done:
                    ins.then_inc(S["pair_free"], 1)

            def ffn(l, f, width):
                u = U_FFN[(l, f)]
                g = G_FFN[(l, f)]
                for half, rows in enumerate(HALVES):
                    key = ("gu", l, f, half)
                    na = APLAN.get(key, 0)

                    def body(it, with_ada):
                        for j in range(2):
                            uu = u + 2 * it + j
                            gg = g + 2 * it + j
                            split_lo(uu + 1, (j + 1) % 2)
                            if with_ada:
                                ada_sum(2 * it + (A0[key] + j))
                            dve.wait_ge(S["silu_ready"], gg + 1)
                            V.tensor_tensor(full[:, j, 0:width], tmp[:, j, 0:width], pair[:, j, 1, 0:width], ALU.mult
                                            ).then_inc(S["u_ready"], 1)
                            dve.wait_ge(S["u_hi"], gg + 1)
                            dve.wait_ge(S["u_ready"], gg + 1)
                            cc = bass.ds(2 * it + j, 1)
                            V.tensor_tensor(a_lo[:, cc, 0:width], full[:, j:j + 1, 0:width],
                                            f32(a_hi[:, cc, 0:width]), ALU.subtract).then_inc(S["pair_free"], 1)
                            if with_ada:
                                ada_out(2 * it + (A0[key] + j))
                    for lo, hi, with_ada in ((0, na, True), (na, rows // 2, False)):
                        if hi > lo:
                            with dve.Fori(lo, hi) as it:
                                step.enter(it - lo if lo else it, 2 * ADA_STEPS if with_ada else 0)
                                body(it, with_ada)
                            step.leave(hi - lo)
                    u += rows
                    g += rows
                    key = ("down", l, f, half)
                    na = APLAN.get(key, 0)
                    if half == 0:
                        dve.wait_ge(S["mod_ready"], MODS_AT[(l, f)])
                        gates(l, 6 * f + 2, 0.5)

                    def dbody(it, with_ada, skip_split=False):
                        for j in range(2):
                            uu = u + 2 * it + j
                            if not (skip_split and j == 1):
                                split_lo(uu + 1, (j + 1) % 2)
                            if with_ada:
                                ada_sum(2 * it + (A0[key] + j))
                            dve.wait_ge(S["pe_unit"], uu + 2)
                            add_x(2 * it + j, pair[:, j, 0], width, True)
                            if with_ada:
                                ada_out(2 * it + (A0[key] + j))
                    last = (l, f, half) == (1, 1, 1)
                    for lo, hi, with_ada in ((0, na, True), (na, KD // 2 - last, False)):
                        if hi > lo:
                            with dve.Fori(lo, hi) as it:
                                step.enter(it - lo if lo else it, 2 * ADA_STEPS if with_ada else 0)
                                dbody(it, with_ada)
                            step.leave(hi - lo)
                    if last:
                        dbody(KD // 2 - 1, False, True)
                    u += KD

            dve.wait_ge(S["vec_tr"], 1)
            V.tensor_copy(vecT[:, :], psx[:, 0, 0:ROWS]).then_inc(S["vec_up"], 1)
            for d in range(KD):
                dve.wait_ge(S["x_tr"], d + 1)
                V.tensor_copy(xT[:, d, :], pair[:, (d % 4) // 2, d % 2]).then_inc(S["x_up"], 1)
            dve.wait_ge(S["dec_exp"], 1)
            V.tensor_scalar(lg[:, :], lg[:, :], -1.0, None, ALU.mult).then_inc(S["pair_free"], 2)
            dve.wait_ge(S["pro_mm"], ADA_PRO)
            dve.wait_ge(S["vec_up"], 1)
            V.tensor_tensor(modT[:, 0:2 * ADA_PRO, :], ps_s[:, 16:16 + 4 * ADA_PRO].rearrange("p (q o) -> p q o", o=2),
                            vecT[:, 0:2 * ADA_PRO].unsqueeze(2).to_broadcast([P, 2 * ADA_PRO, 2]), ALU.add
                            ).then_inc(S["mod_up"], 1)
            dve.wait_ge(S["mod_up"], 1)
            split_lo(0, 0)
            norm(0, 0, 0, N)
            ffn(0, 0, N)
            norm(1, 0, 1, N)

            gates(0, 5, 1.0)

            def retention(hd):
                U = U_RET + 8 * hd
                A = A0["ret"] + 8 * hd
                for j in range(8):
                    split_lo(U + (j + 1), (j + 1) % 2)
                    if j != 5:
                        ada_sum(A + j)
                    p = j % 2
                    if j < 2:
                        ch, sc = (CH_Q, 1.0) if j == 0 else (CH_K, RDK ** -0.5)
                        dve.wait_ge(S["q_ctx_hi"], 2 * hd + (j + 1))
                        x1, x2 = pair[:, p, 0, 0:LAT], pair[:, p, 1, 0:LAT]
                        V.tensor_tensor(tmp[:, 0, 0:LAT], x1, rcos, ALU.mult)
                        step.mark(V.tensor_tensor(tmp[:, 0, LAT:N], x2, rsin, ALU.mult))
                        V.tensor_tensor(tmp[:, 1, 0:LAT], x2, rcos, ALU.mult)
                        v = step.mark(V.tensor_tensor(tmp[:, 1, LAT:N], x1, rsin, ALU.mult))
                        after(v - 1)
                        V.tensor_tensor(full[:, j, 0:LAT], tmp[:, 0, 0:LAT], tmp[:, 0, LAT:N], ALU.subtract)
                        after(v)
                        V.tensor_tensor(full[:, j, LAT:N], tmp[:, 1, 0:LAT], tmp[:, 1, LAT:N], ALU.add
                                        ).then_inc(S["rot_ready"], 1)
                        for cols, src, name in ((slice(LAT, N), pair[:, p, :, LAT:N], "q_ctx_hi"),
                                                (slice(0, LAT), full[:, j, :].rearrange("p (c n) -> p c n", c=2), "q_lat_hi")):
                            dve.wait_ge(S[name], 2 * hd + (j + 1))
                            dve.wait_ge(S["rot_ready"], 2 * hd + (j + 1))
                            ins = V.scalar_tensor_tensor(out=a_lo[:, ch:ch + 2, cols], in0=src, scalar=sc,
                                                         in1=f32(a_hi[:, ch:ch + 2, cols]), op0=ALU.mult,
                                                         op1=ALU.subtract)
                        ins.then_inc(S["pair_free"], 1)
                    elif j < 4:
                        if j == 2:
                            lf, lb = lg[:, bass.ds(hd, 1)], lg[:, bass.ds(hd + RH, 1)]
                            V.tensor_scalar(o_buf[:, 0, 0:BAND], diff, 0.0, lf, ALU.max, ALU.mult).then_inc(S["e_pre"], 1)
                            V.tensor_scalar(tmp[:, 0, 0:BAND], diff, -1.0, 0.0, ALU.mult, ALU.max)
                            v = step.mark(V.tensor_scalar(tmp[:, 1, 0:BAND], diff, -1.0, float(LAT), ALU.mult, ALU.add))
                            V.tensor_scalar(o_buf[:, 2, 0:BAND], diff, float(LAT), lf, ALU.add, ALU.mult).then_inc(S["e_pre"], 1)
                            after(v)
                            V.tensor_scalar(o_buf[:, 1, 0:BAND], tmp[:, 0, 0:BAND], lb, None, ALU.mult).then_inc(S["e_pre"], 1)
                            V.tensor_scalar(o_buf[:, 3, 0:BAND], tmp[:, 1, 0:BAND], lb, None, ALU.mult).then_inc(S["e_pre"], 1)
                            dve.wait_ge(S["e_exp"], hd + 1)
                            dve.wait_ge(S["e_pre"], 4 * hd + 4)
                            V.scalar_tensor_tensor(out=tmp[:, 0, 0:BAND], in0=diff, scalar=0.0, in1=o_buf[:, 0, 0:BAND],
                                                   op0=ALU.is_ge, op1=ALU.mult)
                            v = step.mark(V.scalar_tensor_tensor(out=tmp[:, 1, 0:BAND], in0=diff, scalar=0.0,
                                                                 in1=o_buf[:, 1, 0:BAND], op0=ALU.is_le, op1=ALU.mult))
                            V.tensor_tensor(band[:, 1, :], o_buf[:, 2, 0:BAND], o_buf[:, 3, 0:BAND], ALU.add)
                            after(v)
                            step.mark(V.tensor_tensor(band[:, 0, :], tmp[:, 0, 0:BAND], tmp[:, 1, 0:BAND], ALU.add))
                        dve.wait_ge(S["v_hi"], 2 * hd + (j - 1))
                        cols = slice((j - 2) * 256, (j - 1) * 256)
                        V.tensor_tensor(a_lo[:, CH_V:CH_V + 4, cols],
                                        pair[:, p, :, :].rearrange("p b (t n) -> p (b t) n", t=2),
                                        f32(a_hi[:, CH_V:CH_V + 4, cols]), ALU.subtract).then_inc(S["pair_free"], 1)
                        if j == 3:
                            after(band_step(step))
                            near, far = band[:, 0], band[:, 1]
                            lo_, hi_ = slice(P, BAND), slice(0, LAT)

                            def masked(g):
                                dve.wait_ge(S["s_mm"], 3 * hd + (g + 1))
                                m0, m1 = ((far[:, lo_], near[:, lo_]), (far[:, hi_], near[:, hi_]),
                                          (near[:, lo_], near[:, hi_]))[g]
                                V.tensor_tensor(tmp[:, g % 2, 0:LAT], psx[:, g, 0:LAT], m0, ALU.mult)
                                V.tensor_tensor(tmp[:, g % 2, LAT:N], psx[:, g, LAT:N], m1, ALU.mult
                                                ).then_inc(S["ms_ready"], 1)

                            def masked_lo(g):
                                dve.wait_ge(S["ms_hi"], 3 * hd + (g + 1))
                                dve.wait_ge(S["ms_ready"], 3 * hd + (g + 1))
                                V.tensor_tensor(a_lo[:, CH_S + g, :], tmp[:, g % 2, :], f32(a_hi[:, CH_S + g, :]),
                                                ALU.subtract).then_inc(S["s_split"], 1)
                            masked(0)
                            masked(1)
                            masked_lo(0)
                            dve.wait_ge(S["s_split"], 3 * hd + 1)
                            masked(2)
                            masked_lo(1)
                            masked_lo(2)
                    elif j == 4:
                        dve.wait_ge(S["sg_ready"], 2 * hd + 1)
                        V.memset(mark[:, :], 0.0).then_inc(S["pair_free"], 1)
                    elif j == 5:
                        for e in range(4):
                            dve.wait_ge(S["o_mm"], 4 * hd + (e + 1))
                            V.tensor_copy(o_buf[:, e, :], psx[:, e % 3]).then_inc(S["o_copied"], 1)
                        ada_sum(A + j)
                        norm_rstd(S_RET + hd, 1, N)
                        dve.wait_ge(S["st_bcast"], S_RET + 1 + hd)
                        dve.wait_ge(S["o_copied"], 4 * hd + 4)
                        for e in range(4):
                            v = step.mark(V.tensor_tensor(o_buf[:, e, :], o_buf[:, e, :], psx[:, 1], ALU.mult))
                        dve.wait_ge(S["sg_ready"], 2 * hd + 2)
                        V.memset(mark[:, :], 0.0).then_inc(S["pair_free"], 1)
                        after(v)

                        def og(e):
                            V.tensor_tensor(tmp[:, e % 2, :], o_buf[:, e, :], sg_buf[:, e, :], ALU.mult
                                            ).then_inc(S["og_ready"], 1)
                        og(0)
                        for e in range(4):
                            if e in (1, 2):
                                dve.wait_ge(S["og_lo"], 4 * hd + e)
                            if e < 3:
                                og(e + 1)
                            dve.wait_ge(S["og_hi"], 4 * hd + (e + 1))
                            dve.wait_ge(S["og_ready"], 4 * hd + (e + 1))
                            V.tensor_tensor(a_lo[:, e, :], tmp[:, e % 2, :], f32(a_hi[:, e, :]), ALU.subtract
                                            ).then_inc(S["og_lo"], 1)
                    else:
                        dve.wait_ge(S["pe_unit"], U + (j + 1) + 1)
                        for i in range(4):
                            src = (pair[:, p, 0], pair[:, p, 1], psx[:, 0], psx[:, 2])[i]
                            add_x((j - 6) * 4 + i, src, N, i == 3)
                    ada_out(A + j)

            def band_step(s):
                return s.it * s.per + (s.base + s.local)
            RET_STEPS = 8 * ADA_STEPS + 2 * 2 + 3 + 1 + 4
            with dve.Fori(0, RH) as hd:
                step.enter(hd, RET_STEPS)
                retention(hd)
            step.leave(RH)
            norm(S_NORM[(0, 2)], 0, 2, N)
            ffn(0, 1, N)
            norm(S_NORM[(1, 0)], 1, 0, N)
            ffn(1, 0, N)
            norm(S_NORM[(1, 1)], 1, 1, N)

            U = U_GQA

            def job_norm(job, src, gain, halves):
                norm_rstd(S_GQA + job, 1, N)
                dve.wait_ge(S["st_bcast"], S_GQA + job + 1)
                R = psx[:, job % 2, :]
                if len(src.shape) == 3:
                    gi = full[:, 0, :].rearrange("p (c n) -> p c n", c=2)
                else:
                    gi = full[:, 0, :]
                v = step.mark(V.tensor_copy(park[:, 7, :], R))
                after(v)
                pk = park[:, 7, :].rearrange("p (c n) -> p c n", c=2) if len(src.shape) == 3 else park[:, 7, :]
                v = step.mark(V.scalar_tensor_tensor(out=gi, in0=src, scalar=vecT[:, gain:gain + 1], in1=pk,
                                                     op0=ALU.mult, op1=ALU.mult))
                after(v)
                w = halves * LAT
                V.tensor_copy(tmp[0:64, 0, 0:w], full[64:P, 0, 0:w])
                step.mark(V.tensor_copy(tmp[64:P, 0, 0:w], full[0:64, 0, 0:w]))
                for c in range(halves):
                    cs = slice(c * LAT, (c + 1) * LAT)
                    v = step.mark(V.tensor_tensor(tmp[:, 1, cs], full[:, 0, cs], acos, ALU.mult))
                after(v - halves)
                for c in range(halves):
                    cs = slice(c * LAT, (c + 1) * LAT)
                    v = step.mark(V.tensor_tensor(park[:, 6, cs], tmp[:, 0, cs], asin, ALU.mult))
                after(v)
                v = V.tensor_tensor(full[:, 0, 0:w], tmp[:, 1, 0:w], park[:, 6, 0:w], ALU.add)
                v.then_inc(S["kn_ready"], 1)
                ch = job if job < 2 else CH_GQ + job - 2
                dve.wait_ge(S["kn_hi"], job + 1)
                dve.wait_ge(S["kn_ready"], job + 1)
                V.tensor_tensor(a_lo[:, ch, :], full[:, 0, :], f32(a_hi[:, ch, :]), ALU.subtract).then_inc(S["kn_lo"], 1)
                dve.wait_ge(S["kn_lo"], job + 1)

            def release():
                V.memset(mark[:, :], 0.0).then_inc(S["pair_free"], 1)
            split_lo(U + 1, 1)
            job_norm(0, pair[:, 0, 0], ROW_KG, 1)
            job_norm(1, pair[:, 0, 1], ROW_KG, 1)
            release()
            split_lo(U + 2, 0)
            dve.wait_ge(S["gv_hi"], 1)
            V.tensor_tensor(a_lo[:, CH_GV:CH_GV + 2, :], pair[:, 1, :, :], f32(a_hi[:, CH_GV:CH_GV + 2, :]), ALU.subtract
                            ).then_inc(S["pair_free"], 1)
            for i in range(4):
                split_lo(U + 3 + i, (i + 1) % 2)
                job_norm(2 + i, pair[:, i % 2, :, 0:LAT], ROW_QG, 2)
                release()
            split_lo(U + 7, 1)

            def peak(hh):
                for qb in range(2):
                    n = 2 * hh + qb
                    dve.wait_ge(S["sc_mm"], n + 1)
                    v = step.mark(V.reduce_max(smx[:, n:n + 1], pair[:, hh % 2, qb], AX_X))
                    after(v)
                    V.tensor_scalar(snb[:, n:n + 1], smx[:, n:n + 1], -AHD ** -0.5, None, ALU.mult
                                    ).then_inc(S["nb_ready"], 1)
            peak(0)
            for hh in range(AH):
                for qb in range(2):
                    n = 2 * hh + qb
                    dve.wait_ge(S["p_exp"], n + 1)
                    v = step.mark(V.reciprocal(sinv[:, n:n + 1], sden[:, n:n + 1]))
                    after(v)
                    pb = park[:, 2 * (hh % 2) + qb, :]
                    V.tensor_scalar(pb, pb, sinv[:, n:n + 1], None, ALU.mult).then_inc(S["p_ready"], 1)
                if hh + 1 < AH:
                    peak(hh + 1)
                for b in range(2):
                    dve.wait_ge(S["pt_hi"], 2 * hh + b + 1)
                    V.tensor_tensor(a_lo[:, CH_GP + b, :], psx[:, b], f32(a_hi[:, CH_GP + b, :]), ALU.subtract
                                    ).then_inc(S["pt_lo"], 1)
                dve.wait_ge(S["oT_hi"], hh + 1)
                cs = slice((hh % 2) * LAT, (hh % 2 + 1) * LAT)
                V.tensor_tensor(a_lo[:, CH_GO + hh // 2, cs], psx[:, 2, 0:LAT], f32(a_hi[:, CH_GO + hh // 2, cs]),
                                ALU.subtract).then_inc(S["oT_lo"], 1)
            gates(1, 5, 1.0)
            for i in range(4):
                if i:
                    split_lo(U + 7 + i, (i + 1) % 2)
                dve.wait_ge(S["pe_unit"], U + 7 + i + 1)
                for c in range(2):
                    add_x(2 * i + c, pair[:, i % 2, c], LAT, c == 1)
            norm(S_NORM[(1, 2)], 1, 2, LAT)
            ffn(1, 1, LAT)
            norm_rstd(S_FIN, 1, LAT)
            dve.wait_ge(S["st_bcast"], S_FIN + 1)
            for d in range(KD):
                if d >= 2:
                    dve.wait_ge(S["fin_tr"], d - 1)
                V.scalar_tensor_tensor(out=tmp[:, d % 2, 0:LAT], in0=xT[:, d, 0:LAT], scalar=vecT[:, ROW_FG + d:ROW_FG + d + 1],
                                       in1=psx[:, 1, 0:LAT], op0=ALU.mult, op1=ALU.mult).then_inc(S["fin_ready"], 1)
            dve.wait_ge(S["fin_tr"], KD)
            for t in range(2):
                V.tensor_copy(park[:, 2 * t:2 * t + 2, :], pair[:, t, :, :]).then_inc(S["fin_copied"], 1)

        @block.gpsimd
        def _(pool):
            G = nc.gpsimd
            ps = Steps(S["pool_step"])

            def zero():
                pool.wait_ge(S["pool_step"], ps.mark(G.memset(ssum[:, :], 0.0)))

            def add_square(d, width, done):
                dd = bass.ds(d, 1)
                s3 = sq[:, 0:width].unsqueeze(1)
                v = ps.mark(G.tensor_tensor(s3, xT[:, dd, 0:width], xT[:, dd, 0:width], ALU.mult))
                pool.wait_ge(S["pool_step"], v)
                G.tensor_tensor(ssum[:, 0:width], ssum[:, 0:width], sq[:, 0:width], ALU.add).then_inc(S["ss_ready"], 1)

            def sweep(wait_of, width, n0, order=None):
                zero()
                for d in range(KD):
                    wait_of(d)
                    add_square(d, width, True)
                    pool.wait_ge(S["ss_ready"], n0 + d + 1)

            def sweep_ffn(l, f, width, n0):
                zero()
                u = U_FFN[(l, f)] + UNITS_FFN - KD
                with pool.Fori(0, KD) as d:
                    ps.enter(d, 1)
                    pool.wait_ge(S["pair_free"], u + 2 + d + 1)
                    add_square(d, width, True)
                    pool.wait_ge(S["ss_ready"], d + (n0 + 1))
                ps.leave(KD)

            sweep(lambda d: pool.wait_ge(S["x_up"], d + 1), N, 0)
            pool.wait_ge(S["st_sum"], 1)
            sweep_ffn(0, 0, N, 8)
            assert ps.base + ps.local == POOL_RET, (ps.base, ps.local)
            with pool.Fori(0, RH) as hd:
                ps.enter(hd, 3)
                for e in range(1, 4):
                    pool.wait_ge(S["o_sq"], 4 * hd + (e + 1))
                    v = ps.mark(G.tensor_tensor(ssum[:, :], ssum[:, :], sq[:, :], ALU.add))
                    pool.wait_ge(S["pool_step"], v)
            ps.leave(RH)
            pool.wait_ge(S["st_sum"], S_RET + RH)
            sweep(lambda d: pool.wait_ge(S["pair_free"], U_RET + 8 * (RH - 1) + 8 + d // 4 + 1), N, 16)
            pool.wait_ge(S["st_sum"], S_NORM[(0, 2)] + 1)
            sweep_ffn(0, 1, N, 24)
            pool.wait_ge(S["st_sum"], S_NORM[(1, 0)] + 1)
            sweep_ffn(1, 0, N, 32)
            pool.wait_ge(S["st_sum"], S_GQA + 6)
            sweep(lambda d: pool.wait_ge(S["pair_free"], U_GQA + 6 + d // 2 + 3), LAT, 40)
            pool.wait_ge(S["st_sum"], S_NORM[(1, 2)] + 1)
            sweep_ffn(1, 1, LAT, 48)


NSS = {0: 8, 1: 16, 6: 24, 7: 32, 8: 40, 15: 48, 16: 56}
H0 = {(0, 0): 0, (0, 1): 8, (0, 2): 16, (1, 0): 24, (1, 1): 32, (1, 2): 40}
POOL_RET = 1 + KD + 1 + KD
MODS_NORM = {(0, 0): 0, (0, 1): 28, (0, 2): 60, (1, 0): 64, (1, 1): 64, (1, 2): 64}
MODS_AT = {(0, 0): 12, (0, 1): 64, (1, 0): 64, (1, 1): 64}

_WEIGHTS = ["ada_w", "ffn_w1", "ffn_w2", "ret_w_in", "ret_w_out", "att_w_qkv", "att_w_o"]


def shape_constants():
    import numpy as np

    f = np.float32
    t = np.arange(LAT).astype(f)
    half = RDK // 2
    freq = (f(10000.0) ** (-np.arange(half, dtype=f) / f(half))).astype(f)
    ang = (freq[:, None] * t[None]).astype(f)
    quarter = AHD // 4
    qf = (f(10000.0) ** (-np.arange(quarter, dtype=f) / f(quarter))).astype(f)
    row, col = (np.arange(LAT) // 64).astype(f), (np.arange(LAT) % 64).astype(f)
    ax = np.concatenate([qf[:, None] * row[None], qf[:, None] * col[None]]).astype(f)
    sin = np.sin(ax.astype(np.float64))
    parts = [np.eye(P), np.ones((P, P)), np.arange(BAND)[None] - P - np.arange(P)[:, None],
             np.cos(ang.astype(np.float64)), np.sin(ang.astype(np.float64)),
             np.tile(np.cos(ax.astype(np.float64)), (2, 1)), np.concatenate([-sin, sin])]
    return np.concatenate(parts, axis=1).astype(f)


def kernel(**inputs):
    import numpy as np
    import concourse.bacc as bacc
    from concourse.bass_utils import run_bass_kernel_spmd

    i = {k: np.asarray(v) for k, v in inputs.items()}
    arrays = {
        "x": i["x"][0], "ctx": i["ctx"][0],
        "vecs": np.concatenate([i[n].reshape(-1, P) for n in
                                ("ada_b", "norm_g", "final_g", "c", "c_ctx", "att_q_gain", "att_k_gain")]),
        "dec": np.concatenate([i["ret_decay_f"], i["ret_decay_b"]], axis=1),
        "consts": shape_constants(),
        "ada_w": i["ada_w"], "w1": i["ffn_w1"], "w2": i["ffn_w2"], "ret_in": i["ret_w_in"][0],
        "ret_out": i["ret_w_out"][0], "qkv": i["att_w_qkv"][0], "wo": i["att_w_o"][0],
    }
    arrays = {f"in_{k}": np.ascontiguousarray(v) for k, v in arrays.items()}
    nc = bacc.Bacc("TRN2", target_bir_lowering=False, num_devices=1)
    args = [nc.dram_tensor(k, a.shape, mybir.dt.from_np(a.dtype), kind="ExternalInput").ap() for k, a in arrays.items()]
    out = nc.dram_tensor("out", (LAT, D), F32, kind="ExternalOutput").ap()
    build(nc, *args, out)
    r = run_bass_kernel_spmd(nc, [arrays], core_ids=[0])
    return r.results[0]["out"].reshape(1, LAT, D)
```

```python
from contextlib import ExitStack

import concourse.bass as bass
from concourse import mybir

F32 = mybir.dt.float32
F32R = mybir.dt.float32r
ALU = mybir.AluOpType
ACT = mybir.ActivationFunctionType
AX_X = mybir.AxisListType.X

P = 128
D = 1024
KD = D // P
LAT = 256
CTX = 256
N = LAT + CTX
DEPTH = 2
NMOD = 9
FFN = 2816
EPS = 1e-6
RH, RDK, RDV = 4, 256, 512
AH, AKV, AHD = 8, 2, 128
UNIT = 2048
HALVES = (12, 10)
ADA = 256
ADA_L = NMOD * D // ADA
ADA_PRO = 8
BAND = 384

UNITS_FFN = sum(HALVES) + 2 * KD
UNITS_RET_HEAD = 8
U_FFN = {(0, 0): 0}
U_RET = UNITS_FFN
U_FFN[(0, 1)] = U_RET + RH * UNITS_RET_HEAD
U_FFN[(1, 0)] = U_FFN[(0, 1)] + UNITS_FFN
U_GQA = U_FFN[(1, 0)] + UNITS_FFN
U_FFN[(1, 1)] = U_GQA + 10
U_END = U_FFN[(1, 1)] + UNITS_FFN
G_FFN = {(0, 0): 0, (0, 1): 22, (1, 0): 44, (1, 1): 66}

ROW_NG, ROW_FG, ROW_C, ROW_CX, ROW_QG, ROW_KG, ROWS = 144, 192, 200, 208, 216, 217, 218
C_ID, C_ONE, C_D, C_RC, C_RS, C_AC, C_AS, C_END = 0, 128, 256, 640, 896, 1152, 1408, 1664

CH_Q, CH_K, CH_V, CH_S = 4, 6, 8, 12
CH_GV, CH_GQ, CH_GO, CH_GP = 2, 4, 8, 12
S_NORM = {(0, 0): 0, (0, 1): 1, (0, 2): 6, (1, 0): 7, (1, 1): 8, (1, 2): 15}
S_RET, S_GQA, S_FIN = 2, 9, 16


ADA_RUNS = [(0, 12), (20, 30), (32, 38), (U_FFN[(0, 1)], U_FFN[(0, 1)] + 12),
            (U_FFN[(0, 1)] + 20, U_FFN[(0, 1)] + 30), (U_FFN[(1, 0)], U_FFN[(1, 0)] + 12),
            (U_FFN[(1, 0)] + 20, U_FFN[(1, 0)] + 22)]


def unit_sizes():
    runs = []
    for key in sorted(U_FFN):
        u = U_FFN[key]
        for rows in HALVES:
            runs += [(u, rows, UNIT), (u + rows, KD, rows * P)]
            u += rows + KD
        if key == (0, 0):
            runs.append((U_RET, RH * UNITS_RET_HEAD, UNIT))
        if key == (1, 0):
            runs.append((U_GQA, 10, UNIT))
    return runs


def ada_slice(u):
    a = ADA_PRO
    for first, end in ADA_RUNS:
        if first <= u < end:
            return a + u - first
        a += end - first
    return None


assert sum(end - first for first, end in ADA_RUNS) + ADA_PRO == DEPTH * ADA_L


def bodies(u, count, lag=0):
    at = [ada_slice(u + 2 * b - lag) for b in range(count)]
    runs, lo = [], 0
    for b in range(1, count + 1):
        if b == count or (at[b] is None) != (at[lo] is None) or (at[lo] is not None and at[b] - at[lo] != 2 * (b - lo)):
            runs.append((lo, b, None if at[lo] is None else at[lo] - 2 * lo))
            lo = b
    return runs


class Steps:

    def __init__(self, sem):
        self.sem, self.base, self.it, self.per, self.local = sem, 0, 0, 0, 0

    def enter(self, it, per):
        self.base += self.local
        self.it, self.per, self.local = it, per, 0

    def leave(self, count):
        assert self.local == self.per, (self.local, self.per)
        self.base, self.it, self.per, self.local = self.base + self.per * count, 0, 0, 0

    def mark(self, ins):
        ins.then_inc(self.sem, 1)
        self.local += 1
        return self.it * self.per + (self.base + self.local)


def build(nc, x, ctx, vecs, dec, consts, ada_w, units, out):
    stack = ExitStack()
    with stack:
        def sb(name, shape, dt=F32):
            return stack.enter_context(nc.sbuf_tensor(name, shape, dt))

        def sem(name):
            return stack.enter_context(nc.semaphore(name))

        xT = sb("xT", [P, KD, N])
        h_hi = sb("h_hi", [P, KD, N], F32R)
        h_lo = sb("h_lo", [P, KD, N], F32R)
        a_hi = sb("a_hi", [P, 15, N], F32R)
        a_lo = sb("a_lo", [P, 15, N], F32R)
        raw = sb("raw", [P, 2, UNIT])
        w_hi = sb("w_hi", [P, 2, UNIT], F32R)
        w_lo = sb("w_lo", [P, 2, UNIT], F32R)
        ada = sb("ada", [P, UNIT])
        acc = sb("acc", [P, 2, ADA])
        park = sb("park", [P, 8, N])
        tmp = sb("tmp", [P, 2, N])
        full = sb("full", [P, 2, N])
        ssum = sb("ssum", [P, N])
        sq = sb("sq", [P, N])
        diag = sb("diag", [P, N])
        cst = sb("cst", [P, C_END])
        band = sb("band", [P, 2, BAND])
        vecT = sb("vecT", [P, ROWS])
        modT = sb("modT", [P, DEPTH * NMOD * KD, 2])
        sT = sb("sT", [P, KD, 2])
        aff = sb("aff", [P, KD, 2])
        gate = sb("gate", [P, KD, 2])
        sd = sb("sd", [P, 4])
        rs = sb("rs", [P, 4])
        lg = sb("lg", [P, 2 * RH])
        dec_row = sb("dec_row", [1, 2 * RH])
        smx, snb, sden, sinv = (band[:, 0, 2 * AH * i:2 * AH * (i + 1)] for i in range(4))
        mark = sb("mark", [P, 1])

        pair = stack.enter_context(nc.psum_tensor("pair", [P, 2, 2, N], F32))
        ps_s = stack.enter_context(nc.psum_tensor("ps_s", [P, N], F32))
        psx = stack.enter_context(nc.psum_tensor("psx", [P, 3, N], F32))

        ident = cst[:, C_ID:C_ID + P]
        ones = cst[:, C_ONE:C_ONE + P]
        diff = cst[:, C_D:C_D + BAND]
        rcos, rsin = cst[:, C_RC:C_RC + LAT], cst[:, C_RS:C_RS + LAT]
        acos, asin = cst[:, C_AC:C_AC + LAT], cst[:, C_AS:C_AS + LAT]
        vrows = tmp[:, 0, 0:2 * P]
        o_buf, sg_buf = park[:, 0:4, :], park[:, 4:8, :]

        names = """consts_in vecs_in dec_in x_in raw_landed0 raw_landed1 ada_landed0 ada_landed1 acc_half x_sq o_sum pro_landed0 pro_landed1 pro_landed2
            vec_tr vec_up mod_up x_tr x_up dec_mm dec_exp silu_c s_rdy pro_mm hi_ready lo_ready pe_unit pair_free acc_ready
            ada_mm mod_ready silu_ready u_ready u_hi xsq ss_ready st_sum st_sqrt st_diag st_bcast t_ready n_hi
            h_ready dve_step q_ctx_hi rot_ready q_lat_hi v_hi e_pre e_exp s_mm ms_ready ms_hi s_split o_mm
            o_copied o_sq sg_ready og_ready og_hi og_lo g_sq kn_ready kn_hi kn_lo sc_mm nb_ready p_exp p_ready
            pt_mm pt_hi pt_lo oT_mm oT_hi oT_lo fin_ready fin_tr fin_copied out_done gv_hi""".split()
        S = {n: sem(n) for n in names}
        raw_landed = [S["raw_landed0"], S["raw_landed1"]]
        ada_landed = [S["ada_landed0"], S["ada_landed1"]]
        pro_landed = [S["pro_landed0"], S["pro_landed1"], S["pro_landed2"]]

        def f32(ap):
            return ap.bitcast(F32)

        block = stack.enter_context(nc.Block())

        @block.sync
        def _(sp):
            def load_unit(u, j, size, wait):
                if wait:
                    sp.wait_ge(S["lo_ready"], u - 1)
                sp.dma_start(raw[:, j:j + 1, 0:size], units[bass.ds(u, 1), :, 0:size].rearrange("u p n -> p u n")
                             ).then_inc(raw_landed[j], 16)

            def load_ada(a):
                for half in range(2):
                    if isinstance(a, int) and a == ADA_PRO:
                        sp.wait_ge(S["pro_mm"], ADA_PRO - 2)
                    else:
                        sp.wait_ge((S["acc_half"], S["acc_ready"])[half], a - ADA_PRO)
                    cols = slice(half * UNIT // 2, (half + 1) * UNIT // 2)
                    sp.dma_start(ada[:, cols].unsqueeze(1), ada_w[bass.ds(a, 1), :, cols].rearrange("u p n -> p u n")
                                 ).then_inc(ada_landed[half], 16)

            sp.dma_start(cst[:, :], consts).then_inc(S["consts_in"], 16)
            sp.dma_start(vrows[:, 0:P], vecs[0:P, :]).then_inc(S["vecs_in"], 16)
            sp.dma_start(vrows[0:ROWS - P, P:2 * P], vecs[P:ROWS, :]).then_inc(S["vecs_in"], 16)
            sp.dma_start(dec_row[:, :], dec).then_inc(S["dec_in"], 16)
            slots3 = [raw[:, 0, :], raw[:, 1, :], ada[:, :]]
            for a in range(ADA_PRO):
                if a >= 3:
                    sp.wait_ge(S["pro_mm"], a - 2)
                sp.dma_start(slots3[a % 3], ada_w[a]).then_inc(pro_landed[a % 3], 16)
                if a == 2:
                    xin = park[:, :, :].rearrange("p (t a) n -> p t (a n)", t=4)
                    sp.dma_start(xin[:, 0:2], x.rearrange("(t p) d -> p t d", p=P)).then_inc(S["x_in"], 16)
                    sp.dma_start(xin[:, 2:4], ctx.rearrange("(t p) d -> p t d", p=P)).then_inc(S["x_in"], 16)

            def stream(u, count, size):
                for lo, hi, a0 in bodies(u, count // 2, lag=2):
                    if u + lo == 0:
                        for j in range(2):
                            sp.wait_ge(S["pro_mm"], ADA_PRO - 1 + j)
                            load_unit(j, j, size, False)
                        lo = 1
                    if hi > lo:
                        with sp.Fori(lo, hi) as it:
                            for j in range(2):
                                load_unit(u + 2 * it + j, j, size, True)
                                if a0 is not None:
                                    load_ada(a0 + 2 * it + j)

            for u0, count, size in unit_sizes():
                stream(u0, count, size)
            outv = out.rearrange("(t p) d -> p t d", p=P)
            for t in range(2):
                sp.wait_ge(S["fin_copied"], t + 1)
                sp.dma_start(outv[:, t], park[:, 2 * t:2 * t + 2, :].rearrange("p a n -> p (a n)")
                             ).then_inc(S["out_done"], 16)
            sp.wait_ge(S["out_done"], 32)

        @block.tensor
        def _(pe):
            mm = nc.tensor.matmul

            def mm3(dst, whi, wlo, xhi, xlo, start, stop):
                mm(dst, wlo, xhi, start=start, stop=False)
                mm(dst, whi, xlo, start=False, stop=False)
                return mm(dst, whi, xhi, start=False, stop=stop)

            def wait_unit(u):
                if not isinstance(u, int) or u > 0:
                    pe.wait_ge(S["pair_free"], u + 1)
                pe.wait_ge(S["lo_ready"], u + 1)

            def rows_sum(src, s, tiles, extra=None):
                for t in range(tiles):
                    last = mm(ps_s[:, 8 + t:9 + t], src[:, t * P:(t + 1) * P], ones[:, 0:1], start=True, stop=True)
                last.then_inc(S["st_sum"], 1)

            def rows_bcast(bank, s, width):
                pe.wait_ge(S["st_diag"], s + 1)
                mm(bank[:, 0:width], ones, diag[:, 0:width], start=True, stop=True).then_inc(S["st_bcast"], 1)

            def ada_mm(a):
                pe.wait_ge(S["acc_ready"], a - (ADA_PRO - 1))
                for c in range(2):
                    for cond in range(2):
                        last = mm(ps_s[:, 2 * c + cond:2 * c + cond + 1], acc[:, cond, c * P:(c + 1) * P],
                                  ones[:, 0:1], start=True, stop=True)
                last.then_inc(S["ada_mm"], 1)

            def unit_cols(u, j, width, h0, banks=None):
                wait_unit(u)
                whi = w_hi[:, j, :].rearrange("p (k c n) -> p k c n", k=KD, c=2)
                wlo = w_lo[:, j, :].rearrange("p (k c n) -> p k c n", k=KD, c=2)
                dst = banks or [pair[:, j, 0, 0:width], pair[:, j, 1, 0:width]]
                for k in range(KD):
                    pe.wait_ge(S["h_ready"], h0 + k + 1)
                    for c in range(2):
                        last = mm3(dst[c], whi[:, k, c], wlo[:, k, c], h_hi[:, k, 0:width], h_lo[:, k, 0:width],
                                   k == 0, k == KD - 1)
                last.then_inc(S["pe_unit"], 1)

            def unit_gu(u, j, width, h0):
                wait_unit(u)
                whi = w_hi[:, j, :].rearrange("p (c k n) -> p c k n", c=2, k=KD)
                wlo = w_lo[:, j, :].rearrange("p (c k n) -> p c k n", c=2, k=KD)
                for k in range(KD):
                    pe.wait_ge(S["h_ready"], h0 + k + 1)
                    for c in range(2):
                        last = mm3(pair[:, j, c, 0:width], whi[:, c, k], wlo[:, c, k], h_hi[:, k, 0:width],
                                   h_lo[:, k, 0:width], k == 0, k == KD - 1)
                last.then_inc(S["pe_unit"], 1)

            def unit_down(u, j, rows, width, u_gu):
                wait_unit(u)
                for r in range(rows):
                    pe.wait_ge(S["pair_free"], u_gu + r + 3)
                    last = mm3(pair[:, j, 0, 0:width], w_hi[:, j, r * P:(r + 1) * P], w_lo[:, j, r * P:(r + 1) * P],
                               a_hi[:, r, 0:width], a_lo[:, r, 0:width], r == 0, r == rows - 1)
                last.then_inc(S["pe_unit"], 1)

            def norm(n, u_prev, tiles, bank=1):
                pe.wait_ge(S["ss_ready"], NSS[n])
                rows_sum(ssum, n, tiles)
                rows_bcast(psx[:, bank], n, tiles * P)

            def ffn(l, f, width):
                u = U_FFN[(l, f)]
                h0 = H0[(l, 2 * f)]
                for half, rows in enumerate(HALVES):
                    for lo, hi, a0 in bodies(u, rows // 2):
                        with pe.Fori(lo, hi) as it:
                            for j in range(2):
                                unit_gu(u + 2 * it + j, j, width, h0)
                                if a0 is not None:
                                    ada_mm(a0 + 2 * it + j)
                    u_gu, u = u, u + rows
                    for lo, hi, a0 in bodies(u, KD // 2):
                        with pe.Fori(lo, hi) as it:
                            for j in range(2):
                                unit_down(u + 2 * it + j, j, rows, width, u_gu)
                                if a0 is not None:
                                    ada_mm(a0 + 2 * it + j)
                    u += KD

            pe.wait_ge(S["consts_in"], 16)
            pe.wait_ge(S["vecs_in"], 32)
            nc.tensor.transpose(psx[:, 0, 0:P], vrows[:, 0:P], ident).then_inc(S["pe_unit"], 1)
            nc.tensor.transpose(psx[:, 0, P:ROWS], vrows[0:ROWS - P, P:2 * P], ident[0:ROWS - P, 0:ROWS - P]
                                ).then_inc(S["vec_tr"], 1)
            pe.wait_ge(S["dec_in"], 16)
            mm(psx[:, 1, 0:2 * RH], ones[0:1, :], dec_row[:, :], start=True, stop=True).then_inc(S["dec_mm"], 1)

            def x_transposes(d):
                xin = park[:, :, :].rearrange("p (t a) n -> p t (a n)", t=4)
                if d >= 4:
                    pe.wait_ge(S["x_up"], d - 3)
                for t in range(4):
                    last = nc.tensor.transpose(pair[:, (d % 4) // 2, d % 2, t * P:(t + 1) * P],
                                               xin[:, t, d * P:(d + 1) * P], ident)
                last.then_inc(S["x_tr"], 1)

            slots3 = [raw[:, 0, :], raw[:, 1, :], ada[:, :]]
            for a in range(ADA_PRO):
                if a == 0:
                    pe.wait_ge(S["s_rdy"], 1)
                if a == 3:
                    pe.wait_ge(S["x_in"], 32)
                    for d in range(KD):
                        x_transposes(d)
                pe.wait_ge(pro_landed[a % 3], 16 * (a // 3 + 1))
                w = slots3[a % 3].rearrange("p (k c n) -> p k c n", k=KD, c=2)
                for c in range(2):
                    for k in range(KD):
                        last = mm(ps_s[:, 16 + 4 * a + 2 * c:18 + 4 * a + 2 * c], w[:, k, c], sT[:, k, :],
                                  start=k == 0, stop=k == KD - 1)
                last.then_inc(S["pro_mm"], 1)

            pe.wait_ge(S["mod_up"], 1)
            norm(0, 0, 4)
            ffn(0, 0, N)
            pe.wait_ge(S["mod_ready"], MODS_NORM[(0, 1)])
            norm(1, 0, 4)

            def retention(hd):
                U = U_RET + 8 * hd
                h0 = H0[(0, 1)]
                for j in (0, 1):
                    unit_cols(U + j, j, N, h0)
                for j in (2, 3):
                    wait_unit(U + j)
                    whi = w_hi[:, j % 2, :].rearrange("p (k n) -> p k n", k=KD)
                    wlo = w_lo[:, j % 2, :].rearrange("p (k n) -> p k n", k=KD)
                    for t in range(4):
                        dst = pair[:, j % 2, t // 2, (t % 2) * 256:(t % 2 + 1) * 256]
                        for k in range(KD):
                            last = mm3(dst, h_hi[:, k, t * P:(t + 1) * P], h_lo[:, k, t * P:(t + 1) * P],
                                       whi[:, k], wlo[:, k], k == 0, k == KD - 1)
                    last.then_inc(S["pe_unit"], 1)
                pe.wait_ge(S["pair_free"], U + 3 + 1)
                for g in range(3):
                    for kt, q0, qn in ([(2 + g, 0, N)] if g < 2 else [(0, 0, LAT), (1, LAT, LAT)]):
                        for c in range(2):
                            last = mm3(psx[:, g, q0:q0 + qn], a_hi[:, CH_K + c, kt * P:(kt + 1) * P],
                                       a_lo[:, CH_K + c, kt * P:(kt + 1) * P], a_hi[:, CH_Q + c, 0:qn],
                                       a_lo[:, CH_Q + c, 0:qn], c == 0, c == 1)
                    last.then_inc(S["s_mm"], 1)
                unit_cols(U + 4, 0, N, h0)
                pe.wait_ge(S["s_split"], 3 * hd + 3)
                pe.wait_ge(S["pair_free"], U + 5 + 1)
                for e in range(4):
                    bank = psx[:, e % 3]
                    if e == 3:
                        pe.wait_ge(S["o_copied"], 4 * hd + 1)
                    for n, (kt, ch, c0, qn) in enumerate(((2, 0, 0, N), (3, 1, 0, N), (0, 2, 0, LAT), (1, 2, LAT, LAT))):
                        last = mm3(bank[:, 0:qn], a_hi[:, CH_V + kt, e * P:(e + 1) * P],
                                   a_lo[:, CH_V + kt, e * P:(e + 1) * P], a_hi[:, CH_S + ch, c0:c0 + qn],
                                   a_lo[:, CH_S + ch, c0:c0 + qn], n == 0, n == 3)
                    last.then_inc(S["o_mm"], 1)
                wait_unit(U + 5)
                whi = w_hi[:, 1, :].rearrange("p (k c n) -> p k c n", k=KD, c=2)
                wlo = w_lo[:, 1, :].rearrange("p (k c n) -> p k c n", k=KD, c=2)
                for c in range(2):
                    for k in range(KD):
                        last = mm3(pair[:, 1, c], whi[:, k, c], wlo[:, k, c], h_hi[:, k], h_lo[:, k],
                                   k == 0, k == KD - 1)
                        if c == 1 and k == 3:
                            pe.wait_ge(S["o_copied"], 4 * hd + 4)
                            rows_bcast(psx[:, 1], S_RET + hd, N)
                    if c == 0:
                        pe.wait_ge(S["o_sum"], 3 * hd + 3)
                        rows_sum(ssum, S_RET + hd, 4)
                last.then_inc(S["pe_unit"], 1)
                for j in (6, 7):
                    wait_unit(U + j)
                    whi = w_hi[:, j % 2, :].rearrange("p (k n) -> p k n", k=4)
                    wlo = w_lo[:, j % 2, :].rearrange("p (k n) -> p k n", k=4)
                    for i in range(4):
                        dst = (pair[:, j % 2, 0], pair[:, j % 2, 1], psx[:, 0], psx[:, 2])[i]
                        if i == 2:
                            pe.wait_ge(S["o_copied"], 4 * hd + 4)
                            pe.wait_ge(S["pair_free"], U + (j + 1) + 1)
                        for k in range(4):
                            pe.wait_ge(S["og_lo"], 4 * hd + (k + 1))
                            last = mm3(dst, whi[:, k, i * P:(i + 1) * P], wlo[:, k, i * P:(i + 1) * P],
                                       a_hi[:, k], a_lo[:, k], k == 0, k == 3)
                    last.then_inc(S["pe_unit"], 1)

            with pe.Fori(0, RH) as hd:
                retention(hd)
            norm(S_NORM[(0, 2)], 0, 4)
            ffn(0, 1, N)
            pe.wait_ge(S["mod_ready"], MODS_NORM[(1, 0)])
            norm(S_NORM[(1, 0)], 0, 4)
            ffn(1, 0, N)
            pe.wait_ge(S["mod_ready"], MODS_NORM[(1, 1)])
            norm(S_NORM[(1, 1)], 0, 4)

            h0 = H0[(1, 1)]
            U = U_GQA

            def job_stats(job, bank):
                pe.wait_ge(S["g_sq"], job + 1)
                rows_sum(sq if job % 2 else ssum, S_GQA + job, 4)
                rows_bcast(psx[:, bank], S_GQA + job, N)
            unit_cols(U, 0, N, h0)
            wait_unit(U + 1)
            whi = w_hi[:, 1, :].rearrange("p (k n) -> p k n", k=KD)
            wlo = w_lo[:, 1, :].rearrange("p (k n) -> p k n", k=KD)
            for t in range(4):
                for k in range(KD):
                    last = mm3(pair[:, 1, t // 2, (t % 2) * 256:(t % 2 + 1) * 256], h_hi[:, k, t * P:(t + 1) * P],
                               h_lo[:, k, t * P:(t + 1) * P], whi[:, k], wlo[:, k], k == 0, k == KD - 1)
                if t == 0:
                    job_stats(0, 0)
                if t == 2:
                    job_stats(1, 1)
            last.then_inc(S["pe_unit"], 1)
            for i in range(4):
                j = i % 2
                unit_cols(U + 2 + i, j, LAT, h0, [pair[:, j, 0, 0:LAT], pair[:, j, 1, 0:LAT]])
                if i > 0:
                    pe.wait_ge(S["kn_lo"], 2 + i - 1)
                    job_stats(2 + i - 1, (i - 1) % 2)
            pe.wait_ge(S["kn_lo"], 4)
            job_stats(5, 1)

            def scores(hh):
                g = hh // (AH // AKV)
                pe.wait_ge(S["kn_lo"], 3 + hh // 2)
                if hh >= 2:
                    pe.wait_ge(S["p_exp"], 2 * (hh - 2) + 2)
                else:
                    pe.wait_ge(S["pair_free"], U + 7 + 1)
                for qb in range(2):
                    c0 = (hh % 2) * LAT + qb * P
                    last = mm3(pair[:, hh % 2, qb], a_hi[:, CH_GQ + hh // 2, c0:c0 + P],
                               a_lo[:, CH_GQ + hh // 2, c0:c0 + P], a_hi[:, g], a_lo[:, g], True, True)
                    last.then_inc(S["sc_mm"], 1)

            scores(0)
            for hh in range(AH):
                g = hh // (AH // AKV)
                if hh + 1 < AH:
                    scores(hh + 1)
                for qb in range(2):
                    pe.wait_ge(S["p_ready"], 2 * hh + qb + 1)
                    if hh and qb == 0:
                        pe.wait_ge(S["pt_lo"], 2 * hh)
                    for kt in range(4):
                        last = nc.tensor.transpose(psx[:, kt // 2, (kt % 2) * LAT + qb * P:(kt % 2) * LAT + (qb + 1) * P],
                                                   park[:, 2 * (hh % 2) + qb, kt * P:(kt + 1) * P], ident)
                last.then_inc(S["pt_mm"], 1)
                if hh:
                    pe.wait_ge(S["oT_lo"], hh)
                for kt in range(4):
                    pe.wait_ge(S["pt_lo"], 2 * hh + kt // 2 + 1)
                    vt = (kt % 2) * 256 + g * P
                    last = mm3(psx[:, 2, 0:LAT], a_hi[:, CH_GV + kt // 2, vt:vt + P], a_lo[:, CH_GV + kt // 2, vt:vt + P],
                               a_hi[:, CH_GP + kt // 2, (kt % 2) * LAT:(kt % 2 + 1) * LAT],
                               a_lo[:, CH_GP + kt // 2, (kt % 2) * LAT:(kt % 2 + 1) * LAT], kt == 0, kt == 3)
                last.then_inc(S["oT_mm"], 1)
            for i in range(4):
                j = i % 2
                wait_unit(U + 6 + i)
                whi = w_hi[:, j, :].rearrange("p (k c n) -> p k c n", k=KD, c=2)
                wlo = w_lo[:, j, :].rearrange("p (k c n) -> p k c n", k=KD, c=2)
                for k in range(KD):
                    pe.wait_ge(S["oT_lo"], k + 1)
                    src = (CH_GO + k // 2, (k % 2) * LAT)
                    for c in range(2):
                        last = mm3(pair[:, j, c, 0:LAT], whi[:, k, c], wlo[:, k, c],
                                   a_hi[:, src[0], src[1]:src[1] + LAT], a_lo[:, src[0], src[1]:src[1] + LAT],
                                   k == 0, k == KD - 1)
                last.then_inc(S["pe_unit"], 1)
            norm(S_NORM[(1, 2)], 0, 2)
            ffn(1, 1, LAT)
            norm(S_FIN, 0, 2)
            for d in range(KD):
                pe.wait_ge(S["fin_ready"], d + 1)
                for t in range(2):
                    last = nc.tensor.transpose(pair[:, t, d // 4, (d % 4) * P:(d % 4 + 1) * P],
                                               tmp[:, d % 2, t * P:(t + 1) * P], ident)
                last.then_inc(S["fin_tr"], 1)

        @block.scalar
        def _(act):
            fn = nc.scalar.activation

            def split_hi(base, it, off, mul=2):
                slot = off % 2
                act.wait_ge(raw_landed[slot], it * (8 * mul) + 16 * ((base + off) // 2 + 1))
                v = it * mul + (base + off)
                if not isinstance(v, int) or v >= 2:
                    act.wait_ge(S["pe_unit"], v)
                fn(w_hi[:, slot, :], raw[:, slot, :], ACT.Copy).then_inc(S["hi_ready"], 1)

            def square_x(d, slot, ss, width, wait):
                if wait is not None:
                    act.wait_ge(S["pair_free"], wait)
                if ss or d >= 2:
                    act.wait_ge(S["ss_ready"], d + (ss - 1))
                fn(full[:, slot:slot + 1, 0:width], xT[:, bass.ds(d, 1), 0:width], ACT.Square).then_inc(S["x_sq"], 1)

            def norm(n, l, third, width):
                nc.scalar.preload_act_table(ACT.Sqrt)
                act.wait_ge(S["st_sum"], n + 1)
                fn(sd[:, 0:width // P], ps_s[:, 8:8 + width // P], ACT.Sqrt, scale=1.0 / D, bias=EPS
                   ).then_inc(S["st_sqrt"], 1)
                if l is None:
                    return
                h0 = H0[(l, third)]
                for d in range(KD):
                    act.wait_ge(S["t_ready"], h0 + d + 1)
                    for cond in range(width // 256):
                        q = (l * NMOD + 3 * third) * KD + d
                        last = fn(h_hi[:, d, cond * 256:(cond + 1) * 256], tmp[:, d % 2, cond * 256:(cond + 1) * 256],
                                  ACT.Identity, scale=aff[:, d, cond:cond + 1], bias=modT[:, q, cond:cond + 1])
                    last.then_inc(S["n_hi"], 1)

            def ffn(l, f, width):
                u = U_FFN[(l, f)]
                g = G_FFN[(l, f)]
                nc.scalar.preload_act_table(ACT.Silu)
                for half, rows in enumerate(HALVES):
                    with act.Fori(0, rows // 2) as it:
                        for j in range(2):
                            uu = u + 2 * it + j
                            gg = g + 2 * it + j
                            split_hi(u, it, j + 1)
                            act.wait_ge(S["pe_unit"], uu + 2)
                            fn(tmp[:, j, 0:width], pair[:, j, 0, 0:width], ACT.Silu).then_inc(S["silu_ready"], 1)
                            act.wait_ge(S["u_ready"], gg + 1)
                            fn(a_hi[:, bass.ds(2 * it + j, 1), 0:width], full[:, j:j + 1, 0:width], ACT.Copy
                               ).then_inc(S["u_hi"], 1)
                    u += rows
                    g += rows
                    last = (l, f, half) == (1, 1, 1)

                    def dbody(it, last_body):
                        for j in range(2):
                            if not (last_body and j == 1):
                                split_hi(u, it, j + 1)
                            if half and not (isinstance(it, int) and 2 * it + j == 0):
                                square_x(2 * it + (j - 1), (j + 1) % 2, SS0[(l, f)], width, u + 2 * it + (j + 2))
                    dbody(0, False)
                    with act.Fori(1, KD // 2 - last) as it:
                        dbody(it, False)
                    if last:
                        dbody(KD // 2 - 1, True)
                    if half:
                        square_x(KD - 1, 1, SS0[(l, f)], width, u + KD + 2)
                    u += KD

            act.wait_ge(S["vec_up"], 1)
            for cond, row in enumerate((ROW_C, ROW_CX)):
                last = fn(sT[:, :, cond], vecT[:, row:row + KD], ACT.Silu)
            last.then_inc(S["s_rdy"], 1)
            act.wait_ge(S["dec_mm"], 1)
            fn(lg[:, :], psx[:, 1, 0:2 * RH], ACT.Exp).then_inc(S["dec_exp"], 1)
            split_hi(0, 0, 0)
            for d in range(KD):
                act.wait_ge(S["x_up"], d + 1)
                square_x(d, d % 2, 0, N, None)
            norm(0, 0, 0, N)
            ffn(0, 0, N)
            norm(1, 0, 1, N)

            def retention(hd):
                U = U_RET + 8 * hd
                for j in range(8):
                    split_hi(U_RET, hd, j + 1, 8)
                    if j < 2:
                        ch, sc = (CH_Q, 1.0) if j == 0 else (CH_K, RDK ** -0.5)
                        act.wait_ge(S["pe_unit"], U + (j + 1) + 1)
                        fn(a_hi[:, ch:ch + 2, LAT:N], pair[:, j % 2, :, LAT:N], ACT.Copy, scale=sc
                           ).then_inc(S["q_ctx_hi"], 1)
                        act.wait_ge(S["rot_ready"], 2 * hd + (j + 1))
                        fn(a_hi[:, ch:ch + 2, 0:LAT], full[:, j, :].rearrange("p (c n) -> p c n", c=2), ACT.Copy, scale=sc
                           ).then_inc(S["q_lat_hi"], 1)
                    elif j < 4:
                        if j == 2:
                            act.wait_ge(S["e_pre"], 4 * hd + 4)
                            fn(o_buf[:, :, 0:BAND], o_buf[:, :, 0:BAND], ACT.Exp).then_inc(S["e_exp"], 1)
                        act.wait_ge(S["pe_unit"], U + (j + 1) + 1)
                        fn(a_hi[:, CH_V:CH_V + 4, (j - 2) * 256:(j - 1) * 256],
                           pair[:, j % 2, :, :].rearrange("p b (t n) -> p (b t) n", t=2), ACT.Copy
                           ).then_inc(S["v_hi"], 1)
                        if j == 3:
                            for g in range(3):
                                act.wait_ge(S["ms_ready"], 3 * hd + (g + 1))
                                fn(a_hi[:, CH_S + g, :], tmp[:, g % 2, :], ACT.Copy).then_inc(S["ms_hi"], 1)
                    elif j < 6:
                        if j == 5:
                            for e in range(4):
                                act.wait_ge(S["o_copied"], 4 * hd + (e + 1))
                                if e == 0:
                                    fn(ssum[:, :], o_buf[:, 0, :], ACT.Square).then_inc(S["o_sq"], 1)
                                    continue
                                if e == 3:
                                    act.wait_ge(S["o_sum"], 3 * hd + 1)
                                fn(full[:, e % 2, :], o_buf[:, e, :], ACT.Square).then_inc(S["o_sq"], 1)
                            act.wait_ge(S["st_sum"], S_RET + 1 + hd)
                            fn(sd[:, :], ps_s[:, 8:12], ACT.Sqrt, scale=1.0 / RDV, bias=EPS
                               ).then_inc(S["st_sqrt"], 1)
                        act.wait_ge(S["pe_unit"], U + (j + 1) + 1)
                        fn(sg_buf[:, 2 * (j - 4):2 * (j - 3), :], pair[:, j % 2, :, :], ACT.Silu
                           ).then_inc(S["sg_ready"], 1)
                        if j == 5:
                            for e in range(4):
                                act.wait_ge(S["og_ready"], 4 * hd + (e + 1))
                                fn(a_hi[:, e, :], tmp[:, e % 2, :], ACT.Copy).then_inc(S["og_hi"], 1)

            with act.Fori(0, RH) as hd:
                retention(hd)
            for d in range(KD):
                square_x(d, d % 2, SS_RET, N, U_RET + 8 * RH + 1 + d // 4)
            norm(S_NORM[(0, 2)], 0, 2, N)
            ffn(0, 1, N)
            norm(S_NORM[(1, 0)], 1, 0, N)
            ffn(1, 0, N)
            norm(S_NORM[(1, 1)], 1, 1, N)

            U = U_GQA

            def job_square(job, src):
                if job >= 2:
                    act.wait_ge(S["st_sum"], S_GQA + job - 1)
                fn((sq if job % 2 else ssum)[:, :], src, ACT.Square).then_inc(S["g_sq"], 1)

            def root(job):
                act.wait_ge(S["st_sum"], S_GQA + job + 1)
                fn(sd[:, :], ps_s[:, 8:12], ACT.Sqrt, scale=1.0 / AHD, bias=EPS).then_inc(S["st_sqrt"], 1)

            def job_hi(job):
                act.wait_ge(S["kn_ready"], job + 1)
                fn(a_hi[:, job if job < 2 else CH_GQ + job - 2, :], full[:, 0, :], ACT.Copy).then_inc(S["kn_hi"], 1)
            split_hi(U, 0, 1)
            act.wait_ge(S["pe_unit"], U + 2)
            job_square(0, pair[:, 0, 0])
            job_square(1, pair[:, 0, 1])
            root(0)
            root(1)
            split_hi(U, 0, 2)
            job_hi(0)
            job_hi(1)
            act.wait_ge(S["pe_unit"], U + 3)
            fn(a_hi[:, CH_GV:CH_GV + 2, :], pair[:, 1, :, :], ACT.Copy).then_inc(S["gv_hi"], 1)
            for i in range(4):
                split_hi(U, 0, 3 + i)
                act.wait_ge(S["pe_unit"], U + 3 + i + 1)
                job_square(2 + i, pair[:, i % 2, :, 0:LAT])
                root(2 + i)
                job_hi(2 + i)
            split_hi(U, 0, 7)

            def probs(hh, qb):
                act.wait_ge(S["nb_ready"], 2 * hh + qb + 1)
                n = 2 * hh + qb
                fn(park[:, 2 * (hh % 2) + qb, :], pair[:, hh % 2, qb], ACT.Exp, bias=snb[:, n:n + 1],
                   scale=AHD ** -0.5, accum_out=sden[:, n:n + 1]).then_inc(S["p_exp"], 1)
            probs(0, 0)
            probs(0, 1)
            for hh in range(AH):
                if hh + 1 < AH:
                    if hh >= 1:
                        act.wait_ge(S["pt_mm"], hh)
                    probs(hh + 1, 0)
                    probs(hh + 1, 1)
                act.wait_ge(S["pt_mm"], hh + 1)
                if hh:
                    act.wait_ge(S["oT_mm"], hh)
                for b in range(2):
                    fn(a_hi[:, CH_GP + b, :], psx[:, b], ACT.Copy).then_inc(S["pt_hi"], 1)
                act.wait_ge(S["oT_mm"], hh + 1)
                fn(a_hi[:, CH_GO + hh // 2, (hh % 2) * LAT:(hh % 2 + 1) * LAT], psx[:, 2, 0:LAT], ACT.Copy
                   ).then_inc(S["oT_hi"], 1)
            for i in range(4):
                if i < 3:
                    split_hi(U, 0, 8 + i)
                for d in (2 * i, 2 * i + 1):
                    square_x(d, d % 2, SS_GQA, LAT, U + 9 + i)
            norm(S_NORM[(1, 2)], 1, 2, LAT)
            ffn(1, 1, LAT)
            norm(S_FIN, None, 0, LAT)

        @block.vector
        def _(dve):
            V = nc.vector
            step = Steps(S["dve_step"])

            def after(value):
                dve.wait_ge(S["dve_step"], value)

            def split_lo(v, slot):
                dve.wait_ge(S["hi_ready"], v + 1)
                V.tensor_tensor(w_lo[:, slot, :], raw[:, slot, :], f32(w_hi[:, slot, :]), ALU.subtract
                                ).then_inc(S["lo_ready"], 1)

            def ada_sum(a):
                w = ada[:, :].rearrange("p (k n) -> p k n", k=KD)
                ready = {}
                for k in range(KD):
                    if k % (KD // 2) == 0:
                        dve.wait_ge(ada_landed[2 * k // KD], (a - (ADA_PRO - 1)) * 16)
                    for cond in range(2):
                        s = sT[:, k, cond:cond + 1]
                        if k == 0:
                            ins = V.tensor_scalar(acc[:, cond, :], w[:, k], s, None, ALU.mult)
                        else:
                            if k == KD // 2 and cond == 1:
                                dve.wait_ge(S["acc_half"], a - (ADA_PRO - 1))
                            else:
                                after(ready[cond])
                            ins = V.scalar_tensor_tensor(out=acc[:, cond, :], in0=w[:, k], scalar=s,
                                                         in1=acc[:, cond, :], op0=ALU.mult, op1=ALU.add)
                        if k == KD - 1 and cond == 1:
                            ins.then_inc(S["acc_ready"], 1)
                        elif k == KD // 2 - 1 and cond == 1:
                            ins.then_inc(S["acc_half"], 1)
                        else:
                            ready[cond] = step.mark(ins)

            def ada_out(a):
                dve.wait_ge(S["ada_mm"], a - (ADA_PRO - 1))
                V.tensor_tensor(modT[:, bass.ds(2 * a, 2), :], ps_s[:, 0:4].rearrange("p (c o) -> p c o", o=2),
                                vecT[:, bass.ds(2 * a, 2)].unsqueeze(2).to_broadcast([P, 2, 2]), ALU.add
                                ).then_inc(S["mod_ready"], 1)
            ADA_STEPS = 2 * KD - 2

            def zero_sums():
                after(step.mark(V.memset(ssum[:, :], 0.0)))

            def add_square(d, slot, ss, width):
                dve.wait_ge(S["x_sq"], d + (ss + 1))
                if ss or d:
                    dve.wait_ge(S["ss_ready"], d + ss)
                V.tensor_tensor(ssum[:, 0:width], ssum[:, 0:width], full[:, slot, 0:width], ALU.add
                                ).then_inc(S["ss_ready"], 1)

            def norm_rstd(n, count, width):
                tiles = width // P
                dve.wait_ge(S["st_sqrt"], n + 1)
                r = step.mark(V.reciprocal(rs[:, 0:tiles], sd[:, 0:tiles]))
                after(r)
                for t in range(tiles):
                    last = V.tensor_scalar(diag[:, t * P:(t + 1) * P], ident, rs[:, t:t + 1], None, ALU.mult)
                last.then_inc(S["st_diag"], 1)

            def norm(n, l, third, width):
                g0 = ROW_NG + (3 * l + third) * KD
                q0 = (l * NMOD + 3 * third) * KD
                if MODS_NORM[(l, third)]:
                    dve.wait_ge(S["mod_ready"], MODS_NORM[(l, third)])
                V.scalar_tensor_tensor(out=aff[:, :, :], in0=modT[:, q0 + KD:q0 + 2 * KD, :], scalar=1.0,
                                       in1=vecT[:, g0:g0 + KD].unsqueeze(2).to_broadcast([P, KD, 2]),
                                       op0=ALU.add, op1=ALU.mult)
                norm_rstd(n, 1, width)
                dve.wait_ge(S["st_bcast"], n + 1)
                h0 = H0[(l, third)]

                def t(d):
                    V.tensor_tensor(tmp[:, d % 2, 0:width], xT[:, d, 0:width], psx[:, 1, 0:width], ALU.mult
                                    ).then_inc(S["t_ready"], 1)
                t(0)
                for d in range(KD):
                    if d + 1 < KD:
                        t(d + 1)
                    dve.wait_ge(S["t_ready"], h0 + d + 1)
                    if d >= 2:
                        dve.wait_ge(S["h_ready"], h0 + d - 1)
                    for cond in range(width // 256):
                        v = step.mark(V.tensor_scalar(
                            full[:, d % 2, cond * 256:(cond + 1) * 256], tmp[:, d % 2, cond * 256:(cond + 1) * 256],
                            aff[:, d, cond:cond + 1], modT[:, q0 + d, cond:cond + 1], ALU.mult, ALU.add))
                    dve.wait_ge(S["n_hi"], h0 + d + 1)
                    after(v)
                    V.tensor_tensor(h_lo[:, d, 0:width], full[:, d % 2, 0:width], f32(h_hi[:, d, 0:width]), ALU.subtract
                                    ).then_inc(S["h_ready"], 1)
                dve.wait_ge(S["h_ready"], h0 + KD)

            def gates(l, m, factor):
                q = (l * NMOD + m) * KD
                after(step.mark(V.tensor_scalar(gate[:, :, :], modT[:, q:q + KD, :], factor, None, ALU.mult)))

            def add_x(d, src, width, done):
                dd = bass.ds(d, 1)
                for cond in range(width // 256):
                    cols = slice(cond * 256, (cond + 1) * 256)
                    ins = V.scalar_tensor_tensor(out=xT[:, dd, cols], in0=src[:, cols].unsqueeze(1),
                                                 scalar=gate[:, dd, cond], in1=xT[:, dd, cols],
                                                 op0=ALU.mult, op1=ALU.add)
                if done:
                    ins.then_inc(S["pair_free"], 1)

            def ffn(l, f, width):
                u = U_FFN[(l, f)]
                g = G_FFN[(l, f)]
                for half, rows in enumerate(HALVES):
                    def body(it, a0):
                        for j in range(2):
                            uu = u + 2 * it + j
                            gg = g + 2 * it + j
                            split_lo(uu + 1, (j + 1) % 2)
                            if a0 is not None:
                                ada_sum(2 * it + (a0 + j))
                            dve.wait_ge(S["silu_ready"], gg + 1)
                            V.tensor_tensor(full[:, j, 0:width], tmp[:, j, 0:width], pair[:, j, 1, 0:width], ALU.mult
                                            ).then_inc(S["u_ready"], 1)
                            dve.wait_ge(S["u_hi"], gg + 1)
                            dve.wait_ge(S["u_ready"], gg + 1)
                            cc = bass.ds(2 * it + j, 1)
                            V.tensor_tensor(a_lo[:, cc, 0:width], full[:, j:j + 1, 0:width],
                                            f32(a_hi[:, cc, 0:width]), ALU.subtract).then_inc(S["pair_free"], 1)
                            if a0 is not None:
                                ada_out(2 * it + (a0 + j))
                    for lo, hi, a0 in bodies(u, rows // 2):
                        with dve.Fori(lo, hi) as it:
                            step.enter(it - lo if lo else it, 0 if a0 is None else 2 * ADA_STEPS)
                            body(it, a0)
                        step.leave(hi - lo)
                    u += rows
                    g += rows
                    if half == 0:
                        dve.wait_ge(S["mod_ready"], MODS_AT[(l, f)])
                        gates(l, 6 * f + 2, 0.5)
                    else:
                        zero_sums()

                    def dbody(it, a0, last_body=False):
                        for j in range(2):
                            uu = u + 2 * it + j
                            if not (last_body and j == 1):
                                split_lo(uu + 1, (j + 1) % 2)
                            if a0 is not None:
                                ada_sum(2 * it + (a0 + j))
                            if half and not (isinstance(it, int) and 2 * it + j == 0):
                                add_square(2 * it + (j - 1), (j + 1) % 2, SS0[(l, f)], width)
                            dve.wait_ge(S["pe_unit"], uu + 2)
                            add_x(2 * it + j, pair[:, j, 0], width, True)
                            if a0 is not None:
                                ada_out(2 * it + (a0 + j))
                    last = (l, f, half) == (1, 1, 1)
                    for lo, hi, a0 in bodies(u, KD // 2 - last):
                        if lo == 0:
                            dbody(0, a0)
                            lo = 1
                        if hi > lo:
                            with dve.Fori(lo, hi) as it:
                                step.enter(it - lo, 0 if a0 is None else 2 * ADA_STEPS)
                                dbody(it, a0)
                            step.leave(hi - lo)
                    if last:
                        dbody(KD // 2 - 1, None, True)
                    if half:
                        add_square(KD - 1, 1, SS0[(l, f)], width)
                    u += KD

            dve.wait_ge(S["vec_tr"], 1)
            V.tensor_copy(vecT[:, :], psx[:, 0, 0:ROWS]).then_inc(S["vec_up"], 1)
            for d in range(KD):
                dve.wait_ge(S["x_tr"], d + 1)
                V.tensor_copy(xT[:, d, :], pair[:, (d % 4) // 2, d % 2]).then_inc(S["x_up"], 1)
            zero_sums()
            for d in range(KD):
                add_square(d, d % 2, 0, N)
            dve.wait_ge(S["dec_exp"], 1)
            V.tensor_scalar(lg[:, :], lg[:, :], -1.0, None, ALU.mult).then_inc(S["pair_free"], 2)
            dve.wait_ge(S["pro_mm"], ADA_PRO)
            dve.wait_ge(S["vec_up"], 1)
            V.tensor_tensor(modT[:, 0:2 * ADA_PRO, :], ps_s[:, 16:16 + 4 * ADA_PRO].rearrange("p (q o) -> p q o", o=2),
                            vecT[:, 0:2 * ADA_PRO].unsqueeze(2).to_broadcast([P, 2 * ADA_PRO, 2]), ALU.add
                            ).then_inc(S["mod_up"], 1)
            dve.wait_ge(S["mod_up"], 1)
            split_lo(0, 0)
            norm(0, 0, 0, N)
            ffn(0, 0, N)
            norm(1, 0, 1, N)

            gates(0, 5, 1.0)

            def add_o_square(hd, e):
                dve.wait_ge(S["o_sq"], 4 * hd + (e + 1))
                if e > 1:
                    dve.wait_ge(S["o_sum"], 3 * hd + (e - 1))
                V.tensor_tensor(ssum[:, :], ssum[:, :], full[:, e % 2, :], ALU.add).then_inc(S["o_sum"], 1)

            def retention(hd):
                U = U_RET + 8 * hd
                for j in range(8):
                    split_lo(U + (j + 1), (j + 1) % 2)
                    p = j % 2
                    if j < 2:
                        ch, sc = (CH_Q, 1.0) if j == 0 else (CH_K, RDK ** -0.5)
                        dve.wait_ge(S["q_ctx_hi"], 2 * hd + (j + 1))
                        x1, x2 = pair[:, p, 0, 0:LAT], pair[:, p, 1, 0:LAT]
                        V.tensor_tensor(tmp[:, 0, 0:LAT], x1, rcos, ALU.mult)
                        step.mark(V.tensor_tensor(tmp[:, 0, LAT:N], x2, rsin, ALU.mult))
                        V.tensor_tensor(tmp[:, 1, 0:LAT], x2, rcos, ALU.mult)
                        v = step.mark(V.tensor_tensor(tmp[:, 1, LAT:N], x1, rsin, ALU.mult))
                        after(v - 1)
                        V.tensor_tensor(full[:, j, 0:LAT], tmp[:, 0, 0:LAT], tmp[:, 0, LAT:N], ALU.subtract)
                        after(v)
                        V.tensor_tensor(full[:, j, LAT:N], tmp[:, 1, 0:LAT], tmp[:, 1, LAT:N], ALU.add
                                        ).then_inc(S["rot_ready"], 1)
                        for cols, src, name in ((slice(LAT, N), pair[:, p, :, LAT:N], "q_ctx_hi"),
                                                (slice(0, LAT), full[:, j, :].rearrange("p (c n) -> p c n", c=2), "q_lat_hi")):
                            dve.wait_ge(S[name], 2 * hd + (j + 1))
                            dve.wait_ge(S["rot_ready"], 2 * hd + (j + 1))
                            ins = V.scalar_tensor_tensor(out=a_lo[:, ch:ch + 2, cols], in0=src, scalar=sc,
                                                         in1=f32(a_hi[:, ch:ch + 2, cols]), op0=ALU.mult,
                                                         op1=ALU.subtract)
                        ins.then_inc(S["pair_free"], 1)
                    elif j < 4:
                        if j == 2:
                            lf, lb = lg[:, bass.ds(hd, 1)], lg[:, bass.ds(hd + RH, 1)]
                            V.tensor_scalar(o_buf[:, 0, 0:BAND], diff, 0.0, lf, ALU.max, ALU.mult).then_inc(S["e_pre"], 1)
                            V.tensor_scalar(tmp[:, 0, 0:BAND], diff, -1.0, 0.0, ALU.mult, ALU.max)
                            v = step.mark(V.tensor_scalar(tmp[:, 1, 0:BAND], diff, -1.0, float(LAT), ALU.mult, ALU.add))
                            V.tensor_scalar(o_buf[:, 2, 0:BAND], diff, float(LAT), lf, ALU.add, ALU.mult).then_inc(S["e_pre"], 1)
                            after(v)
                            V.tensor_scalar(o_buf[:, 1, 0:BAND], tmp[:, 0, 0:BAND], lb, None, ALU.mult).then_inc(S["e_pre"], 1)
                            V.tensor_scalar(o_buf[:, 3, 0:BAND], tmp[:, 1, 0:BAND], lb, None, ALU.mult).then_inc(S["e_pre"], 1)
                            dve.wait_ge(S["e_exp"], hd + 1)
                            dve.wait_ge(S["e_pre"], 4 * hd + 4)
                            V.scalar_tensor_tensor(out=tmp[:, 0, 0:BAND], in0=diff, scalar=0.0, in1=o_buf[:, 0, 0:BAND],
                                                   op0=ALU.is_ge, op1=ALU.mult)
                            v = step.mark(V.scalar_tensor_tensor(out=tmp[:, 1, 0:BAND], in0=diff, scalar=0.0,
                                                                 in1=o_buf[:, 1, 0:BAND], op0=ALU.is_le, op1=ALU.mult))
                            V.tensor_tensor(band[:, 1, :], o_buf[:, 2, 0:BAND], o_buf[:, 3, 0:BAND], ALU.add)
                            after(v)
                            step.mark(V.tensor_tensor(band[:, 0, :], tmp[:, 0, 0:BAND], tmp[:, 1, 0:BAND], ALU.add))
                        dve.wait_ge(S["v_hi"], 2 * hd + (j - 1))
                        cols = slice((j - 2) * 256, (j - 1) * 256)
                        V.tensor_tensor(a_lo[:, CH_V:CH_V + 4, cols],
                                        pair[:, p, :, :].rearrange("p b (t n) -> p (b t) n", t=2),
                                        f32(a_hi[:, CH_V:CH_V + 4, cols]), ALU.subtract).then_inc(S["pair_free"], 1)
                        if j == 3:
                            after(band_step(step))
                            near, far = band[:, 0], band[:, 1]
                            lo_, hi_ = slice(P, BAND), slice(0, LAT)

                            def masked(g):
                                dve.wait_ge(S["s_mm"], 3 * hd + (g + 1))
                                m0, m1 = ((far[:, lo_], near[:, lo_]), (far[:, hi_], near[:, hi_]),
                                          (near[:, lo_], near[:, hi_]))[g]
                                V.tensor_tensor(tmp[:, g % 2, 0:LAT], psx[:, g, 0:LAT], m0, ALU.mult)
                                V.tensor_tensor(tmp[:, g % 2, LAT:N], psx[:, g, LAT:N], m1, ALU.mult
                                                ).then_inc(S["ms_ready"], 1)

                            def masked_lo(g):
                                dve.wait_ge(S["ms_hi"], 3 * hd + (g + 1))
                                dve.wait_ge(S["ms_ready"], 3 * hd + (g + 1))
                                V.tensor_tensor(a_lo[:, CH_S + g, :], tmp[:, g % 2, :], f32(a_hi[:, CH_S + g, :]),
                                                ALU.subtract).then_inc(S["s_split"], 1)
                            masked(0)
                            masked(1)
                            masked_lo(0)
                            dve.wait_ge(S["s_split"], 3 * hd + 1)
                            masked(2)
                            masked_lo(1)
                            masked_lo(2)
                    elif j == 4:
                        dve.wait_ge(S["sg_ready"], 2 * hd + 1)
                        V.memset(mark[:, :], 0.0).then_inc(S["pair_free"], 1)
                    elif j == 5:
                        for e in range(4):
                            dve.wait_ge(S["o_mm"], 4 * hd + (e + 1))
                            V.tensor_copy(o_buf[:, e, :], psx[:, e % 3]).then_inc(S["o_copied"], 1)
                            if e >= 2:
                                add_o_square(hd, e - 1)
                        add_o_square(hd, 3)
                        norm_rstd(S_RET + hd, 1, N)
                        dve.wait_ge(S["st_bcast"], S_RET + 1 + hd)
                        dve.wait_ge(S["o_copied"], 4 * hd + 4)
                        for e in range(4):
                            v = step.mark(V.tensor_tensor(o_buf[:, e, :], o_buf[:, e, :], psx[:, 1], ALU.mult))
                        dve.wait_ge(S["sg_ready"], 2 * hd + 2)
                        V.memset(mark[:, :], 0.0).then_inc(S["pair_free"], 1)
                        after(v)

                        def og(e):
                            V.tensor_tensor(tmp[:, e % 2, :], o_buf[:, e, :], sg_buf[:, e, :], ALU.mult
                                            ).then_inc(S["og_ready"], 1)
                        og(0)
                        for e in range(4):
                            if e in (1, 2):
                                dve.wait_ge(S["og_lo"], 4 * hd + e)
                            if e < 3:
                                og(e + 1)
                            dve.wait_ge(S["og_hi"], 4 * hd + (e + 1))
                            dve.wait_ge(S["og_ready"], 4 * hd + (e + 1))
                            V.tensor_tensor(a_lo[:, e, :], tmp[:, e % 2, :], f32(a_hi[:, e, :]), ALU.subtract
                                            ).then_inc(S["og_lo"], 1)
                    else:
                        dve.wait_ge(S["pe_unit"], U + (j + 1) + 1)
                        for i in range(4):
                            src = (pair[:, p, 0], pair[:, p, 1], psx[:, 0], psx[:, 2])[i]
                            add_x((j - 6) * 4 + i, src, N, i == 3)

            def band_step(s):
                return s.it * s.per + (s.base + s.local)
            RET_STEPS = 2 * 2 + 3 + 1 + 4
            with dve.Fori(0, RH) as hd:
                step.enter(hd, RET_STEPS)
                retention(hd)
            step.leave(RH)
            zero_sums()
            for d in range(KD):
                add_square(d, d % 2, SS_RET, N)
            norm(S_NORM[(0, 2)], 0, 2, N)
            ffn(0, 1, N)
            norm(S_NORM[(1, 0)], 1, 0, N)
            ffn(1, 0, N)
            norm(S_NORM[(1, 1)], 1, 1, N)

            U = U_GQA

            def job_norm(job, src, gain, halves):
                norm_rstd(S_GQA + job, 1, N)
                dve.wait_ge(S["st_bcast"], S_GQA + job + 1)
                R = psx[:, job % 2, :]
                if len(src.shape) == 3:
                    gi = full[:, 0, :].rearrange("p (c n) -> p c n", c=2)
                else:
                    gi = full[:, 0, :]
                v = step.mark(V.tensor_copy(park[:, 7, :], R))
                after(v)
                pk = park[:, 7, :].rearrange("p (c n) -> p c n", c=2) if len(src.shape) == 3 else park[:, 7, :]
                v = step.mark(V.scalar_tensor_tensor(out=gi, in0=src, scalar=vecT[:, gain:gain + 1], in1=pk,
                                                     op0=ALU.mult, op1=ALU.mult))
                after(v)
                w = halves * LAT
                V.tensor_copy(tmp[0:64, 0, 0:w], full[64:P, 0, 0:w])
                step.mark(V.tensor_copy(tmp[64:P, 0, 0:w], full[0:64, 0, 0:w]))
                for c in range(halves):
                    cs = slice(c * LAT, (c + 1) * LAT)
                    v = step.mark(V.tensor_tensor(tmp[:, 1, cs], full[:, 0, cs], acos, ALU.mult))
                after(v - halves)
                for c in range(halves):
                    cs = slice(c * LAT, (c + 1) * LAT)
                    v = step.mark(V.tensor_tensor(park[:, 6, cs], tmp[:, 0, cs], asin, ALU.mult))
                after(v)
                v = V.tensor_tensor(full[:, 0, 0:w], tmp[:, 1, 0:w], park[:, 6, 0:w], ALU.add)
                v.then_inc(S["kn_ready"], 1)
                ch = job if job < 2 else CH_GQ + job - 2
                dve.wait_ge(S["kn_hi"], job + 1)
                dve.wait_ge(S["kn_ready"], job + 1)
                V.tensor_tensor(a_lo[:, ch, :], full[:, 0, :], f32(a_hi[:, ch, :]), ALU.subtract).then_inc(S["kn_lo"], 1)
                dve.wait_ge(S["kn_lo"], job + 1)

            def release():
                V.memset(mark[:, :], 0.0).then_inc(S["pair_free"], 1)
            split_lo(U + 1, 1)
            job_norm(0, pair[:, 0, 0], ROW_KG, 1)
            job_norm(1, pair[:, 0, 1], ROW_KG, 1)
            release()
            split_lo(U + 2, 0)
            dve.wait_ge(S["gv_hi"], 1)
            V.tensor_tensor(a_lo[:, CH_GV:CH_GV + 2, :], pair[:, 1, :, :], f32(a_hi[:, CH_GV:CH_GV + 2, :]), ALU.subtract
                            ).then_inc(S["pair_free"], 1)
            for i in range(4):
                split_lo(U + 3 + i, (i + 1) % 2)
                job_norm(2 + i, pair[:, i % 2, :, 0:LAT], ROW_QG, 2)
                release()
            split_lo(U + 7, 1)

            def peak(hh):
                for qb in range(2):
                    n = 2 * hh + qb
                    dve.wait_ge(S["sc_mm"], n + 1)
                    v = step.mark(V.reduce_max(smx[:, n:n + 1], pair[:, hh % 2, qb], AX_X))
                    after(v)
                    V.tensor_scalar(snb[:, n:n + 1], smx[:, n:n + 1], -AHD ** -0.5, None, ALU.mult
                                    ).then_inc(S["nb_ready"], 1)
            peak(0)
            for hh in range(AH):
                for qb in range(2):
                    n = 2 * hh + qb
                    dve.wait_ge(S["p_exp"], n + 1)
                    v = step.mark(V.reciprocal(sinv[:, n:n + 1], sden[:, n:n + 1]))
                    after(v)
                    pb = park[:, 2 * (hh % 2) + qb, :]
                    V.tensor_scalar(pb, pb, sinv[:, n:n + 1], None, ALU.mult).then_inc(S["p_ready"], 1)
                if hh + 1 < AH:
                    peak(hh + 1)
                for b in range(2):
                    dve.wait_ge(S["pt_hi"], 2 * hh + b + 1)
                    V.tensor_tensor(a_lo[:, CH_GP + b, :], psx[:, b], f32(a_hi[:, CH_GP + b, :]), ALU.subtract
                                    ).then_inc(S["pt_lo"], 1)
                dve.wait_ge(S["oT_hi"], hh + 1)
                cs = slice((hh % 2) * LAT, (hh % 2 + 1) * LAT)
                V.tensor_tensor(a_lo[:, CH_GO + hh // 2, cs], psx[:, 2, 0:LAT], f32(a_hi[:, CH_GO + hh // 2, cs]),
                                ALU.subtract).then_inc(S["oT_lo"], 1)
            gates(1, 5, 1.0)
            zero_sums()
            for i in range(4):
                if i:
                    split_lo(U + 7 + i, (i + 1) % 2)
                    for d in (2 * i - 2, 2 * i - 1):
                        add_square(d, d % 2, SS_GQA, LAT)
                dve.wait_ge(S["pe_unit"], U + 7 + i + 1)
                for c in range(2):
                    add_x(2 * i + c, pair[:, i % 2, c], LAT, c == 1)
            for d in (KD - 2, KD - 1):
                add_square(d, d % 2, SS_GQA, LAT)
            norm(S_NORM[(1, 2)], 1, 2, LAT)
            ffn(1, 1, LAT)
            norm_rstd(S_FIN, 1, LAT)
            dve.wait_ge(S["st_bcast"], S_FIN + 1)
            for d in range(KD):
                if d >= 2:
                    dve.wait_ge(S["fin_tr"], d - 1)
                V.scalar_tensor_tensor(out=tmp[:, d % 2, 0:LAT], in0=xT[:, d, 0:LAT], scalar=vecT[:, ROW_FG + d:ROW_FG + d + 1],
                                       in1=psx[:, 1, 0:LAT], op0=ALU.mult, op1=ALU.mult).then_inc(S["fin_ready"], 1)
            dve.wait_ge(S["fin_tr"], KD)
            for t in range(2):
                V.tensor_copy(park[:, 2 * t:2 * t + 2, :], pair[:, t, :, :]).then_inc(S["fin_copied"], 1)


NSS = {0: 8, 1: 16, 6: 24, 7: 32, 8: 40, 15: 48, 16: 56}
H0 = {(0, 0): 0, (0, 1): 8, (0, 2): 16, (1, 0): 24, (1, 1): 32, (1, 2): 40}
SS0 = {(0, 0): 8, (0, 1): 24, (1, 0): 32, (1, 1): 48}
SS_RET, SS_GQA = 16, 40
MODS_NORM = {(0, 0): 0, (0, 1): 28, (0, 2): 28, (1, 0): 50, (1, 1): 64, (1, 2): 64}
MODS_AT = {(0, 0): 12, (0, 1): 28, (1, 0): 62, (1, 1): 64}



def packed_units(w1, w2, ret_in, ret_out, qkv, wo):
    import numpy as np

    units = np.zeros((U_END, P, UNIT), np.float32)

    def put(u, block):
        units[u, :, :block.shape[0] * block.shape[2]] = block.transpose(1, 0, 2).reshape(P, -1)

    for (l, f), u in U_FFN.items():
        up = w1[l, f].reshape(KD, P, 2, FFN // P, P)
        down = w2[l, f].reshape(FFN // P, P, KD, P)
        r0 = 0
        for rows in HALVES:
            for r in range(rows):
                units[u + r] = up[:, :, :, r0 + r].transpose(1, 2, 0, 3).reshape(P, UNIT)
            for d in range(KD):
                put(u + rows + d, down[r0:r0 + rows, :, d])
            u, r0 = u + rows + KD, r0 + rows
    win = ret_in.reshape(KD, P, -1)
    wout = ret_out.reshape(-1, P, D)
    for hd in range(RH):
        cols = (RDK * hd, D + RDK * hd, 2 * D + RDV * hd, 2 * D + RDV * hd + 256,
                4 * D + RDV * hd, 4 * D + RDV * hd + 256)
        for j, c in enumerate(cols):
            put(U_RET + 8 * hd + j, win[:, :, c:c + 256])
        for j in range(2):
            put(U_RET + 8 * hd + 6 + j, wout[4 * hd:4 * hd + 4, :, j * 512:(j + 1) * 512])
    for j, c in enumerate((D, D + 256, 0, 256, 512, 768)):
        put(U_GQA + j, qkv.reshape(KD, P, -1)[:, :, c:c + 256])
    for j in range(4):
        put(U_GQA + 6 + j, wo.reshape(KD, P, D)[:, :, j * 256:(j + 1) * 256])
    return units


def shape_constants():
    import numpy as np

    f = np.float32
    t = np.arange(LAT).astype(f)
    half = RDK // 2
    freq = (f(10000.0) ** (-np.arange(half, dtype=f) / f(half))).astype(f)
    ang = (freq[:, None] * t[None]).astype(f)
    quarter = AHD // 4
    qf = (f(10000.0) ** (-np.arange(quarter, dtype=f) / f(quarter))).astype(f)
    row, col = (np.arange(LAT) // 64).astype(f), (np.arange(LAT) % 64).astype(f)
    ax = np.concatenate([qf[:, None] * row[None], qf[:, None] * col[None]]).astype(f)
    sin = np.sin(ax.astype(np.float64))
    parts = [np.eye(P), np.ones((P, P)), np.arange(BAND)[None] - P - np.arange(P)[:, None],
             np.cos(ang.astype(np.float64)), np.sin(ang.astype(np.float64)),
             np.tile(np.cos(ax.astype(np.float64)), (2, 1)), np.concatenate([-sin, sin])]
    return np.concatenate(parts, axis=1).astype(f)


def kernel(**inputs):
    import numpy as np
    import concourse.bacc as bacc
    from concourse.bass_utils import run_bass_kernel_spmd

    i = {k: np.asarray(v) for k, v in inputs.items()}
    arrays = {
        "x": i["x"][0], "ctx": i["ctx"][0],
        "vecs": np.concatenate([i[n].reshape(-1, P) for n in
                                ("ada_b", "norm_g", "final_g", "c", "c_ctx", "att_q_gain", "att_k_gain")]),
        "dec": np.concatenate([i["ret_decay_f"], i["ret_decay_b"]], axis=1),
        "consts": shape_constants(),
        "ada_w": i["ada_w"].reshape(DEPTH, KD, P, ADA_L, ADA).transpose(0, 3, 2, 1, 4).reshape(-1, P, UNIT),
        "units": packed_units(i["ffn_w1"], i["ffn_w2"], i["ret_w_in"][0], i["ret_w_out"][0],
                              i["att_w_qkv"][0], i["att_w_o"][0]),
    }
    arrays = {f"in_{k}": np.ascontiguousarray(v) for k, v in arrays.items()}
    nc = bacc.Bacc("TRN2", target_bir_lowering=False, num_devices=1)
    args = [nc.dram_tensor(k, a.shape, mybir.dt.from_np(a.dtype), kind="ExternalInput").ap() for k, a in arrays.items()]
    out = nc.dram_tensor("out", (LAT, D), F32, kind="ExternalOutput").ap()
    build(nc, *args, out)
    r = run_bass_kernel_spmd(nc, [arrays], core_ids=[0])
    return r.results[0]["out"].reshape(1, LAT, D)
```

```python
from contextlib import ExitStack

import concourse.bass as bass
from concourse import mybir

F32 = mybir.dt.float32
F32R = mybir.dt.float32r
ALU = mybir.AluOpType
ACT = mybir.ActivationFunctionType
AX_X = mybir.AxisListType.X

P = 128
D = 1024
KD = D // P
LAT = 256
CTX = 256
N = LAT + CTX
DEPTH = 2
NMOD = 9
FFN = 2816
EPS = 1e-6
RH, RDK, RDV = 4, 256, 512
AH, AKV, AHD = 8, 2, 128
UNIT = 2048
HALVES = (12, 10)
ADA = 256
ADA_L = NMOD * D // ADA
ADA_PRO = 8
BAND = 384

UNITS_FFN = sum(HALVES) + 2 * KD
UNITS_RET_HEAD = 8
U_FFN = {(0, 0): 0}
U_RET = UNITS_FFN
U_FFN[(0, 1)] = U_RET + RH * UNITS_RET_HEAD
U_FFN[(1, 0)] = U_FFN[(0, 1)] + UNITS_FFN
U_GQA = U_FFN[(1, 0)] + UNITS_FFN
U_FFN[(1, 1)] = U_GQA + 10
U_END = U_FFN[(1, 1)] + UNITS_FFN
G_FFN = {(0, 0): 0, (0, 1): 22, (1, 0): 44, (1, 1): 66}

ROW_NG, ROW_FG, ROW_C, ROW_CX, ROW_QG, ROW_KG, ROWS = 144, 192, 200, 208, 216, 217, 218
C_ID, C_ONE, C_D, C_RC, C_RS, C_AC, C_AS, C_END = 0, 128, 256, 640, 896, 1152, 1408, 1664

CH_Q, CH_K, CH_V, CH_S = 4, 6, 8, 12
CH_GV, CH_GQ, CH_GO, CH_GP = 2, 4, 8, 12
S_NORM = {(0, 0): 0, (0, 1): 1, (0, 2): 6, (1, 0): 7, (1, 1): 8, (1, 2): 15}
S_RET, S_GQA, S_FIN = 2, 9, 16


ADA_RUNS = [(2, 12), (16, 30), (U_FFN[(0, 1)] + 2, U_FFN[(0, 1)] + 12), (U_FFN[(0, 1)] + 20, U_FFN[(0, 1)] + 30),
            (U_FFN[(1, 0)] + 2, U_FFN[(1, 0)] + 12), (U_FFN[(1, 0)] + 20, U_FFN[(1, 0)] + 30)]


def unit_sizes():
    runs = []
    for key in sorted(U_FFN):
        u = U_FFN[key]
        for rows in HALVES:
            runs += [(u, rows, UNIT), (u + rows, KD, rows * P)]
            u += rows + KD
        if key == (0, 0):
            runs.append((U_RET, RH * UNITS_RET_HEAD, UNIT))
        if key == (1, 0):
            runs.append((U_GQA, 10, UNIT))
    return runs


def ada_slice(u):
    a = ADA_PRO
    for first, end in ADA_RUNS:
        if first <= u < end:
            return a + u - first
        a += end - first
    return None


assert sum(end - first for first, end in ADA_RUNS) + ADA_PRO == DEPTH * ADA_L


def bodies(u, count, lag=0):
    at = [ada_slice(u + 2 * b - lag) for b in range(count)]
    runs, lo = [], 0
    for b in range(1, count + 1):
        if (b == count or (at[b] is None) != (at[lo] is None) or at[b] == DEPTH * ADA_L - 2
                or (at[lo] is not None and at[b] - at[lo] != 2 * (b - lo))):
            runs.append((lo, b, None if at[lo] is None else at[lo] - 2 * lo))
            lo = b
    return runs


class Steps:

    def __init__(self, sem):
        self.sem, self.base, self.it, self.per, self.local = sem, 0, 0, 0, 0

    def enter(self, it, per):
        self.base += self.local
        self.it, self.per, self.local = it, per, 0

    def leave(self, count):
        assert self.local == self.per, (self.local, self.per)
        self.base, self.it, self.per, self.local = self.base + self.per * count, 0, 0, 0

    def last(self):
        return self.it * self.per + (self.base + self.local)

    def mark(self, ins):
        ins.then_inc(self.sem, 1)
        self.local += 1
        return self.last()


def build(nc, x, ctx, vecs, dec, consts, ada_w, units, out):
    stack = ExitStack()
    with stack:
        def sb(name, shape, dt=F32):
            return stack.enter_context(nc.sbuf_tensor(name, shape, dt))

        def sem(name):
            return stack.enter_context(nc.semaphore(name))

        xT = sb("xT", [P, KD, N])
        h_hi = sb("h_hi", [P, KD, N], F32R)
        h_lo = sb("h_lo", [P, KD, N], F32R)
        a_hi = sb("a_hi", [P, 15, N], F32R)
        a_lo = sb("a_lo", [P, 15, N], F32R)
        raw = sb("raw", [P, 2, UNIT])
        w_hi = sb("w_hi", [P, 2, UNIT], F32R)
        w_lo = sb("w_lo", [P, 2, UNIT], F32R)
        ada = sb("ada", [P, UNIT])
        acc = sb("acc", [P, 2, ADA])
        park = sb("park", [P, 8, N])
        tmp = sb("tmp", [P, 2, N])
        full = sb("full", [P, 2, N])
        ssum = sb("ssum", [P, N])
        sq = sb("sq", [P, N])
        diag = sb("diag", [P, N])
        cst = sb("cst", [P, C_END])
        band = sb("band", [P, 2, BAND])
        vecT = sb("vecT", [P, ROWS])
        modT = sb("modT", [P, DEPTH * NMOD * KD, 2])
        sT = sb("sT", [P, KD, 2])
        aff = sb("aff", [P, KD, 2])
        gate = sb("gate", [P, KD, 2])
        sd = sb("sd", [P, 4])
        rs = sb("rs", [P, 4])
        lg = sb("lg", [P, 2 * RH])
        dec_row = sb("dec_row", [1, 2 * RH])
        smx, snb, sden, sinv = (band[:, 0, 2 * AH * i:2 * AH * (i + 1)] for i in range(4))
        mark = sb("mark", [P, 1])
        job_diag = [diag, acc[:, :, :].rearrange("p c n -> p (c n)")]

        pair = stack.enter_context(nc.psum_tensor("pair", [P, 2, 2, N], F32))
        ps_s = stack.enter_context(nc.psum_tensor("ps_s", [P, N], F32))
        psx = stack.enter_context(nc.psum_tensor("psx", [P, 3, N], F32))

        ident = cst[:, C_ID:C_ID + P]
        ones = cst[:, C_ONE:C_ONE + P]
        diff = cst[:, C_D:C_D + BAND]
        rcos, rsin = cst[:, C_RC:C_RC + LAT], cst[:, C_RS:C_RS + LAT]
        acos, asin = cst[:, C_AC:C_AC + LAT], cst[:, C_AS:C_AS + LAT]
        vrows = tmp[:, 0, 0:2 * P]
        o_buf, sg_buf = park[:, 0:4, :], park[:, 4:8, :]

        names = """
            consts_in vecs_in dec_in x_in raw_landed0 raw_landed1 ada_landed0 ada_landed1
            pro_landed0 pro_landed1 pro_landed2 pro_landed3 pro_landed4 pro_landed5 pro_landed6 pro_landed7
            vec_tr vec_up x_tr x_up dec_mm dec_exp s_rdy pro_acc pro_mm mod_up
            hi_ready lo_ready pe_unit pair_free
            acc_half acc_ready ada_mm mod_ready
            x_sq ss_ready st_sum st_sqrt st_diag st_bcast t_ready n_full n_hi h_ready
            silu_ready u_ready u_hi
            q_ctx_hi rot_ready q_lat_hi v_hi e_pre e_exp s_mm ms_ready ms_hi s_split
            o_mm o_copied o_sq o_sum sg_ready og_ready og_hi og_lo
            g_sq gv_hi kn_norm kn_swap kn_ready kn_hi kn_lo
            sc_mm nb_ready p_exp inv_ready p_ready pt_mm pt_hi pt_lo oT_mm oT_hi oT_lo
            fin_ready fin_tr fin_copied out_done dve_step""".split()
        S = {n: sem(n) for n in names}
        raw_landed = [S["raw_landed0"], S["raw_landed1"]]
        ada_landed = [S["ada_landed0"], S["ada_landed1"]]
        pro_landed = [S[f"pro_landed{a}"] for a in range(ADA_PRO)]

        def f32(ap):
            return ap.bitcast(F32)

        pro_slot = [xT[:, 0:4, :].rearrange("p c n -> p (c n)"), raw[:, 0, :], ada[:, :],
                    park[:, 0:4, :].rearrange("p c n -> p (c n)"), xT[:, 4:8, :].rearrange("p c n -> p (c n)"),
                    raw[:, 1, :], raw[:, 1, :], park[:, 4:8, :].rearrange("p c n -> p (c n)")]
        pro_acc = [acc[:, :, :]] + [t.rearrange("p (c n) -> p c n", c=2) for t in (sq[:, :], tmp[:, 0, :], tmp[:, 1, :])]

        block = stack.enter_context(nc.Block())

        @block.sync
        def _(sp):
            def load_unit(u, j, size, wait):
                if wait:
                    sp.wait_ge(S["lo_ready"], u - 1)
                sp.dma_start(raw[:, j:j + 1, 0:size], units[bass.ds(u, 1), :, 0:size].rearrange("u p n -> p u n")
                             ).then_inc(raw_landed[j], 16)

            def load_ada_half(a, half):
                cols = slice(half * UNIT // 2, (half + 1) * UNIT // 2)
                sp.dma_start(ada[:, cols].unsqueeze(1), ada_w[bass.ds(a, 1), :, cols].rearrange("u p n -> p u n")
                             ).then_inc(ada_landed[half], 16)

            def load_ada(a):
                if isinstance(a, int) and a == ADA_PRO:
                    sp.wait_ge(S["pro_mm"], 3)
                    load_ada_half(a, 0)
                else:
                    sp.wait_ge(S["acc_ready"], a - ADA_PRO)
                load_ada_half(a, 1)
                if not (isinstance(a, int) and a == DEPTH * ADA_L - 1):
                    sp.wait_ge(S["acc_half"], a - (ADA_PRO - 1))
                    load_ada_half(a + 1, 0)

            sp.dma_start(cst[:, :], consts).then_inc(S["consts_in"], 16)
            sp.dma_start(vrows[:, 0:P], vecs[0:P, :]).then_inc(S["vecs_in"], 16)
            sp.dma_start(vrows[0:ROWS - P, P:2 * P], vecs[P:ROWS, :]).then_inc(S["vecs_in"], 16)
            sp.dma_start(dec_row[:, :], dec).then_inc(S["dec_in"], 16)

            def load_pro(a):
                sp.dma_start(pro_slot[a], ada_w[a]).then_inc(pro_landed[a], 16)
            for a in (0, 4, 1, 5):
                load_pro(a)
            xin = park[:, :, :].rearrange("p (t a) n -> p t (a n)", t=4)
            sp.dma_start(xin[:, 0:2], x.rearrange("(t p) d -> p t d", p=P)).then_inc(S["x_in"], 16)
            sp.dma_start(xin[:, 2:4], ctx.rearrange("(t p) d -> p t d", p=P)).then_inc(S["x_in"], 16)
            load_pro(2)
            sp.wait_ge(S["pro_acc"], 2)
            load_pro(6)

            def stream(u, count, size):
                def body(it, a0):
                    for j in range(2):
                        if isinstance(it, int) and u + it == 0:
                            if j == 0:
                                sp.wait_ge(S["pro_mm"], 2)
                            else:
                                sp.wait_ge(S["x_tr"], KD)
                                load_pro(3)
                                load_pro(7)
                                sp.wait_ge(S["pro_acc"], 3)
                            load_unit(j, j, size, False)
                        else:
                            load_unit(u + 2 * it + j, j, size, True)
                        if a0 is not None:
                            load_ada(a0 + 2 * it + j)
                for lo, hi, a0 in bodies(u, count // 2, lag=2):
                    if u + lo == 0 or (a0 is not None and a0 + 2 * lo == ADA_PRO):
                        body(lo, a0)
                        lo += 1
                    if hi == lo + 1:
                        body(lo, a0)
                    elif hi > lo:
                        with sp.Fori(lo, hi) as it:
                            body(it, a0)
            for u0, count, size in unit_sizes():
                stream(u0, count, size)
            outv = out.rearrange("(t p) d -> p t d", p=P)
            for t in range(2):
                sp.wait_ge(S["fin_copied"], t + 1)
                sp.dma_start(outv[:, t], park[:, 2 * t:2 * t + 2, :].rearrange("p a n -> p (a n)")
                             ).then_inc(S["out_done"], 16)
            sp.wait_ge(S["out_done"], 32)

        @block.tensor
        def _(pe):
            mm = nc.tensor.matmul

            def mm3(dst, whi, wlo, xhi, xlo, start, stop):
                mm(dst, wlo, xhi, start=start, stop=False)
                mm(dst, whi, xlo, start=False, stop=False)
                return mm(dst, whi, xhi, start=False, stop=stop)

            def wait_unit(u):
                if not isinstance(u, int) or u > 0:
                    pe.wait_ge(S["pair_free"], u + 1)
                pe.wait_ge(S["lo_ready"], u + 1)

            def rows_sum(src, s, tiles, bank=ps_s):
                for t in range(tiles):
                    last = mm(bank[:, 8 + t:9 + t], src[:, t * P:(t + 1) * P], ones[:, 0:1], start=True, stop=True)
                last.then_inc(S["st_sum"], 1)

            def rows_bcast(bank, s, width, src=None):
                pe.wait_ge(S["st_diag"], s + 1)
                mm(bank[:, 0:width], ones, (diag if src is None else src)[:, 0:width], start=True, stop=True).then_inc(S["st_bcast"], 1)

            def ada_mm(a):
                pe.wait_ge(S["acc_ready"], a - (ADA_PRO - 1))
                for c in range(2):
                    for cond in range(2):
                        last = mm(ps_s[:, 2 * c + cond:2 * c + cond + 1], acc[:, cond, c * P:(c + 1) * P],
                                  ones[:, 0:1], start=True, stop=True)
                last.then_inc(S["ada_mm"], 1)

            def unit_cols(u, j, width, h0, halfway=None):
                wait_unit(u)
                whi = w_hi[:, j, :].rearrange("p (k c n) -> p k c n", k=KD, c=2)
                wlo = w_lo[:, j, :].rearrange("p (k c n) -> p k c n", k=KD, c=2)
                dst = [pair[:, j, 0, 0:width], pair[:, j, 1, 0:width]]
                for k in range(KD):
                    if k == KD // 2 and halfway is not None:
                        halfway()
                    pe.wait_ge(S["h_ready"], h0 + k + 1)
                    for c in range(2):
                        last = mm3(dst[c], whi[:, k, c], wlo[:, k, c], h_hi[:, k, 0:width], h_lo[:, k, 0:width],
                                   k == 0, k == KD - 1)
                last.then_inc(S["pe_unit"], 1)

            def unit_gu(u, j, width, h0):
                wait_unit(u)
                whi = w_hi[:, j, :].rearrange("p (c k n) -> p c k n", c=2, k=KD)
                wlo = w_lo[:, j, :].rearrange("p (c k n) -> p c k n", c=2, k=KD)
                for k in range(KD):
                    pe.wait_ge(S["h_ready"], h0 + k + 1)
                    for c in range(2):
                        last = mm3(pair[:, j, c, 0:width], whi[:, c, k], wlo[:, c, k], h_hi[:, k, 0:width],
                                   h_lo[:, k, 0:width], k == 0, k == KD - 1)
                last.then_inc(S["pe_unit"], 1)

            def unit_down(u, j, rows, width, u_gu):
                wait_unit(u)
                for r in range(rows):
                    pe.wait_ge(S["pair_free"], u_gu + r + 3)
                    last = mm3(pair[:, j, 0, 0:width], w_hi[:, j, r * P:(r + 1) * P], w_lo[:, j, r * P:(r + 1) * P],
                               a_hi[:, r, 0:width], a_lo[:, r, 0:width], r == 0, r == rows - 1)
                last.then_inc(S["pe_unit"], 1)

            def norm(n, tiles):
                pe.wait_ge(S["ss_ready"], NSS[n])
                rows_sum(ssum, n, tiles)
                rows_bcast(psx[:, 1], n, tiles * P)

            def ffn(l, f, width):
                u = U_FFN[(l, f)]
                h0 = H0[(l, 2 * f)]
                for half, rows in enumerate(HALVES):
                    for lo, hi, a0 in bodies(u, rows // 2):
                        with pe.Fori(lo, hi) as it:
                            for j in range(2):
                                unit_gu(u + 2 * it + j, j, width, h0)
                                if a0 is not None:
                                    ada_mm(a0 + 2 * it + j)
                    u_gu, u = u, u + rows
                    for lo, hi, a0 in bodies(u, KD // 2):
                        with pe.Fori(lo, hi) as it:
                            for j in range(2):
                                unit_down(u + 2 * it + j, j, rows, width, u_gu)
                                if a0 is not None:
                                    ada_mm(a0 + 2 * it + j)
                    u += KD

            pe.wait_ge(S["consts_in"], 16)
            pe.wait_ge(S["vecs_in"], 32)
            nc.tensor.transpose(psx[:, 0, 0:P], vrows[:, 0:P], ident).then_inc(S["pe_unit"], 1)
            nc.tensor.transpose(psx[:, 0, P:ROWS], vrows[0:ROWS - P, P:2 * P], ident[0:ROWS - P, 0:ROWS - P]
                                ).then_inc(S["vec_tr"], 1)
            pe.wait_ge(S["dec_in"], 16)
            mm(psx[:, 1, 0:2 * RH], ones[0:1, :], dec_row[:, :], start=True, stop=True).then_inc(S["dec_mm"], 1)

            def x_transposes(d):
                xin = park[:, :, :].rearrange("p (t a) n -> p t (a n)", t=4)
                if d >= 4:
                    pe.wait_ge(S["x_up"], d - 3)
                for t in range(4):
                    last = nc.tensor.transpose(pair[:, (d % 4) // 2, d % 2, t * P:(t + 1) * P],
                                               xin[:, t, d * P:(d + 1) * P], ident)
                last.then_inc(S["x_tr"], 1)

            def pro_slice(a):
                pe.wait_ge(pro_landed[a], 16)
                w = pro_slot[a].rearrange("p (k c n) -> p k c n", k=KD, c=2)
                for c in range(2):
                    for k in range(KD):
                        last = mm(ps_s[:, 16 + 4 * a + 2 * c:18 + 4 * a + 2 * c], w[:, k, c], sT[:, k, :],
                                  start=k == 0, stop=k == KD - 1)
                last.then_inc(S["pro_mm"], 1)
            pe.wait_ge(S["s_rdy"], 1)
            pro_slice(0)
            pro_slice(1)
            pe.wait_ge(S["x_in"], 32)
            for d in range(KD):
                x_transposes(d)
            pro_slice(2)

            def pro_rows(i):
                pe.wait_ge(S["pro_acc"], i + 1)
                for c in range(2):
                    for cond in range(2):
                        q = 16 + 4 * (4 + i) + 2 * c + cond
                        last = mm(ps_s[:, q:q + 1], pro_acc[i][:, cond, c * P:(c + 1) * P], ones[:, 0:1],
                                  start=True, stop=True)
                return last
            for i in range(3):
                pro_rows(i)
            pro_slice(3)
            pe.wait_ge(S["ss_ready"], NSS[0])
            rows_sum(ssum, 0, 4, psx[:, 2])
            pro_rows(3).then_inc(S["pro_mm"], 1)
            rows_bcast(psx[:, 1], 0, N)
            ffn(0, 0, N)
            pe.wait_ge(S["mod_ready"], MODS_NORM[(0, 1)])
            norm(1, 4)

            def retention(hd):
                U = U_RET + 8 * hd
                h0 = H0[(0, 1)]
                for j in (0, 1):
                    unit_cols(U + j, j, N, h0)
                for j in (2, 3):
                    wait_unit(U + j)
                    whi = w_hi[:, j % 2, :].rearrange("p (k n) -> p k n", k=KD)
                    wlo = w_lo[:, j % 2, :].rearrange("p (k n) -> p k n", k=KD)
                    for t in range(4):
                        dst = pair[:, j % 2, t // 2, (t % 2) * 256:(t % 2 + 1) * 256]
                        for k in range(KD):
                            last = mm3(dst, h_hi[:, k, t * P:(t + 1) * P], h_lo[:, k, t * P:(t + 1) * P],
                                       whi[:, k], wlo[:, k], k == 0, k == KD - 1)
                    last.then_inc(S["pe_unit"], 1)
                pe.wait_ge(S["pair_free"], U + 3 + 1)
                for g in range(3):
                    for kt, q0, qn in ([(2 + g, 0, N)] if g < 2 else [(0, 0, LAT), (1, LAT, LAT)]):
                        for c in range(2):
                            last = mm3(psx[:, g, q0:q0 + qn], a_hi[:, CH_K + c, kt * P:(kt + 1) * P],
                                       a_lo[:, CH_K + c, kt * P:(kt + 1) * P], a_hi[:, CH_Q + c, 0:qn],
                                       a_lo[:, CH_Q + c, 0:qn], c == 0, c == 1)
                    last.then_inc(S["s_mm"], 1)
                unit_cols(U + 4, 0, N, h0)
                pe.wait_ge(S["s_split"], 3 * hd + 3)
                pe.wait_ge(S["pair_free"], U + 5 + 1)
                for e in range(4):
                    bank = psx[:, e % 3]
                    if e == 3:
                        pe.wait_ge(S["o_copied"], 4 * hd + 1)
                    for n, (kt, ch, c0, qn) in enumerate(((2, 0, 0, N), (3, 1, 0, N), (0, 2, 0, LAT), (1, 2, LAT, LAT))):
                        last = mm3(bank[:, 0:qn], a_hi[:, CH_V + kt, e * P:(e + 1) * P],
                                   a_lo[:, CH_V + kt, e * P:(e + 1) * P], a_hi[:, CH_S + ch, c0:c0 + qn],
                                   a_lo[:, CH_S + ch, c0:c0 + qn], n == 0, n == 3)
                    last.then_inc(S["o_mm"], 1)
                wait_unit(U + 5)
                whi = w_hi[:, 1, :].rearrange("p (k c n) -> p k c n", k=KD, c=2)
                wlo = w_lo[:, 1, :].rearrange("p (k c n) -> p k c n", k=KD, c=2)
                for c in range(2):
                    for k in range(KD):
                        last = mm3(pair[:, 1, c], whi[:, k, c], wlo[:, k, c], h_hi[:, k], h_lo[:, k],
                                   k == 0, k == KD - 1)
                        if c == 1 and k == 2:
                            pe.wait_ge(S["o_copied"], 4 * hd + 4)
                            rows_bcast(psx[:, 1], S_RET + hd, N)
                    if c == 0:
                        pe.wait_ge(S["o_sum"], 3 * hd + 3)
                        rows_sum(ssum, S_RET + hd, 4)
                last.then_inc(S["pe_unit"], 1)
                for j in (6, 7):
                    wait_unit(U + j)
                    whi = w_hi[:, j % 2, :].rearrange("p (k n) -> p k n", k=4)
                    wlo = w_lo[:, j % 2, :].rearrange("p (k n) -> p k n", k=4)
                    banks = (pair[:, j % 2, 0], pair[:, j % 2, 1], psx[:, 0], psx[:, 2])
                    if j == 6:
                        pe.wait_ge(S["o_copied"], 4 * hd + 4)
                    for k, i in ([(k, i) for k in range(4) for i in range(4)] if j == 6 else
                                 [(k, i) for i in range(4) for k in range(4)]):
                        if j == 6:
                            pe.wait_ge(S["og_lo"], 4 * hd + (k + 1))
                        elif (k, i) == (0, 2):
                            pe.wait_ge(S["pair_free"], U + 9)
                        last = mm3(banks[i], whi[:, k, i * P:(i + 1) * P], wlo[:, k, i * P:(i + 1) * P],
                                   a_hi[:, k], a_lo[:, k], k == 0, k == 3)
                    last.then_inc(S["pe_unit"], 1)

            with pe.Fori(0, RH) as hd:
                retention(hd)
            norm(S_NORM[(0, 2)], 4)
            ffn(0, 1, N)
            pe.wait_ge(S["mod_ready"], MODS_NORM[(1, 0)])
            norm(S_NORM[(1, 0)], 4)
            ffn(1, 0, N)
            pe.wait_ge(S["mod_ready"], MODS_NORM[(1, 1)])
            norm(S_NORM[(1, 1)], 4)

            h0 = H0[(1, 1)]
            U = U_GQA

            def job_sum(job):
                pe.wait_ge(S["g_sq"], job + 1)
                pe.wait_ge(S["st_sqrt"], S_GQA + job)
                rows_sum(sq if job % 2 else ssum, S_GQA + job, 4)

            def job_bcast(job):
                if job >= 2:
                    pe.wait_ge(S["kn_norm"], job - 1)
                rows_bcast(psx[:, job % 2], S_GQA + job, N, job_diag[job % 2])
            unit_cols(U, 0, N, h0)
            wait_unit(U + 1)
            whi = w_hi[:, 1, :].rearrange("p (k n) -> p k n", k=KD)
            wlo = w_lo[:, 1, :].rearrange("p (k n) -> p k n", k=KD)
            for t in range(4):
                for k in range(KD):
                    last = mm3(pair[:, 1, t // 2, (t % 2) * 256:(t % 2 + 1) * 256], h_hi[:, k, t * P:(t + 1) * P],
                               h_lo[:, k, t * P:(t + 1) * P], whi[:, k], wlo[:, k], k == 0, k == KD - 1)
                if t < 2:
                    job_sum(t)
                if t in (1, 2):
                    job_bcast(t - 1)
            last.then_inc(S["pe_unit"], 1)
            for i in range(4):
                unit_cols(U + 2 + i, i % 2, LAT, h0, None if i == 0 else lambda: job_sum(1 + i))
                if i:
                    job_bcast(1 + i)
            job_sum(5)

            def scores(hh):
                g = hh // (AH // AKV)
                pe.wait_ge(S["kn_lo"], 3 + hh // 2)
                if hh >= 2:
                    pe.wait_ge(S["p_exp"], 2 * (hh - 2) + 2)
                else:
                    pe.wait_ge(S["pair_free"], U + 7 + 1)
                for qb in range(2):
                    c0 = (hh % 2) * LAT + qb * P
                    last = mm3(pair[:, hh % 2, qb], a_hi[:, CH_GQ + hh // 2, c0:c0 + P],
                               a_lo[:, CH_GQ + hh // 2, c0:c0 + P], a_hi[:, g], a_lo[:, g], True, True)
                    last.then_inc(S["sc_mm"], 1)

            def transposes(hh):
                if hh:
                    pe.wait_ge(S["pt_lo"], 2 * hh)
                else:
                    pe.wait_ge(S["kn_norm"], 6)
                for qb in range(2):
                    pe.wait_ge(S["p_ready"], 2 * hh + qb + 1)
                    for kt in range(4):
                        last = nc.tensor.transpose(psx[:, kt // 2, (kt % 2) * LAT + qb * P:(kt % 2) * LAT + (qb + 1) * P],
                                                   park[:, 2 * (hh % 2) + qb, kt * P:(kt + 1) * P], ident)
                last.then_inc(S["pt_mm"], 1)

            scores(0)
            job_bcast(5)
            scores(1)
            transposes(0)
            for hh in range(AH):
                g = hh // (AH // AKV)
                if hh + 2 < AH:
                    scores(hh + 2)
                if hh:
                    pe.wait_ge(S["oT_lo"], hh)
                for kt in range(4):
                    pe.wait_ge(S["pt_lo"], 2 * hh + kt // 2 + 1)
                    vt = (kt % 2) * 256 + g * P
                    last = mm3(psx[:, 2, 0:LAT], a_hi[:, CH_GV + kt // 2, vt:vt + P], a_lo[:, CH_GV + kt // 2, vt:vt + P],
                               a_hi[:, CH_GP + kt // 2, (kt % 2) * LAT:(kt % 2 + 1) * LAT],
                               a_lo[:, CH_GP + kt // 2, (kt % 2) * LAT:(kt % 2 + 1) * LAT], kt == 0, kt == 3)
                last.then_inc(S["oT_mm"], 1)
                if hh + 1 < AH:
                    transposes(hh + 1)
            for i in range(4):
                j = i % 2
                wait_unit(U + 6 + i)
                whi = w_hi[:, j, :].rearrange("p (k c n) -> p k c n", k=KD, c=2)
                wlo = w_lo[:, j, :].rearrange("p (k c n) -> p k c n", k=KD, c=2)
                for k in range(KD):
                    pe.wait_ge(S["oT_lo"], k + 1)
                    src = (CH_GO + k // 2, (k % 2) * LAT)
                    for c in range(2):
                        last = mm3(pair[:, j, c, 0:LAT], whi[:, k, c], wlo[:, k, c],
                                   a_hi[:, src[0], src[1]:src[1] + LAT], a_lo[:, src[0], src[1]:src[1] + LAT],
                                   k == 0, k == KD - 1)
                last.then_inc(S["pe_unit"], 1)
            norm(S_NORM[(1, 2)], 2)
            ffn(1, 1, LAT)
            norm(S_FIN, 2)
            for d in range(KD):
                pe.wait_ge(S["fin_ready"], d + 1)
                for t in range(2):
                    last = nc.tensor.transpose(pair[:, t, d // 4, (d % 4) * P:(d % 4 + 1) * P],
                                               tmp[:, d % 2, t * P:(t + 1) * P], ident)
                last.then_inc(S["fin_tr"], 1)

        @block.scalar
        def _(act):
            fn = nc.scalar.activation

            def split_hi(base, it, off, mul=2, size=UNIT):
                slot = off % 2
                act.wait_ge(raw_landed[slot], it * (8 * mul) + 16 * ((base + off) // 2 + 1))
                v = it * mul + (base + off)
                if not isinstance(v, int) or v >= 2:
                    act.wait_ge(S["pe_unit"], v)
                fn(w_hi[:, slot, 0:size], raw[:, slot, 0:size], ACT.Copy).then_inc(S["hi_ready"], 1)

            def square_x(d, slot, ss, width, wait):
                if wait is not None:
                    act.wait_ge(S["pair_free"], wait)
                if not isinstance(ss, int) or ss or d >= 2:
                    act.wait_ge(S["ss_ready"], d + (ss - 1))
                fn(full[:, slot:slot + 1, 0:width], xT[:, bass.ds(d, 1), 0:width], ACT.Square).then_inc(S["x_sq"], 1)

            def norm(n, l, third, width, split=None, bank=ps_s):
                if split is not None:
                    split_hi(split - 1, 0, 1)
                act.wait_ge(S["st_sum"], n + 1)
                fn(sd[:, 0:width // P], bank[:, 8:8 + width // P], ACT.Sqrt, scale=1.0 / D, bias=EPS
                   ).then_inc(S["st_sqrt"], 1)
                if l is None:
                    return
                h0 = H0[(l, third)]
                q0 = (l * NMOD + 3 * third) * KD

                def affine(d):
                    act.wait_ge(S["t_ready"], h0 + d + 1)
                    if d >= 2:
                        act.wait_ge(S["h_ready"], h0 + d - 1)
                    for cond in range(width // 256):
                        cols = slice(cond * 256, (cond + 1) * 256)
                        last = fn(full[:, d % 2, cols], tmp[:, d % 2, cols], ACT.Identity,
                                  scale=aff[:, d, cond:cond + 1], bias=modT[:, q0 + d, cond:cond + 1])
                    last.then_inc(S["n_full"], 1)
                for d in range(KD):
                    affine(d)
                    act.wait_ge(S["n_full"], h0 + d + 1)
                    fn(h_hi[:, d, 0:width], full[:, d % 2, 0:width], ACT.Copy).then_inc(S["n_hi"], 1)

            def ffn(l, f, width):
                u = U_FFN[(l, f)]
                g = G_FFN[(l, f)]
                nc.scalar.preload_act_table(ACT.Silu)
                for half, rows in enumerate(HALVES):
                    with act.Fori(0, rows // 2) as it:
                        for j in range(2):
                            uu = u + 2 * it + j
                            gg = g + 2 * it + j
                            act.wait_ge(S["pe_unit"], uu + 2)
                            fn(tmp[:, j, 0:width], pair[:, j, 0, 0:width], ACT.Silu).then_inc(S["silu_ready"], 1)
                            act.wait_ge(S["u_ready"], gg + 1)
                            fn(a_hi[:, bass.ds(2 * it + j, 1), 0:width], full[:, j:j + 1, 0:width], ACT.Copy
                               ).then_inc(S["u_hi"], 1)
                            split_hi(u, it, j + 2)
                    u += rows
                    g += rows
                    last = (l, f, half) == (1, 1, 1)

                    def dbody(it, last_body=False):
                        for j in range(2):
                            if half and not (isinstance(it, int) and 2 * it + j == 0):
                                square_x(2 * it + (j - 1), (j + 1) % 2, SS0[(l, f)], width, u + 2 * it + (j + 2))
                            if half and last_body and j == 1:
                                square_x(KD - 1, 1, SS0[(l, f)], width, u + KD + 2)
                            elif not (last and last_body):
                                split_hi(u, it, j + 2, 2, UNIT if last_body else rows * P)
                    if half:
                        nc.scalar.preload_act_table(ACT.Sqrt)
                    dbody(0)
                    with act.Fori(1, KD // 2 - 1) as it:
                        dbody(it)
                    dbody(KD // 2 - 1, True)
                    u += KD

            act.wait_ge(S["vec_up"], 1)
            for cond, row in enumerate((ROW_C, ROW_CX)):
                last = fn(sT[:, :, cond], vecT[:, row:row + KD], ACT.Silu)
            last.then_inc(S["s_rdy"], 1)
            act.wait_ge(S["dec_mm"], 1)
            fn(lg[:, :], psx[:, 1, 0:2 * RH], ACT.Exp).then_inc(S["dec_exp"], 1)
            for d in range(KD):
                act.wait_ge(S["x_tr"], d + 1)
                if d % 4 == 0:
                    act.wait_ge(S[("pro_mm", "pro_acc")[d // 4]], 1)
                fn(xT[:, d, :], pair[:, (d % 4) // 2, d % 2], ACT.Copy).then_inc(S["x_up"], 1)
                if d:
                    act.wait_ge(S["x_up"], d)
                    square_x(d - 1, (d - 1) % 2, 0, N, None)
            act.wait_ge(S["x_up"], KD)
            square_x(KD - 1, 1, 0, N, None)
            split_hi(0, 0, 0)
            nc.scalar.preload_act_table(ACT.Sqrt)
            norm(0, 0, 0, N, 1, psx[:, 2])
            ffn(0, 0, N)
            norm(1, 0, 1, N, U_RET + 1)

            def retention(hd):
                U = U_RET + 8 * hd
                for j in range(8):
                    if j < 2:
                        ch, sc = (CH_Q, 1.0) if j == 0 else (CH_K, RDK ** -0.5)
                        act.wait_ge(S["pe_unit"], U + (j + 1) + 1)
                        fn(a_hi[:, ch:ch + 2, LAT:N], pair[:, j % 2, :, LAT:N], ACT.Copy, scale=sc
                           ).then_inc(S["q_ctx_hi"], 1)
                        act.wait_ge(S["rot_ready"], 2 * hd + (j + 1))
                        fn(a_hi[:, ch:ch + 2, 0:LAT], full[:, j, :].rearrange("p (c n) -> p c n", c=2), ACT.Copy, scale=sc
                           ).then_inc(S["q_lat_hi"], 1)
                    elif j < 4:
                        if j == 2:
                            act.wait_ge(S["e_pre"], 4 * hd + 4)
                            fn(o_buf[:, :, 0:BAND], o_buf[:, :, 0:BAND], ACT.Exp).then_inc(S["e_exp"], 1)
                        act.wait_ge(S["pe_unit"], U + (j + 1) + 1)
                        fn(a_hi[:, CH_V:CH_V + 4, (j - 2) * 256:(j - 1) * 256],
                           pair[:, j % 2, :, :].rearrange("p b (t n) -> p (b t) n", t=2), ACT.Copy
                           ).then_inc(S["v_hi"], 1)
                        if j == 3:
                            for g in range(3):
                                act.wait_ge(S["ms_ready"], 3 * hd + (g + 1))
                                fn(a_hi[:, CH_S + g, :], tmp[:, g % 2, :], ACT.Copy).then_inc(S["ms_hi"], 1)
                    elif j < 6:
                        if j == 5:
                            for e in range(4):
                                act.wait_ge(S["o_copied"], 4 * hd + (e + 1))
                                if e == 0:
                                    fn(ssum[:, :], o_buf[:, 0, :], ACT.Square).then_inc(S["o_sq"], 1)
                                    continue
                                if e == 3:
                                    act.wait_ge(S["o_sum"], 3 * hd + 1)
                                fn(full[:, e % 2, :], o_buf[:, e, :], ACT.Square).then_inc(S["o_sq"], 1)
                            act.wait_ge(S["st_sum"], S_RET + 1 + hd)
                            fn(sd[:, :], ps_s[:, 8:12], ACT.Sqrt, scale=1.0 / RDV, bias=EPS
                               ).then_inc(S["st_sqrt"], 1)
                            for e in range(2):
                                act.wait_ge(S["og_ready"], 4 * hd + (e + 1))
                                fn(a_hi[:, e, :], tmp[:, e % 2, :], ACT.Copy).then_inc(S["og_hi"], 1)
                        act.wait_ge(S["pe_unit"], U + (j + 1) + 1)
                        fn(sg_buf[:, 2 * (j - 4):2 * (j - 3), :], pair[:, j % 2, :, :], ACT.Silu
                           ).then_inc(S["sg_ready"], 1)
                        if j == 5:
                            for e in range(2, 4):
                                act.wait_ge(S["og_ready"], 4 * hd + (e + 1))
                                fn(a_hi[:, e, :], tmp[:, e % 2, :], ACT.Copy).then_inc(S["og_hi"], 1)
                    elif j == 7:
                        for d in range(4):
                            square_x(d, d % 2, 4 * hd + SS_RET, N, U + 9)
                    split_hi(U_RET, hd, j + 2, 8)

            with act.Fori(0, RH) as hd:
                retention(hd)
            for d in range(4, KD):
                square_x(d, d % 2, SS_RET + 4 * (RH - 1), N, U_RET + 8 * RH + 2)
            norm(S_NORM[(0, 2)], 0, 2, N)
            ffn(0, 1, N)
            norm(S_NORM[(1, 0)], 1, 0, N, U_FFN[(1, 0)] + 1)
            ffn(1, 0, N)
            norm(S_NORM[(1, 1)], 1, 1, N, U_GQA + 1)

            U = U_GQA

            def job_square(job):
                if job >= 2:
                    act.wait_ge(S["st_sum"], S_GQA + job - 1)
                fn((sq if job % 2 else ssum)[:, :], park[:, job, :], ACT.Square).then_inc(S["g_sq"], 1)

            def root(job):
                act.wait_ge(S["st_sum"], S_GQA + job + 1)
                act.wait_ge(S["st_diag"], S_GQA + job)
                fn(sd[:, :], ps_s[:, 8:12], ACT.Sqrt, scale=1.0 / AHD, bias=EPS).then_inc(S["st_sqrt"], 1)

            def job_swap(job):
                w = (1 if job < 2 else 2) * LAT
                act.wait_ge(S["kn_norm"], job + 1)
                fn(tmp[0:P // 2, 0, 0:w], full[P // 2:P, job % 2, 0:w], ACT.Copy)
                fn(tmp[P // 2:P, 0, 0:w], full[0:P // 2, job % 2, 0:w], ACT.Copy).then_inc(S["kn_swap"], 1)

            def job_hi(job):
                act.wait_ge(S["kn_ready"], job + 1)
                fn(a_hi[:, job if job < 2 else CH_GQ + job - 2, :], full[:, job % 2, :], ACT.Copy
                   ).then_inc(S["kn_hi"], 1)
            act.wait_ge(S["pe_unit"], U + 2)
            fn(park[:, 0:2, :], pair[:, 0, :, :], ACT.Copy).then_inc(S["pair_free"], 1)
            act.wait_ge(S["pair_free"], U + 3)
            job_square(0)
            job_square(1)
            split_hi(U, 0, 2)
            root(0)
            root(1)
            for job in range(2):
                job_swap(job)
                job_hi(job)
            act.wait_ge(S["pe_unit"], U + 3)
            fn(a_hi[:, CH_GV:CH_GV + 2, :], pair[:, 1, :, :], ACT.Copy).then_inc(S["gv_hi"], 1)
            split_hi(U, 0, 3)
            act.wait_ge(S["pair_free"], U + 4)
            for i in range(4):
                job = 2 + i
                act.wait_ge(S["pe_unit"], U + 3 + i + 1)
                fn(park[:, job, :].rearrange("p (c n) -> p c n", c=2), pair[:, i % 2, :, 0:LAT], ACT.Copy
                   ).then_inc(S["pair_free"], 1)
                act.wait_ge(S["pair_free"], U + 5 + i)
                job_square(job)
                if i:
                    job_swap(job - 1)
                split_hi(U, 0, 4 + i)
                root(job)
                if i:
                    job_hi(job - 1)

            def probs(hh, qb):
                act.wait_ge(S["nb_ready"], hh + 1)
                n = 2 * hh + qb
                fn(park[:, 2 * (hh % 2) + qb, :], pair[:, hh % 2, qb], ACT.Exp, bias=snb[:, n:n + 1],
                   scale=AHD ** -0.5, accum_out=sden[:, n:n + 1]).then_inc(S["p_exp"], 1)
            def scale(hh):
                act.wait_ge(S["inv_ready"], hh + 1)
                for qb in range(2):
                    n = 2 * hh + qb
                    pb = park[:, 2 * (hh % 2) + qb, :]
                    fn(pb, pb, ACT.Copy, scale=sinv[:, n:n + 1]).then_inc(S["p_ready"], 1)
            probs(0, 0)
            probs(0, 1)
            probs(1, 0)
            probs(1, 1)
            scale(0)
            job_swap(5)
            job_hi(5)
            for hh in range(AH):
                act.wait_ge(S["pt_mm"], hh + 1)
                for b in range(2):
                    fn(a_hi[:, CH_GP + b, :], psx[:, b], ACT.Copy).then_inc(S["pt_hi"], 1)
                if hh + 1 < AH:
                    scale(hh + 1)
                act.wait_ge(S["oT_mm"], hh + 1)
                fn(a_hi[:, CH_GO + hh // 2, (hh % 2) * LAT:(hh % 2 + 1) * LAT], psx[:, 2, 0:LAT], ACT.Copy
                   ).then_inc(S["oT_hi"], 1)
                if hh + 2 < AH:
                    probs(hh + 2, 0)
                    probs(hh + 2, 1)
            nc.scalar.preload_act_table(ACT.Sqrt)
            for i in range(4):
                if i < 3:
                    split_hi(U, 0, 8 + i)
                for d in (2 * i, 2 * i + 1):
                    square_x(d, d % 2, SS_GQA, LAT, U + 9 + i)
            norm(S_NORM[(1, 2)], 1, 2, LAT, U_FFN[(1, 1)] + 1)
            ffn(1, 1, LAT)
            norm(S_FIN, None, 0, LAT)

        @block.vector
        def _(dve):
            V = nc.vector
            step = Steps(S["dve_step"])

            def after(value):
                dve.wait_ge(S["dve_step"], value)

            def split_lo(v, slot, size=UNIT):
                dve.wait_ge(S["hi_ready"], v + 1)
                V.tensor_tensor(w_lo[:, slot, 0:size], raw[:, slot, 0:size], f32(w_hi[:, slot, 0:size]), ALU.subtract
                                ).then_inc(S["lo_ready"], 1)

            def ada_sum(a, half):
                w = ada[:, :].rearrange("p (k n) -> p k n", k=KD)
                dve.wait_ge(ada_landed[half], (a - (ADA_PRO - 1)) * 16)
                if half:
                    dve.wait_ge(S["acc_half"], a - (ADA_PRO - 1))
                ready = {}
                for k in range(half * KD // 2, (half + 1) * KD // 2):
                    for cond in range(2):
                        s = sT[:, k, cond:cond + 1]
                        if k == 0:
                            ins = V.tensor_scalar(acc[:, cond, :], w[:, k], s, None, ALU.mult)
                        else:
                            if k % (KD // 2):
                                after(ready[cond])
                            ins = V.scalar_tensor_tensor(out=acc[:, cond, :], in0=w[:, k], scalar=s,
                                                         in1=acc[:, cond, :], op0=ALU.mult, op1=ALU.add)
                        if (k + 1) % (KD // 2) == 0 and cond == 1:
                            ins.then_inc(S[("acc_half", "acc_ready")[half]], 1)
                        else:
                            ready[cond] = step.mark(ins)

            def ada_end(a):
                ada_out(a)
                if not (isinstance(a, int) and a == DEPTH * ADA_L - 1):
                    ada_sum(a + 1, 0)

            def ada_out(a):
                dve.wait_ge(S["ada_mm"], a - (ADA_PRO - 1))
                V.tensor_tensor(modT[:, bass.ds(2 * a, 2), :], ps_s[:, 0:4].rearrange("p (c o) -> p c o", o=2),
                                vecT[:, bass.ds(2 * a, 2)].unsqueeze(2).to_broadcast([P, 2, 2]), ALU.add
                                ).then_inc(S["mod_ready"], 1)
            ADA_STEPS = 2 * KD - 2

            def zero_sums():
                after(step.mark(V.memset(ssum[:, :], 0.0)))

            def add_square(d, slot, ss, width):
                dve.wait_ge(S["x_sq"], d + (ss + 1))
                if not isinstance(ss, int) or ss or d:
                    dve.wait_ge(S["ss_ready"], d + ss)
                V.tensor_tensor(ssum[:, 0:width], ssum[:, 0:width], full[:, slot, 0:width], ALU.add
                                ).then_inc(S["ss_ready"], 1)

            def norm_rstd(n, width, dst=diag):
                tiles = width // P
                dve.wait_ge(S["st_sqrt"], n + 1)
                r = step.mark(V.reciprocal(rs[:, 0:tiles], sd[:, 0:tiles]))
                after(r)
                for t in range(tiles):
                    last = V.tensor_scalar(dst[:, t * P:(t + 1) * P], ident, rs[:, t:t + 1], None, ALU.mult)
                last.then_inc(S["st_diag"], 1)

            def norm(n, l, third, width, split=None):
                g0 = ROW_NG + (3 * l + third) * KD
                q0 = (l * NMOD + 3 * third) * KD
                if MODS_NORM[(l, third)]:
                    dve.wait_ge(S["mod_ready"], MODS_NORM[(l, third)])
                V.scalar_tensor_tensor(out=aff[:, :, :], in0=modT[:, q0 + KD:q0 + 2 * KD, :], scalar=1.0,
                                       in1=vecT[:, g0:g0 + KD].unsqueeze(2).to_broadcast([P, KD, 2]),
                                       op0=ALU.add, op1=ALU.mult)
                if n:
                    norm_rstd(n, width)
                if split is not None:
                    split_lo(split, 1)
                dve.wait_ge(S["st_bcast"], n + 1)
                h0 = H0[(l, third)]

                def t(d):
                    V.tensor_tensor(tmp[:, d % 2, 0:width], xT[:, d, 0:width], psx[:, 1, 0:width], ALU.mult
                                    ).then_inc(S["t_ready"], 1)
                t(0)
                t(1)
                for d in range(KD):
                    if d + 2 < KD:
                        dve.wait_ge(S["n_full"], h0 + d + 1)
                        t(d + 2)
                    dve.wait_ge(S["n_hi"], h0 + d + 1)
                    V.tensor_tensor(h_lo[:, d, 0:width], full[:, d % 2, 0:width], f32(h_hi[:, d, 0:width]), ALU.subtract
                                    ).then_inc(S["h_ready"], 1)
                dve.wait_ge(S["h_ready"], h0 + KD)

            def gates(l, m, factor):
                q = (l * NMOD + m) * KD
                after(step.mark(V.tensor_scalar(gate[:, :, :], modT[:, q:q + KD, :], factor, None, ALU.mult)))

            def add_x(d, src, width, done):
                dd = bass.ds(d, 1)
                for cond in range(width // 256):
                    cols = slice(cond * 256, (cond + 1) * 256)
                    ins = V.scalar_tensor_tensor(out=xT[:, dd, cols], in0=src[:, cols].unsqueeze(1),
                                                 scalar=gate[:, dd, cond], in1=xT[:, dd, cols],
                                                 op0=ALU.mult, op1=ALU.add)
                if done:
                    ins.then_inc(S["pair_free"], 1)

            def ffn(l, f, width):
                u = U_FFN[(l, f)]
                g = G_FFN[(l, f)]
                for half, rows in enumerate(HALVES):
                    def body(it, a0):
                        for j in range(2):
                            uu = u + 2 * it + j
                            gg = g + 2 * it + j
                            if a0 is not None:
                                ada_sum(2 * it + (a0 + j), 1)
                            dve.wait_ge(S["silu_ready"], gg + 1)
                            V.tensor_tensor(full[:, j, 0:width], tmp[:, j, 0:width], pair[:, j, 1, 0:width], ALU.mult
                                            ).then_inc(S["u_ready"], 1)
                            dve.wait_ge(S["u_hi"], gg + 1)
                            dve.wait_ge(S["u_ready"], gg + 1)
                            cc = bass.ds(2 * it + j, 1)
                            V.tensor_tensor(a_lo[:, cc, 0:width], full[:, j:j + 1, 0:width],
                                            f32(a_hi[:, cc, 0:width]), ALU.subtract).then_inc(S["pair_free"], 1)
                            if a0 is not None:
                                ada_end(2 * it + (a0 + j))
                            split_lo(uu + 2, j)
                    for lo, hi, a0 in bodies(u, rows // 2):
                        if a0 is not None and a0 + 2 * lo == ADA_PRO:
                            ada_sum(ADA_PRO, 0)
                        if hi == lo + 1:
                            body(lo, a0)
                            continue
                        with dve.Fori(lo, hi) as it:
                            step.enter(it - lo if lo else it, 0 if a0 is None else 2 * ADA_STEPS)
                            body(it, a0)
                        step.leave(hi - lo)
                    u += rows
                    g += rows
                    if half == 0:
                        dve.wait_ge(S["mod_ready"], MODS_AT[(l, f)])
                        gates(l, 6 * f + 2, 0.5)
                    else:
                        zero_sums()

                    def dbody(it, a0, last_body=False):
                        for j in range(2):
                            uu = u + 2 * it + j
                            if a0 is not None:
                                ada_sum(2 * it + (a0 + j), 1)
                            if half and not (isinstance(it, int) and 2 * it + j == 0):
                                add_square(2 * it + (j - 1), (j + 1) % 2, SS0[(l, f)], width)
                            dve.wait_ge(S["pe_unit"], uu + 2)
                            add_x(2 * it + j, pair[:, j, 0], width, True)
                            if a0 is not None:
                                ada_end(2 * it + (a0 + j))
                            if half and last_body and j == 1:
                                add_square(KD - 1, 1, SS0[(l, f)], width)
                            elif not (last and last_body):
                                split_lo(uu + 2, j, UNIT if last_body else rows * P)
                    last = (l, f, half) == (1, 1, 1)
                    for lo, hi, a0 in bodies(u, KD // 2):
                        if lo == 0:
                            dbody(0, a0)
                            lo = 1
                        if min(hi, KD // 2 - 1) > lo:
                            with dve.Fori(lo, min(hi, KD // 2 - 1)) as it:
                                step.enter(it - lo, 0 if a0 is None else 2 * ADA_STEPS)
                                dbody(it, a0)
                            step.leave(min(hi, KD // 2 - 1) - lo)
                        if hi == KD // 2:
                            dbody(KD // 2 - 1, a0, True)
                    u += KD

            dve.wait_ge(S["vec_tr"], 1)
            V.tensor_copy(vecT[:, :], psx[:, 0, 0:ROWS]).then_inc(S["vec_up"], 1)
            zero_sums()

            def pro_sum(i):
                a = ADA_PRO - 4 + i
                w = pro_slot[a].rearrange("p (k n) -> p k n", k=KD)
                dve.wait_ge(pro_landed[a], 16)
                ready = {}
                for k in range(KD):
                    for cond in range(2):
                        s = sT[:, k, cond:cond + 1]
                        if k == 0:
                            ins = V.tensor_scalar(pro_acc[i][:, cond, :], w[:, k], s, None, ALU.mult)
                        else:
                            after(ready[cond])
                            ins = V.scalar_tensor_tensor(out=pro_acc[i][:, cond, :], in0=w[:, k], scalar=s,
                                                         in1=pro_acc[i][:, cond, :], op0=ALU.mult, op1=ALU.add)
                        if k == KD - 1 and cond == 1:
                            ins.then_inc(S["pro_acc"], 1)
                        else:
                            ready[cond] = step.mark(ins)
            dve.wait_ge(S["s_rdy"], 1)
            for i in range(3):
                pro_sum(i)
            dve.wait_ge(S["dec_exp"], 1)
            V.tensor_scalar(lg[:, :], lg[:, :], -1.0, None, ALU.mult).then_inc(S["pair_free"], 2)
            for d in range(KD):
                add_square(d, d % 2, 0, N)
            pro_sum(3)
            norm_rstd(0, N)
            split_lo(0, 0)
            dve.wait_ge(S["pro_mm"], 5)
            dve.wait_ge(S["vec_up"], 1)
            V.tensor_tensor(modT[:, 0:2 * ADA_PRO, :], ps_s[:, 16:16 + 4 * ADA_PRO].rearrange("p (q o) -> p q o", o=2),
                            vecT[:, 0:2 * ADA_PRO].unsqueeze(2).to_broadcast([P, 2 * ADA_PRO, 2]), ALU.add
                            ).then_inc(S["mod_up"], 1)
            dve.wait_ge(S["mod_up"], 1)
            norm(0, 0, 0, N)
            split_lo(1, 1)
            ffn(0, 0, N)
            norm(1, 0, 1, N, U_RET + 1)

            gates(0, 5, 1.0)

            def add_o_square(hd, e):
                dve.wait_ge(S["o_sq"], 4 * hd + (e + 1))
                if e > 1:
                    dve.wait_ge(S["o_sum"], 3 * hd + (e - 1))
                V.tensor_tensor(ssum[:, :], ssum[:, :], full[:, e % 2, :], ALU.add).then_inc(S["o_sum"], 1)

            def retention(hd):
                U = U_RET + 8 * hd
                for j in range(8):
                    p = j % 2
                    if j < 2:
                        ch, sc = (CH_Q, 1.0) if j == 0 else (CH_K, RDK ** -0.5)
                        dve.wait_ge(S["q_ctx_hi"], 2 * hd + (j + 1))
                        x1, x2 = pair[:, p, 0, 0:LAT], pair[:, p, 1, 0:LAT]
                        V.tensor_tensor(tmp[:, 0, 0:LAT], x1, rcos, ALU.mult)
                        step.mark(V.tensor_tensor(tmp[:, 0, LAT:N], x2, rsin, ALU.mult))
                        V.tensor_tensor(tmp[:, 1, 0:LAT], x2, rcos, ALU.mult)
                        v = step.mark(V.tensor_tensor(tmp[:, 1, LAT:N], x1, rsin, ALU.mult))
                        after(v - 1)
                        V.tensor_tensor(full[:, j, 0:LAT], tmp[:, 0, 0:LAT], tmp[:, 0, LAT:N], ALU.subtract)
                        after(v)
                        V.tensor_tensor(full[:, j, LAT:N], tmp[:, 1, 0:LAT], tmp[:, 1, LAT:N], ALU.add
                                        ).then_inc(S["rot_ready"], 1)
                        for cols, src, name in ((slice(LAT, N), pair[:, p, :, LAT:N], "q_ctx_hi"),
                                                (slice(0, LAT), full[:, j, :].rearrange("p (c n) -> p c n", c=2), "q_lat_hi")):
                            dve.wait_ge(S[name], 2 * hd + (j + 1))
                            dve.wait_ge(S["rot_ready"], 2 * hd + (j + 1))
                            ins = V.scalar_tensor_tensor(out=a_lo[:, ch:ch + 2, cols], in0=src, scalar=sc,
                                                         in1=f32(a_hi[:, ch:ch + 2, cols]), op0=ALU.mult,
                                                         op1=ALU.subtract)
                        ins.then_inc(S["pair_free"], 1)
                    elif j < 4:
                        if j == 2:
                            lf, lb = lg[:, bass.ds(hd, 1)], lg[:, bass.ds(hd + RH, 1)]
                            V.tensor_scalar(o_buf[:, 0, 0:BAND], diff, 0.0, lf, ALU.max, ALU.mult).then_inc(S["e_pre"], 1)
                            V.tensor_scalar(tmp[:, 0, 0:BAND], diff, -1.0, 0.0, ALU.mult, ALU.max)
                            v = step.mark(V.tensor_scalar(tmp[:, 1, 0:BAND], diff, -1.0, float(LAT), ALU.mult, ALU.add))
                            V.tensor_scalar(o_buf[:, 2, 0:BAND], diff, float(LAT), lf, ALU.add, ALU.mult).then_inc(S["e_pre"], 1)
                            after(v)
                            V.tensor_scalar(o_buf[:, 1, 0:BAND], tmp[:, 0, 0:BAND], lb, None, ALU.mult).then_inc(S["e_pre"], 1)
                            V.tensor_scalar(o_buf[:, 3, 0:BAND], tmp[:, 1, 0:BAND], lb, None, ALU.mult).then_inc(S["e_pre"], 1)
                            dve.wait_ge(S["e_exp"], hd + 1)
                            dve.wait_ge(S["e_pre"], 4 * hd + 4)
                            V.scalar_tensor_tensor(out=tmp[:, 0, 0:BAND], in0=diff, scalar=0.0, in1=o_buf[:, 0, 0:BAND],
                                                   op0=ALU.is_ge, op1=ALU.mult)
                            v = step.mark(V.scalar_tensor_tensor(out=tmp[:, 1, 0:BAND], in0=diff, scalar=0.0,
                                                                 in1=o_buf[:, 1, 0:BAND], op0=ALU.is_le, op1=ALU.mult))
                            V.tensor_tensor(band[:, 1, :], o_buf[:, 2, 0:BAND], o_buf[:, 3, 0:BAND], ALU.add)
                            after(v)
                            step.mark(V.tensor_tensor(band[:, 0, :], tmp[:, 0, 0:BAND], tmp[:, 1, 0:BAND], ALU.add))
                        dve.wait_ge(S["v_hi"], 2 * hd + (j - 1))
                        cols = slice((j - 2) * 256, (j - 1) * 256)
                        V.tensor_tensor(a_lo[:, CH_V:CH_V + 4, cols],
                                        pair[:, p, :, :].rearrange("p b (t n) -> p (b t) n", t=2),
                                        f32(a_hi[:, CH_V:CH_V + 4, cols]), ALU.subtract).then_inc(S["pair_free"], 1)
                        if j == 3:
                            after(step.last())
                            near, far = band[:, 0], band[:, 1]
                            lo_, hi_ = slice(P, BAND), slice(0, LAT)

                            def masked(g):
                                dve.wait_ge(S["s_mm"], 3 * hd + (g + 1))
                                m0, m1 = ((far[:, lo_], near[:, lo_]), (far[:, hi_], near[:, hi_]),
                                          (near[:, lo_], near[:, hi_]))[g]
                                V.tensor_tensor(tmp[:, g % 2, 0:LAT], psx[:, g, 0:LAT], m0, ALU.mult)
                                V.tensor_tensor(tmp[:, g % 2, LAT:N], psx[:, g, LAT:N], m1, ALU.mult
                                                ).then_inc(S["ms_ready"], 1)

                            def masked_lo(g):
                                dve.wait_ge(S["ms_hi"], 3 * hd + (g + 1))
                                dve.wait_ge(S["ms_ready"], 3 * hd + (g + 1))
                                V.tensor_tensor(a_lo[:, CH_S + g, :], tmp[:, g % 2, :], f32(a_hi[:, CH_S + g, :]),
                                                ALU.subtract).then_inc(S["s_split"], 1)
                            masked(0)
                            masked(1)
                            masked_lo(0)
                            dve.wait_ge(S["s_split"], 3 * hd + 1)
                            masked(2)
                            masked_lo(1)
                            masked_lo(2)
                    elif j == 4:
                        dve.wait_ge(S["sg_ready"], 2 * hd + 1)
                        V.memset(mark[:, :], 0.0).then_inc(S["pair_free"], 1)
                    elif j == 5:
                        for e in range(4):
                            dve.wait_ge(S["o_mm"], 4 * hd + (e + 1))
                            V.tensor_copy(o_buf[:, e, :], psx[:, e % 3]).then_inc(S["o_copied"], 1)
                            if e >= 2:
                                add_o_square(hd, e - 1)
                        add_o_square(hd, 3)
                        dve.wait_ge(S["o_copied"], 4 * hd + 4)
                        for e in range(2):
                            v = step.mark(V.tensor_tensor(o_buf[:, e, :], o_buf[:, e, :], sg_buf[:, e, :], ALU.mult))
                        norm_rstd(S_RET + hd, N)
                        after(v)
                        dve.wait_ge(S["st_bcast"], S_RET + 1 + hd)

                        def og(e):
                            V.tensor_tensor(tmp[:, e % 2, :], o_buf[:, e, :],
                                            psx[:, 1] if e < 2 else sg_buf[:, e, :], ALU.mult
                                            ).then_inc(S["og_ready"], 1)

                        def og_lo(e):
                            dve.wait_ge(S["og_hi"], 4 * hd + (e + 1))
                            dve.wait_ge(S["og_ready"], 4 * hd + (e + 1))
                            V.tensor_tensor(a_lo[:, e, :], tmp[:, e % 2, :], f32(a_hi[:, e, :]), ALU.subtract
                                            ).then_inc(S["og_lo"], 1)
                        og(0)
                        og(1)
                        for e in range(2, 4):
                            v = step.mark(V.tensor_tensor(o_buf[:, e, :], o_buf[:, e, :], psx[:, 1], ALU.mult))
                        og_lo(0)
                        og_lo(1)
                        dve.wait_ge(S["sg_ready"], 2 * hd + 2)
                        V.memset(mark[:, :], 0.0).then_inc(S["pair_free"], 1)
                        after(v)
                        dve.wait_ge(S["og_lo"], 4 * hd + 2)
                        og(2)
                        og(3)
                        og_lo(2)
                        og_lo(3)
                    else:
                        if j == 7:
                            zero_sums()
                            for d in range(4):
                                add_square(d, d % 2, 4 * hd + SS_RET, N)
                        dve.wait_ge(S["pe_unit"], U + (j + 1) + 1)
                        for i in range(4):
                            src = (pair[:, p, 0], pair[:, p, 1], psx[:, 0], psx[:, 2])[i]
                            add_x((j - 6) * 4 + i, src, N, i == 3)
                    split_lo(U + (j + 2), j % 2)

            RET_STEPS = 2 * 2 + 3 + 1 + 4 + 1
            with dve.Fori(0, RH) as hd:
                step.enter(hd, RET_STEPS)
                retention(hd)
            step.leave(RH)
            for d in range(4, KD):
                add_square(d, d % 2, SS_RET + 4 * (RH - 1), N)
            norm(S_NORM[(0, 2)], 0, 2, N)
            ffn(0, 1, N)
            norm(S_NORM[(1, 0)], 1, 0, N, U_FFN[(1, 0)] + 1)
            ffn(1, 0, N)
            norm(S_NORM[(1, 1)], 1, 1, N, U_GQA + 1)

            U = U_GQA

            def job_rstd(job):
                norm_rstd(S_GQA + job, N, job_diag[job % 2])

            def job_lo(job):
                ch = job if job < 2 else CH_GQ + job - 2
                dve.wait_ge(S["kn_hi"], job + 1)
                dve.wait_ge(S["kn_ready"], job + 1)
                V.tensor_tensor(a_lo[:, ch, :], full[:, job % 2, :], f32(a_hi[:, ch, :]), ALU.subtract
                                ).then_inc(S["kn_lo"], 1)

            def job_rotate(job):
                gain, halves = (ROW_KG, 1) if job < 2 else (ROW_QG, 2)
                buf, sin_part = full[:, job % 2, :], ada[:, 0:N]
                if job >= 2:
                    dve.wait_ge(S["kn_lo"], job - 1)
                dve.wait_ge(S["st_bcast"], S_GQA + job + 1)
                V.scalar_tensor_tensor(out=buf, in0=park[:, job, :], scalar=vecT[:, gain:gain + 1],
                                       in1=psx[:, job % 2, :], op0=ALU.mult, op1=ALU.mult).then_inc(S["kn_norm"], 1)
                dve.wait_ge(S["kn_norm"], job + 1)
                if job:
                    dve.wait_ge(S["kn_ready"], job)
                for c in range(halves):
                    cs = slice(c * LAT, (c + 1) * LAT)
                    step.mark(V.tensor_tensor(tmp[:, 1, cs], buf[:, cs], acos, ALU.mult))
                if job:
                    job_lo(job - 1)
                dve.wait_ge(S["kn_swap"], job + 1)
                for c in range(halves):
                    cs = slice(c * LAT, (c + 1) * LAT)
                    v = step.mark(V.tensor_tensor(sin_part[:, cs], tmp[:, 0, cs], asin, ALU.mult))
                after(v)
                w = halves * LAT
                V.tensor_tensor(buf[:, 0:w], tmp[:, 1, 0:w], sin_part[:, 0:w], ALU.add).then_inc(S["kn_ready"], 1)

            split_lo(U + 2, 0)
            job_rstd(0)
            job_rstd(1)
            job_rotate(0)
            job_rotate(1)
            dve.wait_ge(S["gv_hi"], 1)
            V.tensor_tensor(a_lo[:, CH_GV:CH_GV + 2, :], pair[:, 1, :, :], f32(a_hi[:, CH_GV:CH_GV + 2, :]), ALU.subtract
                            ).then_inc(S["pair_free"], 1)
            split_lo(U + 3, 1)
            for i in range(4):
                if i:
                    job_rotate(1 + i)
                job_rstd(2 + i)
                split_lo(U + 4 + i, i % 2)

            def peak(hh):
                dve.wait_ge(S["sc_mm"], 2 * hh + 2)
                n = slice(2 * hh, 2 * hh + 2)
                v = step.mark(V.reduce_max(smx[:, n], pair[:, hh % 2, :, :], AX_X))
                after(v)
                V.tensor_scalar(snb[:, n], smx[:, n], -AHD ** -0.5, None, ALU.mult).then_inc(S["nb_ready"], 1)
            def sums(hh):
                dve.wait_ge(S["p_exp"], 2 * hh + 2)
                n = slice(2 * hh, 2 * hh + 2)
                V.reciprocal(sinv[:, n], sden[:, n]).then_inc(S["inv_ready"], 1)
            peak(0)
            peak(1)
            sums(0)
            job_rotate(5)
            job_lo(5)
            sums(1)
            for hh in range(AH):
                for b in range(2):
                    dve.wait_ge(S["pt_hi"], 2 * hh + b + 1)
                    V.tensor_tensor(a_lo[:, CH_GP + b, :], psx[:, b], f32(a_hi[:, CH_GP + b, :]), ALU.subtract
                                    ).then_inc(S["pt_lo"], 1)
                if hh + 2 < AH:
                    peak(hh + 2)
                dve.wait_ge(S["oT_hi"], hh + 1)
                cs = slice((hh % 2) * LAT, (hh % 2 + 1) * LAT)
                V.tensor_tensor(a_lo[:, CH_GO + hh // 2, cs], psx[:, 2, 0:LAT], f32(a_hi[:, CH_GO + hh // 2, cs]),
                                ALU.subtract).then_inc(S["oT_lo"], 1)
                if hh + 2 < AH:
                    sums(hh + 2)
            gates(1, 5, 1.0)
            zero_sums()
            for i in range(4):
                if i:
                    split_lo(U + 7 + i, (i + 1) % 2)
                    for d in (2 * i - 2, 2 * i - 1):
                        add_square(d, d % 2, SS_GQA, LAT)
                dve.wait_ge(S["pe_unit"], U + 7 + i + 1)
                for c in range(2):
                    add_x(2 * i + c, pair[:, i % 2, c], LAT, c == 1)
            for d in (KD - 2, KD - 1):
                add_square(d, d % 2, SS_GQA, LAT)
            norm(S_NORM[(1, 2)], 1, 2, LAT, U_FFN[(1, 1)] + 1)
            ffn(1, 1, LAT)
            norm_rstd(S_FIN, LAT)
            dve.wait_ge(S["st_bcast"], S_FIN + 1)
            for d in range(KD):
                if d >= 2:
                    dve.wait_ge(S["fin_tr"], d - 1)
                V.scalar_tensor_tensor(out=tmp[:, d % 2, 0:LAT], in0=xT[:, d, 0:LAT], scalar=vecT[:, ROW_FG + d:ROW_FG + d + 1],
                                       in1=psx[:, 1, 0:LAT], op0=ALU.mult, op1=ALU.mult).then_inc(S["fin_ready"], 1)
            dve.wait_ge(S["fin_tr"], KD)
            for t in range(2):
                V.tensor_copy(park[:, 2 * t:2 * t + 2, :], pair[:, t, :, :]).then_inc(S["fin_copied"], 1)


NSS = {0: 8, 1: 16, 6: 36, 7: 44, 8: 52, 15: 60, 16: 68}
H0 = {(0, 0): 0, (0, 1): 8, (0, 2): 16, (1, 0): 24, (1, 1): 32, (1, 2): 40}
SS0 = {(0, 0): 8, (0, 1): 36, (1, 0): 44, (1, 1): 60}
SS_RET, SS_GQA = 16, 52
MODS_NORM = {(0, 0): 0, (0, 1): 24, (0, 2): 24, (1, 0): 44, (1, 1): 64, (1, 2): 64}
MODS_AT = {(0, 0): 10, (0, 1): 34, (1, 0): 54, (1, 1): 64}




def packed_units(w1, w2, ret_in, ret_out, qkv, wo):
    import numpy as np

    units = np.zeros((U_END, P, UNIT), np.float32)

    def put(u, block):
        units[u, :, :block.shape[0] * block.shape[2]] = block.transpose(1, 0, 2).reshape(P, -1)

    for (l, f), u in U_FFN.items():
        up = w1[l, f].reshape(KD, P, 2, FFN // P, P)
        down = w2[l, f].reshape(FFN // P, P, KD, P)
        r0 = 0
        for rows in HALVES:
            for r in range(rows):
                units[u + r] = up[:, :, :, r0 + r].transpose(1, 2, 0, 3).reshape(P, UNIT)
            for d in range(KD):
                put(u + rows + d, down[r0:r0 + rows, :, d])
            u, r0 = u + rows + KD, r0 + rows
    win = ret_in.reshape(KD, P, -1)
    wout = ret_out.reshape(-1, P, D)
    for hd in range(RH):
        cols = (RDK * hd, D + RDK * hd, 2 * D + RDV * hd, 2 * D + RDV * hd + 256,
                4 * D + RDV * hd, 4 * D + RDV * hd + 256)
        for j, c in enumerate(cols):
            put(U_RET + 8 * hd + j, win[:, :, c:c + 256])
        for j in range(2):
            put(U_RET + 8 * hd + 6 + j, wout[4 * hd:4 * hd + 4, :, j * 512:(j + 1) * 512])
    for j, c in enumerate((D, D + 256, 0, 256, 512, 768)):
        put(U_GQA + j, qkv.reshape(KD, P, -1)[:, :, c:c + 256])
    for j in range(4):
        put(U_GQA + 6 + j, wo.reshape(KD, P, D)[:, :, j * 256:(j + 1) * 256])
    return units


def shape_constants():
    import numpy as np

    f = np.float32
    t = np.arange(LAT).astype(f)
    half = RDK // 2
    freq = (f(10000.0) ** (-np.arange(half, dtype=f) / f(half))).astype(f)
    ang = (freq[:, None] * t[None]).astype(f)
    quarter = AHD // 4
    qf = (f(10000.0) ** (-np.arange(quarter, dtype=f) / f(quarter))).astype(f)
    row, col = (np.arange(LAT) // 64).astype(f), (np.arange(LAT) % 64).astype(f)
    ax = np.concatenate([qf[:, None] * row[None], qf[:, None] * col[None]]).astype(f)
    sin = np.sin(ax.astype(np.float64))
    parts = [np.eye(P), np.ones((P, P)), np.arange(BAND)[None] - P - np.arange(P)[:, None],
             np.cos(ang.astype(np.float64)), np.sin(ang.astype(np.float64)),
             np.tile(np.cos(ax.astype(np.float64)), (2, 1)), np.concatenate([-sin, sin])]
    return np.concatenate(parts, axis=1).astype(f)


def kernel(**inputs):
    import numpy as np
    import concourse.bacc as bacc
    from concourse.bass_utils import run_bass_kernel_spmd

    i = {k: np.asarray(v) for k, v in inputs.items()}
    arrays = {
        "x": i["x"][0], "ctx": i["ctx"][0],
        "vecs": np.concatenate([i[n].reshape(-1, P) for n in
                                ("ada_b", "norm_g", "final_g", "c", "c_ctx", "att_q_gain", "att_k_gain")]),
        "dec": np.concatenate([i["ret_decay_f"], i["ret_decay_b"]], axis=1),
        "consts": shape_constants(),
        "ada_w": i["ada_w"].reshape(DEPTH, KD, P, ADA_L, ADA).transpose(0, 3, 2, 1, 4).reshape(-1, P, UNIT),
        "units": packed_units(i["ffn_w1"], i["ffn_w2"], i["ret_w_in"][0], i["ret_w_out"][0],
                              i["att_w_qkv"][0], i["att_w_o"][0]),
    }
    arrays = {f"in_{k}": np.ascontiguousarray(v) for k, v in arrays.items()}
    nc = bacc.Bacc("TRN2", target_bir_lowering=False, num_devices=1)
    args = [nc.dram_tensor(k, a.shape, mybir.dt.from_np(a.dtype), kind="ExternalInput").ap() for k, a in arrays.items()]
    out = nc.dram_tensor("out", (LAT, D), F32, kind="ExternalOutput").ap()
    build(nc, *args, out)
    r = run_bass_kernel_spmd(nc, [arrays], core_ids=[0])
    return r.results[0]["out"].reshape(1, LAT, D)
```
